# Optimizing a Trainium2 kernel written in Bass

```python
import math
import jax
import jax.numpy as jnp
from jax import lax
import numpy as np

D_MODEL = 1024
BATCH = 1
SEQ = 256
DEPTH = 2
DEC_BATCH = 8
DEC_SEQ = 1
PAST_LEN = 1024
PAGE_SIZE = 128

N_A_LAYERS = DEPTH // 2
N_B_LAYERS = DEPTH - N_A_LAYERS
A_HEADS = 4
A_INNER = 2 * D_MODEL
A_HEAD_DIM = A_INNER // A_HEADS
A_CONV_W = 4
A_CHUNK = 64
B_HEADS = 16
B_KV_HEADS = 4
B_GROUP = B_HEADS // B_KV_HEADS
B_HEAD_DIM = D_MODEL // B_HEADS
WINDOW = 128
N_BUCKETS = 32
MAX_DISTANCE = 128
P_HEADS = 8
N_KEYS = 128
N_EXPERTS = N_KEYS * N_KEYS
D_KEY = 256
P_TOPK = 16
P_BLOCK = 128
DN_ALPHA = (2 * DEPTH) ** 0.25
DN_BETA = (8 * DEPTH) ** -0.25
LN_EPS = 1e-5
NEG_INF = -1e30

kernel_name = 'yoco_mlstm_swa_sink_peer_step'

def layer_norm(x, g, b):
    xf = x.astype(jnp.float32)
    mu = xf.mean(-1, keepdims=True)
    var = jnp.square(xf - mu).mean(-1, keepdims=True)
    y = (xf - mu) * lax.rsqrt(var + LN_EPS)
    return (y * g.astype(jnp.float32) + b.astype(jnp.float32)).astype(x.dtype)

def post_norm(x, sub, g, b):
    return layer_norm(DN_ALPHA * x + sub, g, b)

def t5_bucket(dist):
    max_exact = N_BUCKETS // 2
    d = jnp.maximum(dist, 0)
    df = jnp.maximum(d, 1).astype(jnp.float32)
    large = max_exact + (jnp.log(df / max_exact) / math.log(MAX_DISTANCE / max_exact)
                         * (N_BUCKETS - max_exact)).astype(jnp.int32)
    large = jnp.minimum(large, N_BUCKETS - 1)
    return jnp.where(d < max_exact, d, large)

def mlstm_chunkwise(q, k, v, log_i, log_f, C0, n0, m0, chunk):
    B, L, H, DH = q.shape
    nc = L // chunk

    def to_chunks(a):
        return jnp.moveaxis(a.reshape((B, nc, chunk) + a.shape[2:]), 1, 0)

    xs = tuple(to_chunks(a.astype(jnp.float32)) for a in (q, k, v, log_i, log_f))
    causal = jnp.tril(jnp.ones((chunk, chunk), dtype=bool))

    def step(carry, inp):
        C, n, m = carry
        qb, kb, vb, ib, fb = inp
        Fh = jnp.swapaxes(jnp.cumsum(fb, axis=1), 1, 2)
        ih = jnp.swapaxes(ib, 1, 2)
        d_intra = jnp.where(causal, Fh[..., :, None] - Fh[..., None, :] + ih[..., None, :], NEG_INF)
        b_inter = Fh + m[..., None]
        m_t = jnp.maximum(b_inter, d_intra.max(-1))
        s = jnp.einsum('bthd,bshd->bhts', qb, kb) * jnp.exp(d_intra - m_t[..., None])
        w_inter = jnp.swapaxes(jnp.exp(b_inter - m_t), 1, 2)[..., None]
        num = jnp.einsum('bhts,bshe->bthe', s, vb) + w_inter * jnp.einsum('bthd,bhde->bthe', qb, C)
        den = jnp.swapaxes(s.sum(-1), 1, 2) + w_inter[..., 0] * jnp.einsum('bthd,bhd->bth', qb, n)
        h = num / jnp.maximum(jnp.abs(den), jnp.exp(-jnp.swapaxes(m_t, 1, 2)))[..., None]
        F_L = Fh[..., -1]
        g = F_L[..., None] - Fh + ih
        m_new = jnp.maximum(F_L + m, g.max(-1))
        decay = jnp.exp(F_L + m - m_new)
        ws = jnp.swapaxes(jnp.exp(g - m_new[..., None]), 1, 2)[..., None]
        wk = ws * kb
        C_new = decay[..., None, None] * C + jnp.einsum('bshd,bshe->bhde', wk, vb)
        n_new = decay[..., None] * n + wk.sum(1)
        return (C_new, n_new, m_new), h

    init = (C0.astype(jnp.float32), n0.astype(jnp.float32), m0.astype(jnp.float32))
    (C, n, m), h = lax.scan(step, init, xs)
    h = jnp.moveaxis(h, 0, 1).reshape(B, L, H, DH)
    return h, C, n, m

def mlstm_mixer(x, conv_buf, C0, n0, m0, w_in, b_in, conv_w, conv_b, w_q, w_k, w_v, w_out, chunk):
    B, L, _ = x.shape
    proj = x @ w_in + b_in
    x_m, o_pre, i_pre, f_pre = jnp.split(
        proj, [A_INNER, 2 * A_INNER, 2 * A_INNER + A_HEADS], axis=-1)
    xp = jnp.concatenate([conv_buf.astype(x.dtype), x_m], axis=1)
    x_c = sum(xp[:, w:w + L] * conv_w[w] for w in range(A_CONV_W)) + conv_b
    x_c = jax.nn.silu(x_c)
    new_buf = xp[:, -(A_CONV_W - 1):]
    xch = x_c.reshape(B, L, A_HEADS, A_HEAD_DIM)
    xmh = x_m.reshape(B, L, A_HEADS, A_HEAD_DIM)
    q = jnp.einsum('blhd,hde->blhe', xch, w_q)
    k = jnp.einsum('blhd,hde->blhe', xch, w_k) * (A_HEAD_DIM ** -0.5)
    v = jnp.einsum('blhd,hde->blhe', xmh, w_v)
    log_i = i_pre.astype(jnp.float32)
    log_f = jax.nn.log_sigmoid(f_pre.astype(jnp.float32))
    h, C, n, m = mlstm_chunkwise(q, k, v, log_i, log_f, C0, n0, m0, chunk)
    h = jax.nn.sigmoid(o_pre) * h.reshape(B, L, A_INNER).astype(x.dtype)
    return h @ w_out, new_buf, C.astype(x.dtype), n.astype(x.dtype), m.astype(x.dtype)

def sink_attend(s, v, sinks, eq):
    sink = sinks.astype(jnp.float32).reshape(B_KV_HEADS, B_GROUP)[..., None]
    m = jnp.maximum(s.max(-1), sink)
    p = jnp.exp(s - m[..., None])
    den = p.sum(-1) + jnp.exp(sink - m)
    p = p / den[..., None]
    return jnp.einsum(eq, p.astype(v.dtype), v)

def swa_prompt(q, k, v, sinks, rel_bias):
    B, S = q.shape[:2]
    nb = S // WINDOW
    qb = q.reshape(B, nb, WINDOW, B_KV_HEADS, B_GROUP, B_HEAD_DIM)
    pad = jnp.zeros((B, WINDOW, B_KV_HEADS, B_HEAD_DIM), k.dtype)

    def band(a):
        ab = jnp.concatenate([pad, a], axis=1).reshape(B, nb + 1, WINDOW, B_KV_HEADS, B_HEAD_DIM)
        return jnp.concatenate([ab[:, :-1], ab[:, 1:]], axis=2)

    kb, vb = band(k), band(v)
    qi = jnp.arange(WINDOW)[:, None]
    kj = jnp.arange(2 * WINDOW)[None, :]
    dist = qi + WINDOW - kj
    blk = jnp.arange(nb)[:, None, None]
    valid = (dist >= 0) & (dist < WINDOW) & (blk * WINDOW - WINDOW + kj >= 0)
    bias = rel_bias[t5_bucket(dist)].astype(jnp.float32)
    bias = bias.transpose(2, 0, 1).reshape(B_KV_HEADS, B_GROUP, WINDOW, 2 * WINDOW)
    s = jnp.einsum('bnqkgd,bnskd->bnkgqs', qb, kb).astype(jnp.float32) * (B_HEAD_DIM ** -0.5) + bias
    s = jnp.where(valid[None, :, None, None], s, NEG_INF)
    o = sink_attend(s, vb, sinks, 'bnkgqs,bnskd->bnqkgd')
    return o.reshape(B, S, B_HEADS * B_HEAD_DIM)

def swa_decode(q, k_all, v_all, sinks, rel_bias):
    B, L = q.shape[:2]
    qpos = jnp.arange(L)[:, None] + WINDOW
    kpos = jnp.arange(WINDOW + L)[None, :]
    dist = qpos - kpos
    valid = (dist >= 0) & (dist < WINDOW)
    bias = rel_bias[t5_bucket(dist)].astype(jnp.float32)
    bias = bias.transpose(2, 0, 1).reshape(B_KV_HEADS, B_GROUP, L, WINDOW + L)
    s = jnp.einsum('bqkgd,bskd->bkgqs', q, k_all).astype(jnp.float32) * (B_HEAD_DIM ** -0.5) + bias
    s = jnp.where(valid, s, NEG_INF)
    o = sink_attend(s, v_all, sinks, 'bkgqs,bskd->bqkgd')
    return o.reshape(B, L, B_HEADS * B_HEAD_DIM)

def peer(x, w_q, subkeys, u, v):
    B, L, D = x.shape
    T = B * L
    xt = x.reshape(T, D)
    q = (xt @ w_q).reshape(T, P_HEADS, 2, D_KEY // 2)
    sc = jnp.einsum('thpc,hpnc->thpn', q, subkeys).astype(jnp.float32)
    top_s, top_i = lax.top_k(sc, P_TOPK)
    cand = top_s[:, :, 0, :, None] + top_s[:, :, 1, None, :]
    cand_idx = top_i[:, :, 0, :, None] * N_KEYS + top_i[:, :, 1, None, :]
    best_s, best_pos = lax.top_k(cand.reshape(T, P_HEADS, P_TOPK * P_TOPK), P_TOPK)
    idx = jnp.take_along_axis(cand_idx.reshape(T, P_HEADS, P_TOPK * P_TOPK), best_pos, axis=-1)
    gate = jax.nn.softmax(best_s, axis=-1)
    idx = idx.reshape(T, P_HEADS * P_TOPK)
    gate = gate.reshape(T, P_HEADS * P_TOPK).astype(x.dtype)
    pad = (-T) % P_BLOCK
    xt = jnp.pad(xt, ((0, pad), (0, 0)))
    idx = jnp.pad(idx, ((0, pad), (0, 0)))
    gate = jnp.pad(gate, ((0, pad), (0, 0)))
    nblk = (T + pad) // P_BLOCK

    def block(args):
        xb, ib, gb = args
        ub = jnp.take(u, ib, axis=0)
        a = jax.nn.gelu(jnp.einsum('td,ted->te', xb, ub), approximate=False)
        vb = jnp.take(v, ib, axis=0)
        return jnp.einsum('te,ted->td', a * gb, vb)

    out = lax.map(block, (xt.reshape(nblk, P_BLOCK, D),
                          idx.reshape(nblk, P_BLOCK, -1),
                          gate.reshape(nblk, P_BLOCK, -1)))
    return out.reshape(-1, D)[:T].reshape(B, L, D)

def trunk(x, conv0, C0, n0, m0, k_buf, v_buf, p, prompt):
    B, L, _ = x.shape
    if prompt:
        conv0 = jnp.zeros((N_A_LAYERS, B, A_CONV_W - 1, A_INNER), x.dtype)
        C0 = jnp.zeros((N_A_LAYERS, B, A_HEADS, A_HEAD_DIM, A_HEAD_DIM), x.dtype)
        n0 = jnp.zeros((N_A_LAYERS, B, A_HEADS, A_HEAD_DIM), x.dtype)
        m0 = jnp.zeros((N_A_LAYERS, B, A_HEADS), x.dtype)
    new_conv, new_C, new_n, new_m = [], [], [], []
    k_all = v_all = new_k_win = new_v_win = None
    for layer in range(DEPTH):
        if layer < N_A_LAYERS:
            a = layer
            h, cb, C, n, m = mlstm_mixer(
                x, conv0[a], C0[a], n0[a], m0[a], p['a_w_in'][a], p['a_b_in'][a],
                p['a_conv_w'][a], p['a_conv_b'][a], p['a_w_q'][a], p['a_w_k'][a],
                p['a_w_v'][a], p['a_w_out'][a], A_CHUNK if prompt else L)
            new_conv.append(cb)
            new_C.append(C)
            new_n.append(n)
            new_m.append(m)
        else:
            if layer == N_A_LAYERS:
                k_new, v_new = jnp.split(x @ p['kv_w'], 2, axis=-1)
                k_new = k_new.reshape(B, L, B_KV_HEADS, B_HEAD_DIM)
                v_new = v_new.reshape(B, L, B_KV_HEADS, B_HEAD_DIM)
                if prompt:
                    k_all, v_all = k_new, v_new
                else:
                    k_all = jnp.concatenate([k_buf.astype(x.dtype), k_new], axis=1)
                    v_all = jnp.concatenate([v_buf.astype(x.dtype), v_new], axis=1)
                new_k_win = k_all[:, -WINDOW:]
                new_v_win = v_all[:, -WINDOW:]
            bl = layer - N_A_LAYERS
            q = (x @ p['b_w_q'][bl]).reshape(B, L, B_KV_HEADS, B_GROUP, B_HEAD_DIM)
            if prompt:
                o = swa_prompt(q, k_all, v_all, p['b_sinks'][bl], p['rel_bias'])
            else:
                o = swa_decode(q, k_all, v_all, p['b_sinks'][bl], p['rel_bias'])
            h = o @ p['b_w_o'][bl]
        x = post_norm(x, h, p['ln_mix_g'][layer], p['ln_mix_b'][layer])
        f = peer(x, p['peer_w_q'][layer], p['peer_subkeys'][layer], p['peer_u'][layer], p['peer_v'][layer])
        x = post_norm(x, f, p['ln_ffn_g'][layer], p['ln_ffn_b'][layer])
    return (x, jnp.stack(new_C), jnp.stack(new_n), jnp.stack(new_m), jnp.stack(new_conv),
            new_k_win, new_v_win)

def setup_inputs(seed: int = 0) -> dict:
    key = jax.random.key(seed)
    ks = iter(jax.random.split(key, 40))

    def nrm(shape, scale):
        return jax.random.normal(next(ks), shape, jnp.float32) * scale

    NA, NB = N_A_LAYERS, N_B_LAYERS
    kvw = B_KV_HEADS * B_HEAD_DIM
    a_b_in = jnp.concatenate([
        nrm((NA, 2 * A_INNER), 0.02),
        nrm((NA, A_HEADS), 0.1),
        jnp.linspace(3.0, 6.0, A_HEADS)[None, :] + nrm((NA, A_HEADS), 0.1),
    ], axis=-1)
    kv_w = jnp.concatenate([nrm((D_MODEL, kvw), D_MODEL ** -0.5),
                            nrm((D_MODEL, kvw), D_MODEL ** -0.5 * DN_BETA)], axis=-1)
    return {
        'x_prompt': nrm((BATCH, SEQ, D_MODEL), 1.0),
        'x_sample': nrm((DEC_BATCH, DEC_SEQ, D_MODEL), 1.0),
        'state_mlstm_C': nrm((NA, DEC_BATCH, A_HEADS, A_HEAD_DIM, A_HEAD_DIM), 0.05),
        'state_mlstm_n': nrm((NA, DEC_BATCH, A_HEADS, A_HEAD_DIM), 0.05),
        'state_mlstm_m': nrm((NA, DEC_BATCH, A_HEADS), 0.5),
        'state_mlstm_conv': nrm((NA, DEC_BATCH, A_CONV_W - 1, A_INNER), 1.0),
        'cache_k_win': nrm((DEC_BATCH, WINDOW, B_KV_HEADS, B_HEAD_DIM), 1.0),
        'cache_v_win': nrm((DEC_BATCH, WINDOW, B_KV_HEADS, B_HEAD_DIM), DN_BETA),
        'a_w_in': nrm((NA, D_MODEL, 2 * A_INNER + 2 * A_HEADS), D_MODEL ** -0.5),
        'a_b_in': a_b_in,
        'a_conv_w': nrm((NA, A_CONV_W, A_INNER), A_CONV_W ** -0.5),
        'a_conv_b': nrm((NA, A_INNER), 0.02),
        'a_w_q': nrm((NA, A_HEADS, A_HEAD_DIM, A_HEAD_DIM), A_HEAD_DIM ** -0.5),
        'a_w_k': nrm((NA, A_HEADS, A_HEAD_DIM, A_HEAD_DIM), A_HEAD_DIM ** -0.5),
        'a_w_v': nrm((NA, A_HEADS, A_HEAD_DIM, A_HEAD_DIM), A_HEAD_DIM ** -0.5 * DN_BETA),
        'a_w_out': nrm((NA, A_INNER, D_MODEL), A_INNER ** -0.5 * DN_BETA),
        'kv_w': kv_w,
        'b_w_q': nrm((NB, D_MODEL, B_HEADS * B_HEAD_DIM), D_MODEL ** -0.5),
        'b_w_o': nrm((NB, B_HEADS * B_HEAD_DIM, D_MODEL), (B_HEADS * B_HEAD_DIM) ** -0.5 * DN_BETA),
        'b_sinks': nrm((NB, B_HEADS), 0.5),
        'rel_bias': nrm((N_BUCKETS, B_HEADS), 0.1),
        'ln_mix_g': 1.0 + nrm((DEPTH, D_MODEL), 0.02),
        'ln_mix_b': nrm((DEPTH, D_MODEL), 0.02),
        'ln_ffn_g': 1.0 + nrm((DEPTH, D_MODEL), 0.02),
        'ln_ffn_b': nrm((DEPTH, D_MODEL), 0.02),
        'peer_w_q': nrm((DEPTH, D_MODEL, P_HEADS * D_KEY), D_MODEL ** -0.5),
        'peer_subkeys': nrm((DEPTH, P_HEADS, 2, N_KEYS, D_KEY // 2), (D_KEY // 2) ** -0.5),
        'peer_u': nrm((DEPTH, N_EXPERTS, D_MODEL), D_MODEL ** -0.5),
        'peer_v': nrm((DEPTH, N_EXPERTS, D_MODEL), D_MODEL ** -0.5 * DN_BETA),
    }

def reference(x_prompt, x_sample, state_mlstm_C, state_mlstm_n, state_mlstm_m, state_mlstm_conv,
              cache_k_win, cache_v_win, a_w_in, a_b_in, a_conv_w, a_conv_b, a_w_q, a_w_k, a_w_v,
              a_w_out, kv_w, b_w_q, b_w_o, b_sinks, rel_bias, ln_mix_g, ln_mix_b, ln_ffn_g,
              ln_ffn_b, peer_w_q, peer_subkeys, peer_u, peer_v):
    p = {'a_w_in': a_w_in, 'a_b_in': a_b_in, 'a_conv_w': a_conv_w, 'a_conv_b': a_conv_b,
         'a_w_q': a_w_q, 'a_w_k': a_w_k, 'a_w_v': a_w_v, 'a_w_out': a_w_out, 'kv_w': kv_w,
         'b_w_q': b_w_q, 'b_w_o': b_w_o, 'b_sinks': b_sinks, 'rel_bias': rel_bias,
         'ln_mix_g': ln_mix_g, 'ln_mix_b': ln_mix_b, 'ln_ffn_g': ln_ffn_g, 'ln_ffn_b': ln_ffn_b,
         'peer_w_q': peer_w_q, 'peer_subkeys': peer_subkeys, 'peer_u': peer_u, 'peer_v': peer_v}
    y_prompt, p_C, p_n, p_m, p_conv, p_k, p_v = trunk(
        x_prompt, None, None, None, None, None, None, p, True)
    y_sample, s_C, s_n, s_m, s_conv, s_k, s_v = trunk(
        x_sample, state_mlstm_conv, state_mlstm_C, state_mlstm_n, state_mlstm_m,
        cache_k_win, cache_v_win, p, False)
    return (y_prompt, y_sample, p_C, p_n, p_m, p_conv, p_k, p_v, s_C, s_n, s_m, s_conv, s_k, s_v)


_drawn_inputs = setup_inputs


def setup_inputs(seed=0):
    import zlib

    import numpy as np

    out = dict(_drawn_inputs(seed))
    spreads = {}
    factors = {'b_sinks': 8.0,
     'rel_bias': 8.0,
     'peer_w_q': 7.073,
     'peer_subkeys': 7.458,
     'peer_u': 8.0,
     'peer_v': 7.327}
    for name, (base, spread) in spreads.items():
        noise = np.random.default_rng([zlib.crc32(name.encode()), seed]).standard_normal(out[name].shape)
        drawn = base * np.exp(spread * noise) if base else spread * noise
        out[name] = jnp.asarray(drawn.astype(out[name].dtype))
    for name, factor in factors.items():
        out[name] = (out[name] * factor).astype(out[name].dtype)
    return out
```

```python
from contextlib import ExitStack

import numpy as np

import concourse.bass as bass
from concourse import mybir

F32 = mybir.dt.float32
U32 = mybir.dt.uint32
ALU = mybir.AluOpType
ACT = mybir.ActivationFunctionType
AX = mybir.AxisListType

P = 128
D = 1024
TP = 256
NSM = 8
T = TP + NSM
DC = D // P
INNER = 2048
IC = INNER // P
HA = 4
DH = INNER // HA
HC = DH // P
CONV_W = 4
KVH = 4
GROUP = 4
HB = 16
HD = 64
WINDOW = 128
NB = 32
PH = 8
NK = 128
TOPK = 16
DEPTH = 2
ALPHA = (2 * DEPTH) ** 0.25
LN_EPS = 1e-5
NEG = -1e30
LOWEST = -3.0e38
RING = 4
XPW = 3 + TP + 4 * NSM
BIASW = 3 * WINDOW

U_IN = 0
U_QKV = U_IN + 2 * IC
U_OUT = U_QKV + 6 * HA
U_PQ = [U_OUT + 2 * DC, 0]
U_U = [U_PQ[0] + 2 * PH, 0]
U_V = [U_U[0] + NK, 0]
U_KV = U_V[0] + NK
U_BQ = U_KV + 4
U_BO = U_BQ + DC
U_PQ[1] = U_BO + DC
U_U[1] = U_PQ[1] + 2 * PH
U_V[1] = U_U[1] + NK
N_UNITS = U_V[1] + NK

COLS = {}
_at = 0
for _n, _c in (("b_in", 2 * IC), ("conv_w", CONV_W * IC), ("conv_b", IC),
               ("mix_g", 2 * DC), ("mix_b", 2 * DC), ("ffn_g", 2 * DC), ("ffn_b", 2 * DC)):
    COLS[_n] = (_at, _c)
    _at += _c
NCOLS = _at

CONSTS = {}
_at = 0
for _n, _c in (("ident", P), ("iota", P), ("iota16", TOPK), ("causal", P), ("mean", P), ("ones", 2 * P), ("eps", 1)):
    CONSTS[_n] = (_at, _c)
    _at += _c
NCONST = _at
TILES = [(0, P), (P, P), (TP, NSM)]


def build(nc, io):
    with ExitStack() as ctx:
        _build(nc, io, ctx)


def _build(nc, io, ctx):
    def sb(name, shape, dt=F32):
        return ctx.enter_context(nc.sbuf_tensor(name, shape, dt))

    sems = {}

    def sem(name):
        if name not in sems:
            sems[name] = ctx.enter_context(nc.semaphore(name))
        return sems[name]

    ring = sb("ring", [P, RING, 1024])
    x = sb("x", [P, DC, T])
    big = sb("big", [P, NK * T])
    scb = sb("scb", [P, 3 * 2048])
    tmp = sb("tmp", [P, 1024])
    const = sb("const", [P, NCONST])
    cols = sb("cols", [P, NCOLS])
    top_s = sb("top_s", [P, 2 * PH, TOPK])
    top_iu = sb("top_iu", [P, 2 * PH, TOPK], U32)
    top_if = sb("top_if", [P, 2 * PH, TOPK])
    best_s = sb("best_s", [P, 3, PH, TOPK])
    best_u = sb("best_u", [P, PH, TOPK], U32)
    rank_u = sb("rank_u", [P, PH, TOPK], U32)
    rank_f = sb("rank_f", [P, 2, PH, TOPK])
    sel_i = sb("sel_i", [P, 3, PH * TOPK])
    sel_j = sb("sel_j", [P, 3, PH * TOPK])
    gsum = sb("gsum", [P, 3, PH])
    turned = sb("turned", [P, 3, T])

    pa = ctx.enter_context(nc.psum_tensor("pa", [P, 4, 512], F32))
    pb = ctx.enter_context(nc.psum_tensor("pb", [P, 4, 512], F32))

    def cst(name, rows=P):
        a, n = CONSTS[name]
        return const[0:rows, a:a + n]

    def col(name, i):
        return cols[:, COLS[name][0] + i:COLS[name][0] + i + 1]

    ident, iota, causal, mean, ones = cst("ident"), cst("iota"), cst("causal"), cst("mean"), cst("ones")
    ones_col = ones[:, 0:1]

    at = [0]
    at_scb = [0]

    def carve(*dims, of=None, at=at):
        n = 1
        for d in dims:
            n *= d
        of = big if of is None else of
        v = of[:, at[0]:at[0] + n]
        at[0] += n
        if len(dims) == 1:
            return v
        names = "abcd"[:len(dims)]
        return v.rearrange("p (%s) -> p %s" % (" ".join(names), " ".join(names)), **dict(zip(names, dims)))

    xp = carve(IC, XPW)
    xc = carve(IC, T)
    so = carve(IC, T)
    qt = carve(2, HC, T)
    kt = carve(2, HC, T)
    vn = carve(2, 2, DH)
    vs = carve(2, DH)
    wk = carve(2, DH)
    cs = carve(3, HC, DH)
    c_out = carve(HC, DH)
    conv_in = carve(IC, NSM, 3)
    conv_out = carve(IC, 3 + 3 * NSM)
    conv_acc = carve(2, XPW - 3)
    w_gate = carve(DC, 8)
    p0 = carve(TP)
    p1 = carve(P)
    em = carve(TP)
    den = carve(TP)
    hn = carve(HC, TP, of=tmp, at=[0])
    gcol = carve(16)
    sg = carve(HA, 2 * NSM)
    kws = carve(HC, NSM)
    qm = carve(HC, NSM, NSM)
    n_in = carve(HA, HC, NSM)
    n_new = carve(HA, HC, NSM)
    n_prompt = carve(HA, HC)
    qn = carve(HC, NSM)
    rows = carve(8, 272, of=scb, at=at_scb)
    b_rows = carve(2)
    m_in = carve(NSM)
    m_out = carve(1 + NSM)
    em_s = carve(HA)
    den_s = carve(2)
    hs = carve(DH, of=scb, at=at_scb)
    sel4 = carve(HA, P, of=scb, at=at_scb)
    sel8 = carve(NSM, P, of=scb, at=at_scb)
    rt = carve(BIASW, of=scb, at=at_scb)
    relb = carve(HB, of=scb, at=at_scb)
    onehot = carve(WINDOW, of=scb, at=at_scb)
    used_a = at[0]

    at[0] = 0
    qb = carve(DC, T)
    ktb = carve(2, T)
    vnb = carve(2, KVH * HD)
    vsb = carve(KVH * HD)
    kw = carve(2, NSM, WINDOW)
    vw = carve(NSM, KVH * HD)
    bias = carve(HB, 2 * WINDOW)
    bias_s = carve(WINDOW)
    ss = carve(2, 4, 2 * WINDOW)
    pt = carve(2, 4, 2, WINDOW)
    ot = carve(DC, T)
    qbd = carve(NSM, 2, P)
    sink = carve(HB)
    sink_s = carve(1)
    mx = carve(2, 4)
    sx = carve(2, 4)
    dx = carve(2, 4)
    ss_s = carve(WINDOW)
    pt_s = carve(P)
    small_s = carve(4)

    w3 = big[:, :].rearrange("p (i t) -> p i t", t=T)
    pq = w3[:, NK - 2 * PH:NK, :]
    skeys = big[:, (NK - 3 * PH) * T:(NK - 3 * PH) * T + 2 * PH * NK].rearrange("p (h n) -> p h n", n=NK)
    assert used_a <= NK * T

    sub = scb[:, 0:DC * T].rearrange("p (c t) -> p c t", t=T)
    sq = scb[:, DC * T:2 * DC * T].rearrange("p (c t) -> p c t", t=T)
    rstd = tmp[:, 0:T]
    scores = scb[:, :].rearrange("p (a h n) -> p a h n", a=3, n=NK)
    hot = scb[:, :].rearrange("p (s k t n) -> p s k t n", s=3, k=2, t=8)

    landed = [sem(f"unit_landed_{k}") for k in range(RING)]
    units_used = sem("units_used")
    evacuated = sem("bank_evacuated")

    def gate_bank(s):
        return pb[:, 2 * s:2 * s + 2, :] if s < 2 else pa[:, 0:2, :]

    out_groups = 2 * IC + HA * 2 * HC + DC
    peer_total = 2 * PH + NK + DC
    peer_groups = [out_groups + peer_total, 0]
    kv_groups = peer_groups[0] + 2
    bq_groups = kv_groups + DC
    bo_groups = bq_groups + DC
    peer_groups[1] = bo_groups + peer_total

    block = ctx.enter_context(nc.Block())

    @block.sync
    def _(sp):
        sp.dma_start(const[:, :], io["const"]).then_inc(sem("const_in"), 16)
        sp.dma_start(cols[:, :], io["cols"]).then_inc(sem("cols_in"), 16)
        sp.dma_start(x[:, :, :], io["x"]).then_inc(sem("x_in"), 16)
        sp.dma_start(w_gate, io["w_gate"]).then_inc(sem("gate_in"), 16)
        sp.dma_start(b_rows[0:HA, :], io["b_gate"]).then_inc(sem("gate_in"), 16)
        sp.dma_start(m_in[0:HA, :], io["m_in"]).then_inc(sem("gate_in"), 16)
        sp.dma_start(sel4[0:HA, :, :], io["sel4"]).then_inc(sem("gate_in"), 16)
        sp.dma_start(sel8[0:NSM, :, :], io["sel8"]).then_inc(sem("gate_in"), 16)
        for k in range(RING):
            sp.dma_start(ring[:, k, :], io["units"][k]).then_inc(landed[k], 16)
        sp.dma_start(conv_in, io["conv_in"]).then_inc(sem("conv_in"), 16)
        sp.dma_start(n_in, io["n_in"]).then_inc(sem("state_n_in"), 16)
        with sp.Fori(1, N_UNITS // RING) as it:
            for k in range(RING):
                sp.wait_ge(units_used, it * RING + (k + 1 - RING))
                sp.dma_start(ring[:, k, :], io["units"][it * RING + k]).then_inc(landed[k], 16)

    @block.tensor
    def _(pe):
        unit = [0]
        group = [0]

        def mm(out, lhs, rhs, start=True, stop=True):
            return pe.matmul(out, lhs, rhs, start=start, stop=stop)

        def next_unit():
            n = unit[0]
            pe.wait_ge(landed[n % RING], 16 * (n // RING + 1))
            unit[0] += 1
            return ring[:, n % RING, :]

        def next_bank():
            g = group[0]
            if g >= 4:
                pe.wait_ge(evacuated, g - 3)
            group[0] += 1
            return pa[:, g % 4, :]

        def project(src, n_tiles):
            for _ in range(n_tiles):
                w = next_unit()
                out = next_bank()
                for k in range(DC):
                    last = mm(out[:, 0:T], w[:, k * P:(k + 1) * P], src[:, k, :], k == 0, k == DC - 1)
                last.then_inc(units_used, 1)

        def norm(li):
            pe.wait_ge(sem("ln_sum"), li + 1)
            for k in range(DC):
                last = mm(pb[:, 0, 0:T], mean, x[:, k, :], k == 0, k == DC - 1)
            last.then_inc(sem("ln_mean"), 1)
            pe.wait_ge(sem("ln_square"), li + 1)
            for k in range(DC):
                last = mm(pb[:, 1, 0:T], mean, sq[:, k, :], k == 0, k == DC - 1)
            last.then_inc(sem("ln_var"), 1)

        def peer(L):
            pe.wait_ge(sem("x_ready"), 2 * L + 1)
            project(x, 2 * PH)
            pe.wait_ge(sem("skeys_in"), 16 * (L + 1))
            pe.wait_ge(evacuated, group[0])
            for a, (t0, n) in enumerate(TILES):
                if L or a:
                    pe.wait_ge(sem("scores_copied"), 3 * L + a)
                for h in range(2 * PH):
                    last = mm(pb[0:n, h // 4, (h % 4) * NK:(h % 4 + 1) * NK], pq[:, h, t0:t0 + n], skeys[:, h, :])
                last.then_inc(sem("scores_done"), 1)
            base, g0 = unit[0], group[0]
            assert base % RING == 0 and base == U_U[L]
            with pe.Fori(0, NK // RING) as it:
                for k in range(RING):
                    pe.wait_ge(landed[k], it * 16 + 16 * (base // RING + 1))
                    pe.wait_ge(evacuated, it * RING + (g0 + k - 3))
                    out = pa[:, (g0 + k) % 4, 0:T]
                    for c in range(DC):
                        last = mm(out, ring[:, k, c * P:(c + 1) * P], x[:, c, :], c == 0, c == DC - 1)
                    last.then_inc(units_used, 1)
            unit[0] += NK
            group[0] += NK
            pe.wait_ge(sem("gates_done"), L + 1)
            for a, (t0, n) in enumerate(TILES):
                for b, src in enumerate((sel_i, sel_j)):
                    pe.transpose(pb[:, b, t0:t0 + n], src[0:n, a, :], ident[0:n, 0:n])
                last = pe.transpose(pb[:, 2, t0:t0 + n], best_s[0:n, a, :, :].rearrange("p h k -> p (h k)"),
                                    ident[0:n, 0:n])
            last.then_inc(sem("choice_turned"), 1)
            pe.wait_ge(evacuated, group[0])

            def gate_set(n, s):
                pe.wait_ge(sem("hot_i"), n + 1)
                pe.wait_ge(sem("hot_j"), n + 1)
                for t in range(8):
                    out = gate_bank(s)[:, t // 4, (t % 4) * NK:(t % 4 + 1) * NK]
                    last = mm(out, hot[:, s, 1, t, :], hot[:, s, 0, t, :])
                last.then_inc(sem("gates_spread"), 1)

            for s in range(3):
                gate_set(33 * L + s, s)
            with pe.Fori(1, T // 24) as it:
                for s in range(3):
                    pe.wait_ge(sem("gates_applied"), it * 3 + (33 * L + s - 2))
                    gate_set(it * 3 + (33 * L + s), s)
            pe.wait_ge(sem("gates_applied"), 33 * (L + 1))
            for m in range(DC):
                out = next_bank()[:, 0:T]
                base = unit[0]
                for c in range(RING):
                    y_unit(pe, base, 0, c, out, first=(c == 0), last=False)
                with pe.Fori(1, 3) as it:
                    for c in range(RING):
                        y_unit(pe, base, it, c, out, first=False, last=False)
                for c in range(RING):
                    y_unit(pe, base, 3, c, out, first=False, last=(c == RING - 1))
                unit[0] += 16

        def y_unit(pe, base, it, c, out, first, last):
            pe.wait_ge(landed[c], it * 16 + 16 * (base // RING + 1))
            for i in range(8):
                rhs = big[:, bass.ds(it * (32 * T) + (c * 8 + i) * T, T)]
                ins = mm(out, ring[:, c, i * P:(i + 1) * P], rhs, first and i == 0, last and i == 7)
            ins.then_inc(units_used, 1)

        pe.wait_ge(sem("const_in"), 16)
        pe.wait_ge(sem("x_in"), 16)
        pe.wait_ge(sem("gate_in"), 80)
        for g in range(2):
            for k in range(DC):
                last = mm(pb[0:HA, g, 0:T], w_gate[:, k, g * HA:(g + 1) * HA], x[:, k, :], k == 0, k == DC - 1)
        last.then_inc(sem("gate_pre"), 1)
        pe.wait_ge(sem("bias_in"), 32)
        mm(pb[0:HB, 2, 0:WINDOW], relb[0:NB, :], onehot[0:NB, :]).then_inc(sem("bias_rows"), 1)
        project(x, 2 * IC)

        pe.wait_ge(sem("gate_exps"), 1)
        for s in range(2):
            pe.transpose(pb[:, 2, s * HA:(s + 1) * HA], rows[0:HA, 4, s * P:(s + 1) * P], ident[0:HA, 0:HA])
            pe.transpose(pb[:, 2, 8 + s * HA:8 + (s + 1) * HA], rows[0:HA, 7, s * P:(s + 1) * P], ident[0:HA, 0:HA])
        pe.transpose(pb[0:NSM, 2, 16:20], rows[0:HA, 6, TP:T], ident[0:HA, 0:HA])
        for h in range(HA):
            last = mm(pb[:, 3, h * 16:(h + 1) * 16], sel4[0:HA, h, :], rows[0:HA, 7, TP:TP + 16])
        last.then_inc(sem("gate_cols"), 1)

        def head_project(h):
            if h >= 2:
                pe.wait_ge(sem("head_done"), h - 1)
            if h == 0:
                pe.wait_ge(sem("conv_done"), IC)
            for part in range(2):
                for _ in range(2):
                    w = next_unit()
                    for m in range(2):
                        out = next_bank()
                        for k in range(HC):
                            last = mm(out[:, 0:T], w[:, k * 256 + m * P:k * 256 + (m + 1) * P], xc[:, h * HC + k, :],
                                      k == 0, k == HC - 1)
                    last.then_inc(units_used, 1)
            if h == 0:
                pe.wait_ge(sem("gate_cols_kept"), 1)
            for u in range(2):
                w = next_unit()
                for k in range(2):
                    kk = 2 * u + k
                    src = xp[:, h * HC + kk, :]
                    rhs = w[:, k * DH:(k + 1) * DH]
                    mm(pb[:, 0, :], src[:, 3:3 + P], rhs, kk == 0, kk == HC - 1)
                    mm(pb[:, 1, :], src[:, 3 + P:3 + TP], rhs, kk == 0, kk == HC - 1)
                    last = mm(pb[0:NSM, 2, :], src[:, TP + 6:XPW:4], rhs, kk == 0, kk == HC - 1)
                last.then_inc(units_used, 1)

        def head_prompt(h):
            q, k = qt[:, h % 2], kt[:, h % 2]
            pe.wait_ge(sem("v_kept"), min(h + 2, HA))
            mm(pb[:, 3, 0:TP], sel4[0:HA, h, :], rows[0:HA, 5, 0:TP])
            mm(pb[:, 3, TP:2 * TP], sel4[0:HA, h, :], rows[0:HA, 6, 0:TP]).then_inc(sem("rows_spread"), 1)
            for c in range(HC):
                mm(pb[:, 2, 0:TP], k[:, c, 0:P], q[:, c, 0:TP], c == 0, c == HC - 1)
            for c in range(HC):
                last = mm(pb[:, 2, TP:TP + P], k[:, c, P:TP], q[:, c, P:TP], c == 0, c == HC - 1)
            last.then_inc(sem("scores_t"), 1)
            for s in range(2):
                for c in range(HC):
                    last = pe.transpose(pb[:, s, c * P:(c + 1) * P], k[:, c, s * P:(s + 1) * P], ident)
            last.then_inc(sem("k_turned"), 1)
            pe.wait_ge(sem("weights_t"), h + 1)
            mm(pb[:, 3, 0:P], ones[:, 0:P], p0[:, 0:P])
            mm(pb[:, 3, P:TP], ones[:, 0:P], p0[:, P:TP], True, False)
            mm(pb[:, 3, P:TP], ones[:, 0:P], p1, False, True).then_inc(sem("den_done"), 1)
            for c in range(HC):
                o = pb[:, c // 2, (c % 2) * TP:(c % 2 + 1) * TP]
                v0, v1 = vn[:, h % 2, 0, c * P:(c + 1) * P], vn[:, h % 2, 1, c * P:(c + 1) * P]
                mm(o[:, 0:P], v0, p0[:, 0:P])
                mm(o[:, P:TP], v0, p0[:, P:TP], True, False)
                last = mm(o[:, P:TP], v1, p1, False, True)
            last.then_inc(sem("num_done"), 1)
            pe.wait_ge(sem("den_kept"), h + 1)
            for c in range(HC):
                b = 2 + c % 2
                if c >= 2:
                    pe.wait_ge(sem("c_kept"), HC * h + c - 1)
                mm(pb[:, b, :], wk[:, 0, c * P:(c + 1) * P], vn[:, h % 2, 0, :], True, False)
                mm(pb[:, b, :], wk[:, 1, c * P:(c + 1) * P], vn[:, h % 2, 1, :], False, True).then_inc(sem("c_done"), 1)
            pe.wait_ge(sem("num_used"), h + 1)
            for c in range(HC):
                mm(pb[:, 0, c:c + 1], wk[:, 0, c * P:(c + 1) * P], ones_col, True, False)
                last = mm(pb[:, 0, c:c + 1], wk[:, 1, c * P:(c + 1) * P], ones_col, False, True)
            last.then_inc(sem("n_done"), 1)

        def head_sample(h):
            pe.wait_ge(sem("sample_ready"), h + 1)
            pe.wait_ge(sem("n_kept"), h + 1)
            for c in range(HC):
                last = mm(pb[0:NSM, 0, 4:5], qn[:, c, :], ones_col, c == 0, c == HC - 1)
            last.then_inc(sem("den_s_done"), 1)

            def spread_v(b):
                if b == 0:
                    pe.wait_ge(sem("c_kept"), HC * (h + 1))
                if b >= 2:
                    pe.wait_ge(sem("state_new"), NSM * h + b - 1)
                mm(pb[:, 2 + b % 2, :], sel8[0:NSM, b, :], vs[0:NSM, h % 2, :]).then_inc(sem("v_spread"), 1)

            spread_v(0)
            for b in range(NSM):
                if b + 1 < NSM:
                    spread_v(b + 1)
                n = NSM * h + b
                pe.wait_ge(sem("state_new"), n + 1)
                for c in range(HC):
                    last = mm(pb[0:NSM, 1, :], qm[:, c, b, :], cs[:, n % 3, c, :], b == 0 and c == 0,
                              b == NSM - 1 and c == HC - 1)
                last.then_inc(sem("state_read"), 1)
            pe.wait_ge(sem("h_sample"), h + 1)
            for c in range(HC):
                last = pe.transpose(pb[:, 0, 8 + c * NSM:8 + (c + 1) * NSM], hs[0:NSM, c * P:(c + 1) * P],
                                    ident[0:NSM, 0:NSM])
            last.then_inc(sem("head_done"), 1)

        head_project(0)
        for h in range(HA):
            if h:
                pe.wait_ge(sem("head_gated"), h)
            if h + 1 < HA:
                head_project(h + 1)
            head_prompt(h)
            head_sample(h)
        pe.wait_ge(sem("head_gated"), HA)
        for m in range(DC):
            out = next_bank()
            for half in range(2):
                w = next_unit()
                for k in range(DC):
                    last = mm(out[:, 0:T], w[:, k * P:(k + 1) * P], so[:, half * DC + k, :],
                              half == 0 and k == 0, half == 1 and k == DC - 1)
                last.then_inc(units_used, 1)
        norm(0)
        peer(0)
        norm(1)
        pe.wait_ge(sem("x_ready"), 2)
        project(x, 2)
        for u in range(2):
            w = next_unit()
            for k in range(4):
                kk = 4 * u + k
                rhs = w[:, k * 256:(k + 1) * 256]
                mm(pb[:, 0, 0:256], x[:, kk, 0:P], rhs, kk == 0, kk == DC - 1)
                mm(pb[:, 1, 0:256], x[:, kk, P:TP], rhs, kk == 0, kk == DC - 1)
                last = mm(pb[0:NSM, 2, 0:256], x[:, kk, TP:T], rhs, kk == 0, kk == DC - 1)
            last.then_inc(units_used, 1)
        project(x, DC)
        pe.wait_ge(evacuated, group[0])
        pe.wait_ge(sem("vb_kept"), 1)

        groups = [(blk, g4) for blk in range(2) for g4 in range(4)]

        def att_scores(i):
            blk, g4 = groups[i]
            if i >= 2:
                pe.wait_ge(sem("att_scored"), i - 1)
            for e in range(4):
                half, c = e // 2, 2 * g4 + e % 2
                r = slice(half * HD, (half + 1) * HD)
                nk = P * (blk + 1)
                last = mm(pa[:, 2 * (i % 2) + e // 2, (e % 2) * 256:(e % 2) * 256 + nk],
                          qb[r, c, blk * P:(blk + 1) * P], ktb[r, c // 4, 0:nk])
            last.then_inc(sem("att_scores"), 1)

        def att_values(i):
            blk, g4 = groups[i]
            pe.wait_ge(sem("att_probs"), i + 1)
            if i >= 1:
                pe.wait_ge(sem("att_turned_kept"), i)
            for e in range(4):
                for s in range(blk + 1):
                    last = pe.transpose(pb[:, e // 2, (e % 2) * 256 + s * P:(e % 2) * 256 + (s + 1) * P],
                                        ss[:, i % 2, e, s * P:(s + 1) * P], ident)
            last.then_inc(sem("att_turned"), 1)
            pe.wait_ge(sem("att_turned_kept"), i + 1)
            if i >= 1:
                pe.wait_ge(sem("att_out_kept"), i)
            for e in range(4):
                half, c = e // 2, 2 * g4 + e % 2
                g = 2 * (c // 4) + half
                for s in range(blk + 1):
                    last = mm(pb[half * HD:(half + 1) * HD, 2, (e % 2) * P:(e % 2 + 1) * P],
                              vnb[:, s, g * HD:(g + 1) * HD], pt[:, i % 2, e, s, :], s == 0, s == blk)
            last.then_inc(sem("att_out"), 1)

        att_scores(0)
        for i in range(8):
            if i + 1 < 8:
                att_scores(i + 1)
            att_values(i)
        pe.wait_ge(sem("q_spread"), 1)
        pe.wait_ge(sem("window_ready"), 1)
        for b in range(NSM):
            for G in range(2):
                last = mm(pb[:, 3, 0:WINDOW], qbd[:, b, G, :], kw[:, G, b, :], b == 0 and G == 0,
                          b == NSM - 1 and G == 1)
        last.then_inc(sem("att_s_scores"), 1)
        pe.wait_ge(sem("att_s_probs"), 1)
        pe.transpose(pb[:, 3, 128:256], ss_s, ident).then_inc(sem("att_s_turned"), 1)
        pe.wait_ge(sem("att_s_kept"), 1)
        pe.wait_ge(sem("vw_in"), 32)
        for b in range(NSM):
            for G in range(2):
                o = 256 + (b * 2 + G) * 8
                last = mm(pb[:, 3, o:o + 8], vw[:, b, G * P:(G + 1) * P], pt_s[:, b * 16 + G * 8:b * 16 + G * 8 + 8])
        last.then_inc(sem("att_s_out"), 1)
        pe.wait_ge(sem("ot_ready"), 1)
        project(ot, DC)
        norm(2)
        peer(1)
        norm(3)

    @block.scalar
    def _(act):
        group = [0]
        chain = [0]

        def link(ins):
            chain[0] += 1
            ins.then_inc(sem("act_chain"), 1)
            act.wait_ge(sem("act_chain"), chain[0])

        def bank(units):
            act.wait_ge(units_used, units)
            group[0] += 1
            return pa[:, (group[0] - 1) % 4, 0:T]

        def norm(li):
            act.wait_ge(sem("ln_centred"), li + 1)
            nc.scalar.activation(sq, x[:, :, :], ACT.Square).then_inc(sem("ln_square"), 1)
            act.wait_ge(sem("ln_var"), li + 1)
            nc.scalar.activation(rstd, pb[:, 1, 0:T], ACT.Sqrt, bias=cst("eps")).then_inc(sem("ln_std"), 1)

        def peer(L):
            act.wait_ge(sem("skeys_in"), 16 * (L + 1))
            for h in range(2 * PH):
                src = bank(U_PQ[L] + h + 1)
                nc.scalar.copy(pq[:, h, :], src).then_inc(evacuated, 1)
            for a, (t0, n) in enumerate(TILES):
                act.wait_ge(sem("scores_done"), 3 * L + a + 1)
                nc.scalar.copy(scores[0:n, a].rearrange("p h n -> p (h n)"),
                               pb[0:n, :, :].rearrange("p b n -> p (b n)")).then_inc(sem("scores_copied"), 1)
            g0 = group[0]
            with act.Fori(0, NK // 4) as it:
                for k in range(4):
                    act.wait_ge(units_used, it * 4 + (U_U[L] + k + 1))
                    nc.scalar.activation(big[:, bass.ds(it * (4 * T) + k * T, T)], pa[:, (g0 + k) % 4, 0:T],
                                         ACT.Gelu).then_inc(evacuated, 1)
            group[0] += NK
            act.wait_ge(sem("best_shifted"), L + 1)
            for a, (t0, n) in enumerate(TILES):
                v = best_s[0:n, a].rearrange("p h k -> p (h k)")
                last = nc.scalar.activation(v, v, ACT.Exp)
            last.then_inc(sem("best_exp"), 1)
            with act.Fori(0, T // 24) as it:
                for s in range(3):
                    n = it * 3 + (33 * L + s + 1)
                    v = hot[:, s, 1, :, :]
                    act.wait_ge(sem("lane_minus_j"), n)
                    nc.scalar.activation(v, v, ACT.Abs).then_inc(sem("lane_abs"), 1)
                    act.wait_ge(sem("lane_abs"), n)
                    nc.scalar.activation(v, v, ACT.Relu, bias=1.0, scale=-1.0).then_inc(sem("hot_j"), 1)
            for m in range(DC):
                src = bank(U_V[L] + 16 * (m + 1))
                nc.scalar.copy(sub[:, m, :], src).then_inc(evacuated, 1)

        act.wait_ge(sem("gate_in"), 80)
        act.wait_ge(sem("gate_pre"), 1)
        nc.scalar.activation(rows[0:HA, 0, 0:T], pb[0:HA, 0, 0:T], ACT.Identity, bias=b_rows[0:HA, 0:1]).then_inc(
            sem("gate_i"), 1)
        link(nc.scalar.activation(rows[0:HA, 1, 0:T], pb[0:HA, 1, 0:T], ACT.Identity, bias=b_rows[0:HA, 1:2]))
        link(nc.scalar.activation(rows[0:HA, 2, 0:T], rows[0:HA, 1, 0:T], ACT.Abs))
        link(nc.scalar.activation(rows[0:HA, 2, 0:T], rows[0:HA, 2, 0:T], ACT.Exp, scale=-1.0))
        nc.scalar.activation(rows[0:HA, 2, 0:T], rows[0:HA, 2, 0:T], ACT.Ln, bias=1.0).then_inc(sem("gate_soft"), 1)
        act.wait_ge(sem("gate_scanned"), 1)
        nc.scalar.activation(rows[0:HA, 6, 0:T], rows[0:HA, 6, 0:T], ACT.Exp, scale=-1.0)
        nc.scalar.activation(rows[0:HA, 7, :], rows[0:HA, 7, :], ACT.Exp).then_inc(sem("gate_exps"), 1)
        act.wait_ge(sem("cols_in"), 16)
        for c in range(IC):
            src = bank(U_IN + c + 1)
            b = col("b_in", c)
            nc.scalar.activation(xp[:, c, 3:3 + TP], src[:, 0:TP], ACT.Identity, bias=b)
            nc.scalar.activation(xp[:, c, TP + 6:XPW:4], src[:, TP:T], ACT.Identity, bias=b).then_inc(evacuated, 1)
        for c in range(IC):
            src = bank(U_IN + IC + c + 1)
            nc.scalar.activation(so[:, c, :], src, ACT.Sigmoid, bias=col("b_in", IC + c)).then_inc(evacuated, 1)
        for c in range(IC):
            act.wait_ge(sem("conv_summed"), c + 1)
            acc = conv_acc[:, c % 2, :]
            nc.scalar.activation(xc[:, c, 0:TP], acc[:, 0:TP], ACT.Silu, bias=col("conv_b", c))
            nc.scalar.activation(xc[:, c, TP:T], acc[:, TP + 3:XPW - 3:4], ACT.Silu,
                                 bias=col("conv_b", c)).then_inc(sem("conv_done"), 1)

        def head_keep(h):
            n = U_QKV + 6 * h
            if h >= 2:
                act.wait_ge(sem("head_done"), h - 1)
                act.wait_ge(sem("head_gated"), h - 1)
            for i, (dst, scale) in enumerate(((qt, 1.0), (kt, DH ** -0.5))):
                for m in range(HC):
                    src = bank(n + 2 * i + m // 2 + 1)
                    nc.scalar.mul(dst[:, h % 2, m, :], src, scale).then_inc(evacuated, 1)
            act.wait_ge(units_used, n + 6)
            for s in range(2):
                nc.scalar.copy(vn[:, h % 2, s, :], pb[:, s, :])
            nc.scalar.copy(vs[0:NSM, h % 2, :], pb[0:NSM, 2, :]).then_inc(sem("v_kept"), 1)

        head_keep(0)
        for h in range(HA):
            if h + 1 < HA:
                head_keep(h + 1)
            act.wait_ge(sem("decay_arg"), h + 1)
            nc.scalar.activation(p0, p0, ACT.Exp)
            nc.scalar.activation(p1, p1, ACT.Exp).then_inc(sem("decay_exp"), 1)
            act.wait_ge(sem("den_done"), h + 1)
            if h:
                act.wait_ge(sem("num_used"), h)
            nc.scalar.activation(den, pb[:, 3, 0:TP], ACT.Abs).then_inc(sem("den_kept"), 1)
            if h:
                act.wait_ge(sem("c_stored"), 16 * h)
            for c in range(HC):
                act.wait_ge(sem("c_done"), HC * h + c + 1)
                nc.scalar.copy(c_out[:, c, :], pb[:, 2 + c % 2, :]).then_inc(sem("c_kept"), 1)
            act.wait_ge(sem("n_done"), h + 1)
            nc.scalar.copy(n_prompt[:, h, :], pb[:, 0, 0:HC]).then_inc(sem("n_kept"), 1)
            for b in range(NSM):
                n = NSM * h + b
                act.wait_ge(sem(f"state_in_{n % 3}"), 16 * (n // 3 + 1))
                v = cs[:, n % 3].rearrange("p c e -> p (c e)")
                nc.scalar.mul(v, v, sg[:, h, NSM + b:NSM + b + 1]).then_inc(sem("state_decayed"), 1)
            act.wait_ge(sem("den_s_done"), h + 1)
            nc.scalar.activation(den_s[0:NSM, 0:1], pb[0:NSM, 0, 4:5], ACT.Abs).then_inc(sem("den_s_kept"), 1)
        for m in range(DC):
            src = bank(U_OUT + 2 * (m + 1))
            nc.scalar.copy(sub[:, m, :], src).then_inc(evacuated, 1)
        norm(0)
        peer(0)
        norm(1)
        for c in range(2):
            src = bank(U_KV + c + 1)
            nc.scalar.copy(ktb[:, c, :], src).then_inc(evacuated, 1)
        act.wait_ge(units_used, U_KV + 4)
        for s in range(2):
            nc.scalar.copy(vnb[:, s, :], pb[:, s, 0:256])
        nc.scalar.copy(vsb[0:NSM, :], pb[0:NSM, 2, 0:256]).then_inc(sem("vb_kept"), 1)
        for c in range(DC):
            src = bank(U_BQ + c + 1)
            nc.scalar.copy(qb[:, c, :], src).then_inc(evacuated, 1)
        for i in range(8):
            nk = P * (1 + i // 4)
            act.wait_ge(sem("att_shifted"), i + 1)
            nc.scalar.activation(ss[:, i % 2, :, 0:nk], ss[:, i % 2, :, 0:nk], ACT.Exp)
            nc.scalar.activation(dx[:, i % 2, :], dx[:, i % 2, :], ACT.Exp).then_inc(sem("att_exp"), 1)
            act.wait_ge(sem("att_turned"), i + 1)
            nb = i // 4 + 1
            src = pb[:, 0:2, :].rearrange("p b (e s q) -> p (b e) s q", e=2, s=2)
            nc.scalar.copy(pt[:, i % 2, :, 0:nb, :], src[:, :, 0:nb, :]).then_inc(sem("att_turned_kept"), 1)
        act.wait_ge(sem("att_s_shifted"), 1)
        nc.scalar.activation(ss_s, ss_s, ACT.Exp)
        nc.scalar.activation(small_s[:, 1:2], small_s[:, 1:2], ACT.Exp).then_inc(sem("att_s_exp"), 1)
        for m in range(DC):
            src = bank(U_BO + m + 1)
            nc.scalar.copy(sub[:, m, :], src).then_inc(evacuated, 1)
        norm(2)
        peer(1)
        norm(3)
        act.wait_ge(sem("x_ready"), 4)
        act.dma_start(io["y"], x[:, :, :]).then_inc(sem("y_out"), 16)
        act.wait_ge(sem("y_out"), 16)

    @block.vector
    def _(dve):
        V = nc.vector
        chain = [0]

        def link(ins):
            chain[0] += 1
            ins.then_inc(sem("dve_chain"), 1)
            dve.wait_ge(sem("dve_chain"), chain[0])

        def norm(li, gn, bn, L):
            link(V.scalar_tensor_tensor(x[:, :, :], x[:, :, :], ALPHA, sub, ALU.mult, ALU.add))
            V.engine_nop().then_inc(sem("ln_sum"), 1)
            dve.wait_ge(sem("ln_mean"), li + 1)
            link(V.tensor_tensor(x[:, :, :], x[:, :, :], pb[:, 0:1, 0:T].to_broadcast([P, DC, T]), ALU.subtract))
            V.engine_nop().then_inc(sem("ln_centred"), 1)
            dve.wait_ge(sem("ln_std"), li + 1)
            link(V.reciprocal(rstd, rstd))
            link(V.tensor_tensor(x[:, :, :], x[:, :, :],
                                 tmp[:, 0:T].rearrange("p (o t) -> p o t", o=1).to_broadcast([P, DC, T]), ALU.mult))
            for c in range(DC):
                last = V.tensor_scalar(x[:, c, :], x[:, c, :], col(gn, L * DC + c), col(bn, L * DC + c),
                                       ALU.mult, ALU.add)
            last.then_inc(sem("x_ready"), 1)
            dve.wait_ge(sem("x_ready"), li + 1)

        def top16(vals, outs, idx, n):
            for step in range(2):
                o = slice(8 * step, 8 * step + 8)
                for v, s in zip(vals, outs):
                    last = V.max(s[:, o], v)
                link(last)
                for v, s, i in zip(vals, outs, idx):
                    last = V.max_index(i[:, o], s[:, o], v)
                if step == 0:
                    for v, s in zip(vals, outs):
                        last = V.match_replace(v, s[:, o], v, LOWEST)
                link(last)

        def choose(L, a, n):
            dve.wait_ge(sem("scores_copied"), 3 * L + a + 1)
            sc = scores[0:n, a]
            top16([sc[:, h] for h in range(2 * PH)], [top_s[0:n, h] for h in range(2 * PH)],
                  [top_iu[0:n, h] for h in range(2 * PH)], n)
            ts = top_s[0:n].rearrange("p (h two) k -> p h two k", two=2)
            cand = sc.rearrange("p (h two) (b c) -> p h (two b) c", two=2, c=TOPK)
            for h in range(PH):
                last = V.tensor_tensor(cand[:, h], ts[:, h, 0, :].rearrange("p (k o) -> p k o", o=1).to_broadcast(
                    [n, TOPK, TOPK]), ts[:, h, 1:2, :].to_broadcast([n, TOPK, TOPK]), ALU.add)
            link(last)
            link(V.tensor_copy(top_if[0:n], top_iu[0:n]))
            flat = sc.rearrange("p (h two) c -> p h (two c)", two=2)
            bs = best_s[0:n, a]
            top16([flat[:, h] for h in range(PH)], [bs[:, h] for h in range(PH)],
                  [best_u[0:n, h] for h in range(PH)], n)
            for half, (op, arg) in enumerate(((ALU.logical_shift_right, 4), (ALU.bitwise_and, 15))):
                link(V.tensor_scalar(rank_u[0:n], best_u[0:n], arg, None, op))
                link(V.tensor_copy(rank_f[0:n, half], rank_u[0:n]))
            i16 = cst("iota16", n).rearrange("p (o k) -> p o k", o=1).to_broadcast([n, TOPK, TOPK])
            tf = top_if[0:n].rearrange("p (h two) k -> p h two k", two=2)
            for half, dst in enumerate((sel_i, sel_j)):
                for hq in range(PH // 4):
                    eq = tmp[0:n].rearrange("p (h k r) -> p h k r", h=4, r=TOPK)
                    for e in range(4):
                        h = 4 * hq + e
                        last = V.tensor_tensor(eq[:, e], rank_f[0:n, half, h, :].rearrange(
                            "p (k o) -> p k o", o=1).to_broadcast([n, TOPK, TOPK]), i16, ALU.is_equal)
                    link(last)
                    for e in range(4):
                        last = V.tensor_tensor(eq[:, e], eq[:, e], tf[:, 4 * hq + e, half:half + 1, :].to_broadcast(
                            [n, TOPK, TOPK]), ALU.mult)
                    link(last)
                    link(V.tensor_reduce(dst[0:n, a, 64 * hq:64 * (hq + 1)],
                                         tmp[0:n].rearrange("p (k r) -> p k r", r=TOPK), AX.X, ALU.add))
            V.tensor_copy(gsum[0:n, a, :], bs[:, :, 0])
            link(V.engine_nop())
            link(V.tensor_tensor(bs, bs, gsum[0:n, a, :].rearrange("p (h o) -> p h o", o=1).to_broadcast(
                [n, PH, TOPK]), ALU.subtract))

        def peer(L):
            for a, (t0, n) in enumerate(TILES):
                choose(L, a, n)
            V.engine_nop().then_inc(sem("best_shifted"), 1)
            dve.wait_ge(sem("best_exp"), L + 1)
            for a, (t0, n) in enumerate(TILES):
                last = V.tensor_reduce(gsum[0:n, a, :], best_s[0:n, a], AX.X, ALU.add)
            link(last)
            for a, (t0, n) in enumerate(TILES):
                last = V.reciprocal(gsum[0:n, a, :], gsum[0:n, a, :])
            link(last)
            for a, (t0, n) in enumerate(TILES):
                last = V.tensor_tensor(best_s[0:n, a], best_s[0:n, a], gsum[0:n, a, :].rearrange(
                    "p (h o) -> p h o", o=1).to_broadcast([n, PH, TOPK]), ALU.mult)
            last.then_inc(sem("gates_done"), 1)
            dve.wait_ge(sem("choice_turned"), L + 1)
            V.tensor_copy(turned[:, :, :], pb[:, 0:3, 0:T]).then_inc(sem("choice_kept"), 1)
            dve.wait_ge(sem("choice_kept"), L + 1)

            def hot_i(it, s):
                for t in range(8):
                    c = it * 24 + (8 * s + t)
                    last = V.tensor_scalar(hot[:, s, 0, t, :], iota, turned[:, 0, bass.ds(c, 1)],
                                           turned[:, 2, bass.ds(c, 1)], ALU.is_equal, ALU.mult)
                last.then_inc(sem("hot_i"), 1)

            def apply(it, s, n):
                dve.wait_ge(sem("gates_spread"), n + 1)
                w = big[:, :].rearrange("p (i t) -> p i t", t=T)[:, :, bass.ds(it * 24 + 8 * s, 8)]
                g = gate_bank(s).rearrange("p b (t i) -> p i (b t)", t=4)
                V.tensor_tensor(w, w, g, ALU.mult).then_inc(sem("gates_applied"), 1)

            n0 = 33 * L
            for s in range(3):
                hot_i(0, s)
                if s:
                    apply(0, s - 1, n0 + s - 1)
            with dve.Fori(1, T // 24) as it:
                for s in range(3):
                    n = it * 3 + (n0 + s)
                    dve.wait_ge(sem("gates_spread"), n - 2)
                    hot_i(it, s)
                    if s:
                        apply(it, s - 1, n - 1)
                    else:
                        apply(it - 1, 2, n - 1)
            apply(T // 24 - 1, 2, n0 + 32)
            dve.wait_ge(evacuated, peer_groups[L])

        link(V.memset(rt[0:HB, :], NEG))
        dve.wait_ge(sem("bias_rows"), 1)
        V.tensor_copy(rt[0:HB, WINDOW:2 * WINDOW], pb[0:HB, 2, 0:WINDOW]).then_inc(sem("bias_rows_kept"), 1)
        V.memset(qm, 0.0)
        V.memset(xp[:, :, 0:3], 0.0)
        dve.wait_ge(sem("conv_in"), 16)
        link(V.tensor_copy(xp[:, :, 3 + TP:XPW].rearrange("p c (b w) -> p c b w", w=4)[:, :, :, 0:3], conv_in))
        dve.wait_ge(sem("gate_soft"), 1)
        R = rows[0:HA]
        r = lambda i, a=0, b=T: R[:, i, a:b]
        link(V.scalar_tensor_tensor(r(1), r(1), 0.0, r(2), ALU.min, ALU.subtract))
        link(V.tensor_tensor_scan(r(3, 0, TP), ones[0:HA, 0:TP], r(1, 0, TP), 0.0, ALU.mult, ALU.add))
        link(V.tensor_tensor(r(4, 0, TP), r(0, 0, TP), r(3, 0, TP), ALU.subtract))
        link(V.tensor_tensor_scan(r(2, 0, TP), ones[0:HA, 0:TP], r(4, 0, TP), 0.0, ALU.mult, ALU.max))
        V.tensor_scalar(r(5, 0, TP), r(2, 0, TP), -1.0, None, ALU.mult)
        V.tensor_tensor(r(6, 0, TP), r(3, 0, TP), r(2, 0, TP), ALU.add)
        V.tensor_scalar(r(7, 0, TP), r(4, 0, TP), r(2, TP - 1, TP), None, ALU.subtract)
        link(V.tensor_tensor(r(3, TP, T), r(1, TP, T), m_in[0:HA, :], ALU.add))
        link(V.tensor_tensor(r(6, TP, T), r(3, TP, T), r(0, TP, T), ALU.max))
        V.tensor_tensor(r(7, TP, T), r(0, TP, T), r(6, TP, T), ALU.subtract)
        V.tensor_copy(m_out[0:HA, 0:1], r(6, TP - 1, TP))
        V.tensor_copy(m_out[0:HA, 1:1 + NSM], r(6, TP, T)).then_inc(sem("m_kept"), 1)
        V.tensor_tensor(r(7, T, T + NSM), r(3, TP, T), r(6, TP, T), ALU.subtract).then_inc(sem("gate_scanned"), 1)
        dve.wait_ge(sem("gate_cols"), 1)
        V.tensor_copy(gcol, pb[:, 2, 0:16])
        V.tensor_copy(em_s[0:NSM, :], pb[0:NSM, 2, 16:20])
        link(V.tensor_copy(sg.rearrange("p h n -> p (h n)"), pb[:, 3, 0:64]))
        V.engine_nop().then_inc(sem("gate_cols_kept"), 1)
        dve.wait_ge(evacuated, 2 * IC)
        dve.wait_ge(sem("cols_in"), 16)
        N = XPW - 3
        for c in range(IC):
            acc = conv_acc[:, c % 2, :]
            if c >= 2:
                dve.wait_ge(sem("conv_done"), c - 1)
            link(V.tensor_scalar(acc, xp[:, c, 3:3 + N], col("conv_w", 3 * IC + c), None, ALU.mult))
            for w in (2, 1, 0):
                ins = V.scalar_tensor_tensor(acc, xp[:, c, w:w + N], col("conv_w", w * IC + c), acc,
                                             ALU.mult, ALU.add)
                if w:
                    link(ins)
            ins.then_inc(sem("conv_summed"), 1)
        V.tensor_copy(conv_out[:, :, 0:3], xp[:, :, TP:TP + 3])
        V.tensor_copy(conv_out[:, :, 3:].rearrange("p c (b w) -> p c b w", w=3),
                      xp[:, :, 3 + TP:XPW].rearrange("p c (b w) -> p c b w", w=4)[:, :, :, 1:4]).then_inc(
            sem("conv_kept"), 1)

        for h in range(HA):
            q, k = qt[:, h % 2], kt[:, h % 2]
            dve.wait_ge(sem("rows_spread"), h + 1)
            V.tensor_copy(em, pb[:, 3, TP:2 * TP])
            V.tensor_scalar(p0, pb[:, 3, 0:TP], gcol[:, h:h + 1], 0.0, ALU.add, ALU.min)
            V.tensor_scalar(p1, pb[:, 3, P:TP], gcol[:, HA + h:HA + h + 1], 0.0, ALU.add, ALU.min).then_inc(
                sem("decay_arg"), 1)
            dve.wait_ge(sem("k_turned"), h + 1)
            for s in range(2):
                V.tensor_scalar(wk[:, s, :], pb[:, s, :], gcol[:, 8 + HA * s + h:9 + HA * s + h], None, ALU.mult)
            dve.wait_ge(sem("decay_exp"), h + 1)
            V.tensor_tensor(p0[:, 0:P], p0[:, 0:P], causal, ALU.mult)
            link(V.tensor_tensor(p1, p1, causal, ALU.mult))
            V.tensor_tensor(p0, p0, pb[:, 2, 0:TP], ALU.mult)
            V.tensor_tensor(p1, p1, pb[:, 2, TP:TP + P], ALU.mult).then_inc(sem("weights_t"), 1)
            dve.wait_ge(sem("den_kept"), h + 1)
            link(V.tensor_tensor(den, den, em, ALU.max))
            link(V.reciprocal(den, den))
            dve.wait_ge(sem("num_done"), h + 1)
            link(V.tensor_tensor(hn, pb[:, 0:2, :].rearrange("p b (c t) -> p (b c) t", t=TP),
                                 den.rearrange("p (o t) -> p o t", o=1).to_broadcast([P, HC, TP]), ALU.mult))
            sov = so[:, h * HC:(h + 1) * HC, 0:TP]
            V.tensor_tensor(sov, sov, hn, ALU.mult).then_inc(sem("num_used"), 1)
            if h == 0:
                dve.wait_ge(sem("state_n_in"), 16)
            if h:
                dve.wait_ge(sem("state_read"), NSM * h)
            ws = sg[:, h, 0:NSM].rearrange("p (o b) -> p o b", o=1).to_broadcast([P, HC, NSM])
            wd = sg[:, h, NSM:2 * NSM].rearrange("p (o b) -> p o b", o=1).to_broadcast([P, HC, NSM])
            V.tensor_tensor(kws, k[:, :, TP:T], ws, ALU.mult)
            for c in range(HC):
                V.tensor_copy(qm[:, c].rearrange("p a b -> p (a b)")[:, 0:64:9], q[:, c, TP:T])
            link(V.tensor_tensor(n_new[:, h], n_in[:, h], wd, ALU.mult))
            link(V.tensor_tensor(n_new[:, h], n_new[:, h], kws, ALU.add))
            V.tensor_tensor(qn, q[:, :, TP:T], n_new[:, h], ALU.mult).then_inc(sem("sample_ready"), 1)
            for b in range(NSM):
                n = NSM * h + b
                dve.wait_ge(sem("v_spread"), n + 1)
                dve.wait_ge(sem("state_decayed"), n + 1)
                for c in range(HC):
                    st = cs[:, n % 3, c, :]
                    last = V.scalar_tensor_tensor(st, pb[:, 2 + b % 2, :], kws[:, c, b:b + 1], st,
                                                  ALU.mult, ALU.add)
                last.then_inc(sem("state_new"), 1)
            dve.wait_ge(sem("den_s_kept"), h + 1)
            link(V.tensor_tensor(den_s[0:NSM, 0:1], den_s[0:NSM, 0:1], em_s[0:NSM, h:h + 1], ALU.max))
            link(V.reciprocal(den_s[0:NSM, 1:2], den_s[0:NSM, 0:1]))
            dve.wait_ge(sem("state_read"), NSM * (h + 1))
            V.tensor_scalar(hs[0:NSM, :], pb[0:NSM, 1, :], den_s[0:NSM, 1:2], None, ALU.mult).then_inc(
                sem("h_sample"), 1)
            dve.wait_ge(sem("head_done"), h + 1)
            sov = so[:, h * HC:(h + 1) * HC, TP:T]
            V.tensor_tensor(sov, sov, pb[:, 0, 8:8 + HC * NSM].rearrange("p (c b) -> p c b", b=NSM),
                            ALU.mult).then_inc(sem("head_gated"), 1)
        dve.wait_ge(evacuated, out_groups)
        norm(0, "mix_g", "mix_b", 0)
        peer(0)
        norm(1, "ffn_g", "ffn_b", 0)
        V.memset(qbd, 0.0)
        dve.wait_ge(evacuated, kv_groups)
        dve.wait_ge(sem("kw_in"), 16)
        V.tensor_copy(kw[:, :, :, WINDOW - 1], ktb[:, :, TP:T]).then_inc(sem("window_ready"), 1)
        dve.wait_ge(evacuated, bq_groups)
        link(V.engine_nop())
        pitch = qbd.ap[0][0]
        for half in range(2):
            rr = slice(half * HD, (half + 1) * HD)
            base = qbd[rr, 0, 0, 2 * half:2 * half + 1]
            for G in range(2):
                dst = bass.AP(base.tensor, base.offset + G * (P + 8),
                              [[pitch, HD], [4, 2], [1, 2], [2 * P + 16, NSM]])
                last = V.tensor_copy(dst, qb[rr, 4 * G:4 * G + 4, TP:T].rearrange("p (a c) b -> p a c b", c=2))
        last.then_inc(sem("q_spread"), 1)
        dve.wait_ge(sem("bias_b_in"), 64)
        for i in range(8):
            blk, g4 = i // 4, i % 4
            nk = P * (blk + 1)
            s4 = ss[:, i % 2, :, 0:nk]
            dve.wait_ge(sem("att_scores"), i + 1)
            if i >= 2:
                dve.wait_ge(sem("att_turned"), i - 1)
            src = pa[:, 2 * (i % 2):2 * (i % 2) + 2, :].rearrange("p b (e k) -> p (b e) k", e=2)[:, :, 0:nk]
            link(V.scalar_tensor_tensor(s4, src, HD ** -0.5, bias[:, 4 * g4:4 * g4 + 4, 2 * P - nk:2 * P],
                                        ALU.mult, ALU.add))
            V.engine_nop().then_inc(sem("att_scored"), 1)
            m, sk, dn = mx[:, i % 2, :], sink[:, 4 * g4:4 * g4 + 4], dx[:, i % 2, :]
            link(V.tensor_reduce(m, s4, AX.X, ALU.max))
            link(V.tensor_tensor(m, m, sk, ALU.max))
            V.tensor_tensor(dn, sk, m, ALU.subtract)
            V.tensor_tensor(s4, s4, m.rearrange("p (e o) -> p e o", o=1).to_broadcast([P, 4, nk]),
                            ALU.subtract).then_inc(sem("att_shifted"), 1)
            dve.wait_ge(sem("att_exp"), i + 1)
            link(V.tensor_reduce(sx[:, i % 2, :], s4, AX.X, ALU.add))
            link(V.tensor_tensor(dn, dn, sx[:, i % 2, :], ALU.add))
            link(V.reciprocal(dn, dn))
            V.tensor_tensor(s4, s4, dn.rearrange("p (e o) -> p e o", o=1).to_broadcast([P, 4, nk]),
                            ALU.mult).then_inc(sem("att_probs"), 1)
            dve.wait_ge(sem("att_out"), i + 1)
            V.tensor_copy(ot[:, 2 * g4:2 * g4 + 2, blk * P:(blk + 1) * P],
                          pb[:, 2, 0:2 * P].rearrange("p (c q) -> p c q", c=2)).then_inc(sem("att_out_kept"), 1)
        dve.wait_ge(sem("att_s_scores"), 1)
        link(V.scalar_tensor_tensor(ss_s, pb[:, 3, 0:WINDOW], HD ** -0.5, bias_s, ALU.mult, ALU.add))
        link(V.tensor_reduce(small_s[:, 0:1], ss_s, AX.X, ALU.max))
        link(V.tensor_tensor(small_s[:, 0:1], small_s[:, 0:1], sink_s, ALU.max))
        V.tensor_tensor(small_s[:, 1:2], sink_s, small_s[:, 0:1], ALU.subtract)
        V.tensor_scalar(ss_s, ss_s, small_s[:, 0:1], None, ALU.subtract).then_inc(sem("att_s_shifted"), 1)
        dve.wait_ge(sem("att_s_exp"), 1)
        link(V.tensor_reduce(small_s[:, 2:3], ss_s, AX.X, ALU.add))
        link(V.tensor_tensor(small_s[:, 2:3], small_s[:, 2:3], small_s[:, 1:2], ALU.add))
        link(V.reciprocal(small_s[:, 3:4], small_s[:, 2:3]))
        V.tensor_scalar(ss_s, ss_s, small_s[:, 3:4], None, ALU.mult).then_inc(sem("att_s_probs"), 1)
        dve.wait_ge(sem("att_s_turned"), 1)
        V.tensor_copy(pt_s, pb[:, 3, 128:256]).then_inc(sem("att_s_kept"), 1)
        dve.wait_ge(sem("att_s_out"), 1)
        for half in range(2):
            rr = slice(half * HD, (half + 1) * HD)
            src = pb[rr, 3, 256:256 + NSM * 16].rearrange("p (b a h c) -> p a c b h", b=NSM, h=2, c=2)
            last = V.tensor_copy(ot[rr, :, TP:T].rearrange("p (a c) b -> p a c b", c=2), src[:, :, :, :, half])
        last.then_inc(sem("ot_ready"), 1)
        dve.wait_ge(evacuated, bo_groups)
        norm(2, "mix_g", "mix_b", 1)
        peer(1)
        norm(3, "ffn_g", "ffn_b", 1)

    @block.gpsimd
    def _(pool):
        pool.dma_start(relb[0:NB, :], io["rel_bias"]).then_inc(sem("bias_in"), 16)
        pool.dma_start(onehot[0:NB, :], io["onehot"]).then_inc(sem("bias_in"), 16)
        pool.wait_ge(sem("bias_rows_kept"), 1)
        pool.dma_start(io["bias_rows"], rt[0:HB, :].rearrange("p (o w) -> p o w", o=1).to_broadcast(
            [HB, P, BIASW])).then_inc(sem("bias_stored"), 16)
        for n in range(3):
            pool.dma_start(cs[:, n], io["state_in"][n]).then_inc(sem(f"state_in_{n}"), 16)
        pool.wait_ge(sem("m_kept"), 1)
        pool.dma_start(io["m_out"], m_out[0:HA, :]).then_inc(sem("small_out"), 16)
        pool.wait_ge(sem("conv_kept"), 1)
        pool.dma_start(io["conv_out"], conv_out).then_inc(sem("small_out"), 16)
        for h in range(HA):
            pool.wait_ge(sem("c_kept"), HC * (h + 1))
            pool.dma_start(io["c_prompt"][h], c_out).then_inc(sem("c_stored"), 16)
            for b in range(NSM):
                n = NSM * h + b
                pool.wait_ge(sem("state_new"), n + 1)
                pool.dma_start(io["state_out"][n], cs[:, n % 3]).then_inc(sem(f"state_out_{n % 3}"), 16)
                if n >= 1 and n + 2 < NSM * HA:
                    o = n - 1
                    pool.wait_ge(sem("state_read"), o + 1)
                    pool.wait_ge(sem(f"state_out_{o % 3}"), 16 * (o // 3 + 1))
                    pool.dma_start(cs[:, o % 3], io["state_in"][n + 2]).then_inc(sem(f"state_in_{o % 3}"), 16)
        pool.wait_ge(sem("head_gated"), HA)
        pool.wait_ge(sem("n_kept"), HA)
        pool.dma_start(io["n_prompt"], n_prompt).then_inc(sem("small_out"), 16)
        pool.dma_start(io["n_sample"], n_new).then_inc(sem("small_out"), 16)
        pool.wait_ge(sem("small_out"), 64)
        pool.wait_ge(sem("c_stored"), 16 * HA)
        for s in range(3):
            pool.wait_ge(sem(f"state_out_{s}"), 16 * ((NSM * HA - s + 2) // 3))

        def load_skeys(L):
            pool.dma_start(skeys, io["skeys"][L]).then_inc(sem("skeys_in"), 16)

        def hot_j(L):
            pool.wait_ge(sem("choice_kept"), L + 1)
            io_b = iota.rearrange("p (o n) -> p o n", o=1).to_broadcast([P, 8, NK])

            def one(it, s):
                v = turned[:, 1, bass.ds(it * 24 + 8 * s, 8)].rearrange("p (t o) -> p t o", o=1)
                nc.gpsimd.tensor_tensor(hot[:, s, 1, :, :], io_b, v.to_broadcast([P, 8, NK]),
                                        ALU.subtract).then_inc(sem("lane_minus_j"), 1)

            for s in range(3):
                one(0, s)
            with pool.Fori(1, T // 24) as it:
                for s in range(3):
                    pool.wait_ge(sem("gates_spread"), it * 3 + (33 * L + s - 2))
                    one(it, s)

        pool.wait_ge(sem("ln_sum"), 1)
        load_skeys(0)
        hot_j(0)
        pool.wait_ge(sem("x_ready"), 2)
        pool.dma_start(kw[:, :, :, 0:WINDOW - 1], io["kw_in"]).then_inc(sem("kw_in"), 16)
        pool.dma_start(vw[0:WINDOW - 1], io["vw_in"]).then_inc(sem("vw_in"), 16)
        pool.wait_ge(sem("bias_stored"), 16)
        br = io["bias_rows"]
        pool.dma_start(bias, bass.AP(br.tensor, br.offset + WINDOW - 1,
                                     [[BIASW - 1, P], [P * BIASW, HB], [1, 2 * WINDOW]])).then_inc(sem("bias_b_in"), 16)
        pool.dma_start(bias_s, bass.AP(br.tensor, br.offset + WINDOW,
                                       [[0, NSM], [P * BIASW, HB], [1, WINDOW]])).then_inc(sem("bias_b_in"), 16)
        sk = io["sinks"]
        pool.dma_start(sink, bass.AP(sk.tensor, sk.offset, [[0, P], [1, HB]])).then_inc(sem("bias_b_in"), 16)
        pool.dma_start(sink_s, bass.AP(sk.tensor, sk.offset, [[0, NSM], [1, HB], [1, 1]])).then_inc(
            sem("bias_b_in"), 16)
        pool.wait_ge(sem("vb_kept"), 1)
        pool.dma_start(vw[WINDOW - 1:WINDOW, :, :], vsb[0:NSM, :]).then_inc(sem("vw_in"), 16)
        pool.dma_start(io["k_prompt"], ktb[:, :, P:TP]).then_inc(sem("win_out"), 16)
        pool.dma_start(io["v_prompt"], vnb[:, 1, :]).then_inc(sem("win_out"), 16)
        pool.wait_ge(sem("window_ready"), 1)
        pool.dma_start(io["k_sample"], kw).then_inc(sem("win_out"), 16)
        pool.wait_ge(sem("vw_in"), 32)
        pool.dma_start(io["v_sample"], vw).then_inc(sem("win_out"), 16)
        pool.wait_ge(sem("win_out"), 64)
        pool.wait_ge(sem("ln_sum"), 3)
        load_skeys(1)
        hot_j(1)


def _head_order():
    return [4 * (2 * (c // 4) + half) + c % 4 for c in range(DC) for half in range(2)]


def _row_order():
    return [_head_order()[2 * (2 * a + c) + half] for a in range(DC // 2) for half in range(2) for c in range(2)]


def _constants():
    f = np.float32
    c = np.zeros((P, NCONST), f)
    lane = np.arange(P)

    def put(name, v):
        a, n = CONSTS[name]
        c[:, a:a + n] = v
    put("ident", np.eye(P, dtype=f))
    put("iota", np.broadcast_to(lane.astype(f), (P, P)))
    put("iota16", np.broadcast_to(lane[:TOPK].astype(f), (P, TOPK)))
    put("causal", (lane[:, None] <= lane[None, :]).astype(f))
    put("mean", np.full((P, P), 1.0 / D, f))
    put("ones", np.ones((P, 2 * P), f))
    put("eps", np.full((P, 1), LN_EPS, f))
    sel4 = np.zeros((HA, HA, P), f)
    sel8 = np.zeros((NSM, NSM, P), f)
    for i in range(HA):
        sel4[i, i] = 1
    for i in range(NSM):
        sel8[i, i] = 1
    onehot = np.zeros((NB, WINDOW), f)
    exact = NB // 2
    for y in range(WINDOW):
        d = WINDOW - 1 - y
        b = d if d < exact else min(NB - 1, exact + int(np.log(d / exact) / np.log(128 / exact) * (NB - exact)))
        onehot[b, y] = 1
    return c, sel4, sel8, onehot


def kernel(x_prompt, x_sample, state_mlstm_C, state_mlstm_n, state_mlstm_m, state_mlstm_conv,
           cache_k_win, cache_v_win, a_w_in, a_b_in, a_conv_w, a_conv_b, a_w_q, a_w_k, a_w_v,
           a_w_out, kv_w, b_w_q, b_w_o, b_sinks, rel_bias, ln_mix_g, ln_mix_b, ln_ffn_g,
           ln_ffn_b, peer_w_q, peer_subkeys, peer_u, peer_v):
    import concourse.bacc as bacc
    from concourse.bass_utils import run_bass_kernel_spmd

    f = np.float32
    A = lambda a: np.asarray(a)
    order = _head_order()
    rows = _row_order()
    qcols = np.concatenate([np.arange(h * HD, (h + 1) * HD) for h in order])

    units = np.empty((N_UNITS, P, 1024), f)

    def kxm(w):
        m = w.shape[1] // P
        return w.reshape(DC, P, m, P).transpose(2, 1, 0, 3).reshape(m, P, 1024)

    w_in = A(a_w_in)[0]
    units[U_IN:U_QKV] = kxm(w_in[:, 0:2 * INNER])
    for h in range(HA):
        n = U_QKV + 6 * h
        for i, w in enumerate((A(a_w_q)[0, h], A(a_w_k)[0, h])):
            units[n + 2 * i:n + 2 * i + 2] = w.reshape(HC, P, 2, 256).transpose(2, 1, 0, 3).reshape(2, P, 1024)
        units[n + 4:n + 6] = A(a_w_v)[0, h].reshape(2, 2, P, DH).transpose(0, 2, 1, 3).reshape(2, P, 1024)
    units[U_OUT:U_PQ[0]] = A(a_w_out)[0].reshape(2, DC, P, DC, P).transpose(3, 0, 2, 1, 4).reshape(2 * DC, P, 1024)
    kv = A(kv_w)
    units[U_KV:U_KV + 2] = kxm(kv[:, 0:256])
    units[U_KV + 2:U_KV + 4] = kv[:, 256:512].reshape(2, 4, P, 256).transpose(0, 2, 1, 3).reshape(2, P, 1024)
    units[U_BQ:U_BO] = kxm(A(b_w_q)[0][:, qcols])
    units[U_BO:U_PQ[1]] = kxm(A(b_w_o)[0][qcols, :])
    for L in range(2):
        units[U_PQ[L]:U_U[L]] = kxm(A(peer_w_q)[L])
        units[U_U[L]:U_V[L]] = A(peer_u)[L].reshape(NK, NK, DC, P).transpose(0, 3, 2, 1).reshape(NK, P, 1024)
        units[U_V[L]:U_V[L] + NK] = A(peer_v)[L].reshape(16, 8, NK, DC, P).transpose(3, 0, 2, 1, 4).reshape(
            NK, P, 1024)

    def fm(a):
        c = a.shape[-1] // P
        a = np.moveaxis(a, -1, 0)
        return np.moveaxis(a.reshape((c, P) + a.shape[1:]), 0, 1)

    const, sel4, sel8, onehot = _constants()
    xs = np.concatenate([A(x_prompt)[0], A(x_sample)[:, 0]], axis=0)
    b_in = A(a_b_in)[0]
    cols = np.concatenate([
        fm(b_in[0:2 * INNER]).reshape(P, -1),
        np.moveaxis(fm(A(a_conv_w)[0]), 2, 1).reshape(P, -1),
        fm(A(a_conv_b)[0]).reshape(P, -1),
    ] + [np.moveaxis(fm(A(w)), 2, 1).reshape(P, -1) for w in (ln_mix_g, ln_mix_b, ln_ffn_g, ln_ffn_b)], axis=1)
    C = A(state_mlstm_C)[0]
    arrays = {
        "units": units,
        "x": fm(xs),
        "const": const, "cols": cols, "sel4": sel4, "sel8": sel8, "onehot": onehot,
        "w_gate": w_in[:, 2 * INNER:].reshape(DC, P, 8).transpose(1, 0, 2),
        "b_gate": b_in[2 * INNER:].reshape(2, HA).T,
        "m_in": A(state_mlstm_m)[0].T,
        "conv_in": fm(A(state_mlstm_conv)[0]),
        "n_in": A(state_mlstm_n)[0].reshape(NSM, HA, HC, P).transpose(3, 1, 2, 0),
        "state_in": C.transpose(1, 0, 2, 3).reshape(HA * NSM, HC, P, DH).transpose(0, 2, 1, 3),
        "kw_in": A(cache_k_win)[:, 1:].reshape(NSM, WINDOW - 1, 2, P).transpose(3, 2, 0, 1),
        "vw_in": A(cache_v_win)[:, 1:].reshape(NSM, WINDOW - 1, KVH * HD).transpose(1, 0, 2),
        "rel_bias": A(rel_bias)[:, rows],
        "sinks": A(b_sinks)[0][rows],
        "skeys": A(peer_subkeys).transpose(0, 4, 1, 2, 3).reshape(2, P, 2 * PH, NK),
    }
    outs = {
        "y": (P, DC, T), "c_prompt": (HA, P, HC, DH), "n_prompt": (P, HA, HC), "m_out": (HA, 1 + NSM),
        "conv_out": (P, IC, 3 + 3 * NSM), "k_prompt": (P, 2, WINDOW), "v_prompt": (WINDOW, KVH * HD),
        "state_out": (HA * NSM, P, HC, DH), "n_sample": (P, HA, HC, NSM),
        "k_sample": (P, 2, NSM, WINDOW), "v_sample": (WINDOW, NSM, KVH * HD),
    }
    nc = bacc.Bacc("TRN2", target_bir_lowering=False, num_devices=1)
    io, feed = {}, {}
    for name, a in arrays.items():
        a = np.ascontiguousarray(a)
        feed["in_" + name] = a
        io[name] = nc.dram_tensor("in_" + name, a.shape, F32, kind="ExternalInput").ap()
    for name, shape in outs.items():
        io[name] = nc.dram_tensor("out_" + name, shape, F32, kind="ExternalOutput").ap()
    io["bias_rows"] = nc.dram_tensor("bias_rows", (HB, P, BIASW), F32, kind="Internal").ap()
    build(nc, io)
    r = run_bass_kernel_spmd(nc, [feed], core_ids=[0]).results[0]
    o = {name: r["out_" + name] for name in outs}

    y = o["y"].transpose(2, 1, 0).reshape(T, D)
    conv = o["conv_out"].transpose(2, 1, 0).reshape(3 + 3 * NSM, INNER)
    so_ = o["state_out"].reshape(HA, NSM, P, HC, DH).transpose(1, 0, 3, 2, 4).reshape(1, NSM, HA, DH, DH)
    return tuple(np.ascontiguousarray(a) for a in (
        y[:TP].reshape(1, TP, D),
        y[TP:].reshape(NSM, 1, D),
        o["c_prompt"].transpose(0, 2, 1, 3).reshape(1, 1, HA, DH, DH),
        o["n_prompt"].transpose(1, 2, 0).reshape(1, 1, HA, DH),
        o["m_out"][:, 0].reshape(1, 1, HA),
        conv[0:3].reshape(1, 1, 3, INNER),
        o["k_prompt"].transpose(2, 1, 0).reshape(1, WINDOW, KVH, HD),
        o["v_prompt"].reshape(1, WINDOW, KVH, HD),
        so_,
        o["n_sample"].transpose(3, 1, 2, 0).reshape(1, NSM, HA, DH),
        o["m_out"][:, 1:].T.reshape(1, NSM, HA),
        conv[3:].reshape(1, NSM, 3, INNER),
        o["k_sample"].transpose(2, 3, 1, 0).reshape(NSM, WINDOW, KVH, HD),
        o["v_sample"].transpose(1, 0, 2).reshape(NSM, WINDOW, KVH, HD),
    ))
```

```python
from contextlib import ExitStack

import numpy as np

import concourse.bass as bass
from concourse import mybir

F32 = mybir.dt.float32
U32 = mybir.dt.uint32
ALU = mybir.AluOpType
ACT = mybir.ActivationFunctionType
AX = mybir.AxisListType

P = 128
D = 1024
TP = 256
NSM = 8
T = TP + NSM
DC = D // P
INNER = 2048
IC = INNER // P
HA = 4
DH = INNER // HA
HC = DH // P
CONV_W = 4
KVH = 4
GROUP = 4
HB = 16
HD = 64
WINDOW = 128
NB = 32
PH = 8
NK = 128
TOPK = 16
DEPTH = 2
ALPHA = (2 * DEPTH) ** 0.25
LN_EPS = 1e-5
NEG = -1e30
LOWEST = -3.0e38
RING = 4
XPW = 3 + TP + 4 * NSM
BIASW = 3 * WINDOW

U_IN = 0
U_QKV = U_IN + 2 * IC
U_OUT = U_QKV + 6 * HA
U_PQ = [U_OUT + 2 * DC, 0]
U_U = [U_PQ[0] + 2 * PH, 0]
U_V = [U_U[0] + NK, 0]
U_KV = U_V[0] + NK
U_BQ = U_KV + 4
U_BO = U_BQ + DC
U_PQ[1] = U_BO + DC
U_U[1] = U_PQ[1] + 2 * PH
U_V[1] = U_U[1] + NK
N_UNITS = U_V[1] + NK

PHASES = [("pool", U_IN, U_QKV), ("pe", U_QKV, U_PQ[0]), ("pool", U_PQ[0], U_V[0]), ("dve", U_V[0], U_KV),
          ("pe", U_KV, U_BQ), ("pool", U_BQ, U_BO), ("pe", U_BO, U_PQ[1]), ("pool", U_PQ[1], U_V[1]),
          ("dve", U_V[1], N_UNITS)]


def _before(n, *kinds):
    return sum(max(0, min(n, b) - a) for kind, a, b in PHASES if kind in kinds)


def n_split(n):
    return _before(n, "pool", "dve")

COLS = {}
_at = 0
for _n, _c in (("mix_g", 2 * DC), ("mix_b", 2 * DC), ("ffn_g", 2 * DC), ("ffn_b", 2 * DC), ("eps", 1)):
    COLS[_n] = (_at, _c)
    _at += _c
NCOLS = _at
COLS_A = {}
_at = 0
for _n, _c in (("b_in", 2 * IC), ("conv_w", CONV_W * IC), ("conv_b", IC), ("causal", P), ("fold", NSM)):
    COLS_A[_n] = (_at, _c)
    _at += _c
NCOLS_A = _at

CONSTS = {}
_at = 0
for _n, _c in (("ident", P), ("iota", P), ("ones", P)):
    CONSTS[_n] = (_at, _c)
    _at += _c
NCONST = _at
SETS = T // 8
TILES = [(0, P), (P, P), (TP, NSM)]


def build(nc, io):
    with ExitStack() as ctx:
        _build(nc, io, ctx)


def _build(nc, io, ctx):
    def sb(name, shape, dt=F32):
        return ctx.enter_context(nc.sbuf_tensor(name, shape, dt))

    sems = {}

    def sem(name):
        if name not in sems:
            sems[name] = ctx.enter_context(nc.semaphore(name))
        return sems[name]

    f32r = mybir.dt.float32r
    n_big, n_x = NK * T, DC * T
    sizes = [("big", n_big), ("raw", RING * 1024), ("halves", 4096), ("xh", n_x), ("xl", n_x), ("scb", 4096),
             ("top", 528 + 2 * 256 + 2 * 128 + 384 + 768), ("const", NCONST), ("cols", NCOLS)]
    total = sum(n for _, n in sizes)
    sb("arena", [P, total])
    base = nc.sbuf_base - 4 * total
    start = {}
    where = 0
    for name, n in sizes:
        start[name] = where
        where += n

    def area(name):
        return nc.alloc_sbuf_tensor_at(name, [P, dict(sizes)[name]], F32, offset=base + 4 * start[name])[:, :]

    def rounded(name, over, shape, skip=0):
        return nc.alloc_sbuf_tensor_at(name, shape, f32r, offset=base + 4 * (start[over] + skip))

    big = area("big")
    ring = area("raw").rearrange("p (k n) -> p k n", k=RING)
    scb = area("scb")
    const, cols = area("const"), area("cols")
    split = rounded("split", "halves", [P, 4, 2, 512])
    xh = rounded("xh", "xh", [P, DC, T])
    xl = rounded("xl", "xl", [P, DC, T])
    wsplit = rounded("wsplit", "scb", [P, 4, 2, T])
    xh_f, xl_f, split_f, wsplit_f = (v[:].bitcast(F32) for v in (xh, xl, split, wsplit))

    def cst(name, rows=P):
        a, n = CONSTS[name]
        return const[0:rows, a:a + n]

    def col(name, i):
        return cols[:, COLS[name][0] + i:COLS[name][0] + i + 1]

    ident, iota, ones = cst("ident"), cst("iota"), cst("ones")
    ones_col = ones[:, 0:1]

    def carver(of):
        at = [0]

        def carve(*dims, dt=F32):
            n = 1
            for d in dims:
                n *= d
            v = of[:, at[0]:at[0] + n]
            at[0] += n
            if dt is not F32:
                v = v.bitcast(dt)
            if len(dims) == 1:
                return v
            names = "abcd"[:len(dims)]
            return v.rearrange("p (%s) -> p %s" % (" ".join(names), " ".join(names)), **dict(zip(names, dims)))
        return carve

    top = area("top")
    carve = carver(top)
    tmp = carve(528)
    top_s = carve(2 * PH, TOPK)
    top_iu = carve(2 * PH, TOPK, dt=U32)
    best_u = carve(PH, TOPK, dt=U32)
    rank_f = carve(PH, TOPK)
    best_s = carve(3, PH, TOPK)
    sel_i = carve(3, PH * TOPK)
    sel_j = carve(3, PH * TOPK)
    top_if = top_iu.bitcast(F32)
    rank_u = rank_f.bitcast(U32)
    gsum = rank_f.rearrange("p h k -> p (h k)")[:, 0:3 * PH].rearrange("p (a h) -> p a h", a=3)
    turned = top[:, 0:3 * T].rearrange("p (k t) -> p k t", k=3)

    pa = ctx.enter_context(nc.psum_tensor("pa", [P, 4, 512], F32))
    pb = ctx.enter_context(nc.psum_tensor("pb", [P, 4, 512], F32))

    carve = carver(big)
    so = carve(IC, T)
    xp = carve(IC, XPW)
    cs = carve(3, HC, DH)
    c_out = carve(HC, DH)
    conv_out = carve(IC, 3 + 3 * NSM)
    n_in = carve(HA, HC, NSM)
    n_new = carve(HA, HC, NSM)
    n_prompt = carve(HA, HC)
    m_in = carve(NSM)
    m_out = carve(1 + NSM)
    conv_in = carve(IC, NSM, 3)
    w_gate = carve(DC, 8)
    relb = carve(HB)
    onehot = carve(WINDOW)
    cols_a = carve(NCOLS_A)
    b_rows = carve(2)
    gcol = carve(16)
    sg = carve(HA, 2 * NSM)
    em_s = carve(HA)
    den_s = carve(2)
    kws = carve(HC, NSM)
    qm = carve(HC, NSM, 32)
    qn = carve(HC, 4, 32)
    conv_acc = carve(2, XPW - 3)
    vn = carve(2, 2, DH)
    vs = carve(2, DH)
    wk = carve(2, DH)
    den = carve(TP)
    qt = carve(2, HC, T)
    kt = carve(2, HC, T)
    xc = big[:, n_big - IC * T:].rearrange("p (c t) -> p c t", t=T)
    carve = carver(scb)
    rows = carve(8, 272)
    sel4 = carve(HA, P)
    sel8 = carve(NSM, P)
    rt = carve(BIASW)
    carve = carver(top)
    hn = carve(HC, TP)
    hs = carve(DH)
    em = carve(TP)
    p0 = carve(TP)
    p1 = carve(P)
    em_row = carve(4, 32)

    def col_a(name, i=0, n=1):
        return cols_a[:, COLS_A[name][0] + i:COLS_A[name][0] + i + n]

    causal, fold = col_a("causal", 0, P), col_a("fold", 0, NSM)

    carve = carver(big)
    qb = carve(DC, T)
    ktb = carve(2, T)
    vnb = carve(2, KVH * HD)
    vsb = carve(KVH * HD)
    kw = carve(2, NSM, WINDOW)
    vw = carve(NSM, KVH * HD)
    bias = carve(HB, 2 * WINDOW)
    bias_s = carve(WINDOW)
    ss = carve(2, 4, 2 * WINDOW)
    pt = carve(2, 4, 2, WINDOW)
    ot = carve(DC, T)
    qbd = carve(NSM, 2, P)
    sink = carve(HB)
    sink_s = carve(1)
    mx = carve(2, 4)
    sx = carve(2, 4)
    dx = carve(2, 4)
    ss_s = carve(WINDOW)
    pt_s = carve(P)
    small_s = carve(4)

    sub, sq, x = (big[:, n_big - k * n_x:n_big - (k - 1) * n_x].rearrange("p (c t) -> p c t", t=T)
                  for k in (3, 2, 1))
    rstd = tmp[:, 0:T]

    w3 = big.rearrange("p (i t) -> p i t", t=T)
    skeys = big[:, (NK - 5 * PH) * T:(NK - 5 * PH) * T + 2 * PH * NK].rearrange("p (h n) -> p h n", n=NK)
    pq = w3[:, NK - 4 * PH:NK - 2 * PH, :]
    scores = scb.rearrange("p (a h n) -> p a h n", a=2, n=NK)
    score_of = [scores[:, 0], scores[:, 1], pb[:, :, :].rearrange("p b (h n) -> p (b h) n", n=NK)]
    hot = scb.rearrange("p (s k t n) -> p s k t n", s=2, k=2, t=8)

    landed = [sem(f"unit_landed_{k}") for k in range(RING)]
    units_used = sem("units_used")
    halves_used = sem("halves_used")
    high_done = sem("high_done")
    low_done = {k: sem(f"low_done_{k}") for k in ("pool", "dve")}
    evacuated = sem("bank_evacuated")

    def gate_bank(s):
        return pb[:, 2 * s:2 * s + 2, :]

    out_groups = 2 * IC + HA * 2 * HC + DC
    peer_total = 2 * PH + NK
    peer_groups = [out_groups + peer_total, 0]
    kv_groups = peer_groups[0] + 2
    bq_groups = kv_groups + DC
    bo_groups = bq_groups + DC
    peer_groups[1] = bo_groups + peer_total

    block = ctx.enter_context(nc.Block())

    @block.sync
    def _(sp):
        sp.dma_start(x, io["x"]).then_inc(sem("x_in"), 16)
        for k in range(RING):
            sp.dma_start(ring[:, k, :], io["units"][k]).then_inc(landed[k], 16)
        for dst, name in ((w_gate, "w_gate"), (b_rows[0:HA, :], "b_gate"), (m_in[0:HA, :], "m_in"),
                          (sel4[0:HA, :, :], "sel4"), (sel8[0:NSM, :, :], "sel8")):
            sp.dma_start(dst, io[name]).then_inc(sem("gate_in"), 16)
        sp.dma_start(const, io["const"]).then_inc(sem("const_in"), 16)
        sp.dma_start(cols, io["cols"]).then_inc(sem("cols_in"), 16)
        sp.dma_start(cols_a, io["cols_a"]).then_inc(sem("cols_in"), 16)
        sp.dma_start(conv_in, io["conv_in"]).then_inc(sem("conv_in"), 16)
        sp.dma_start(n_in, io["n_in"]).then_inc(sem("state_n_in"), 16)
        for kind, a, b in PHASES:
            done = _before(a, kind)
            b = min(b, N_UNITS - RING)
            with sp.Fori(0, (b - a) // RING) as it:
                for k in range(RING):
                    if kind == "pe":
                        sp.wait_ge(units_used, it * RING + (done + k + 1))
                    else:
                        sp.wait_ge(low_done[kind], it * (2 * RING) + 2 * (done + k + 1))
                    sp.dma_start(ring[:, k, :], io["units"][it * RING + (a + RING + k)]).then_inc(landed[k], 16)

    @block.tensor
    def _(pe):
        unit = [0]
        group = [0]

        def mm(out, lhs, rhs, start=True, stop=True):
            return pe.matmul(out, lhs, rhs, start=start, stop=stop)

        def next_unit():
            n = unit[0]
            pe.wait_ge(landed[n % RING], 16 * (n // RING + 1))
            unit[0] += 1
            return ring[:, n % RING, :]

        def next_bank():
            g = group[0]
            if g >= 4:
                pe.wait_ge(evacuated, g - 3)
            group[0] += 1
            return pa[:, g % 4, :]

        def project(src, n_tiles):
            for _ in range(n_tiles):
                w = next_unit()
                out = next_bank()
                for k in range(DC):
                    last = mm(out[:, 0:T], w[:, k * P:(k + 1) * P], src[:, k, :], k == 0, k == DC - 1)
                last.then_inc(units_used, 1)

        def three(out, w_set, w_at, high, low, first, last):
            w = slice(w_at, w_at + P)
            mm(out, split[:, w_set, 0, w], high, first, False)
            mm(out, split[:, w_set, 0, w], low, False, False)
            return mm(out, split[:, w_set, 1, w], high, False, last)

        def x_tile(out, kind, low_count, k):
            for half in range(2):
                pe.wait_ge(low_done[kind], low_count - 1 + half)
                for c in range(4):
                    kk = 4 * half + c
                    last = three(out, 2 * (k % 2) + half, c * P, xh[:, kk, :], xl[:, kk, :], kk == 0, kk == DC - 1)
                last.then_inc(halves_used, 1)

        def project_x(n_tiles):
            for k in range(n_tiles):
                out = next_bank()
                x_tile(out[:, 0:T], "pool", 2 * _before(unit[0] + 1, "pool"), n_split(unit[0]))
                unit[0] += 1

        def norm(li):
            pe.wait_ge(sem("ln_sum"), li + 1)
            for k in range(DC):
                last = mm(pb[:, 0, 0:T], ones, x[:, k, :], k == 0, k == DC - 1)
            last.then_inc(sem("ln_mean"), 1)
            pe.wait_ge(sem("ln_square"), li + 1)
            for k in range(DC):
                last = mm(pb[:, 1, 0:T], ones, sq[:, k, :], k == 0, k == DC - 1)
            last.then_inc(sem("ln_var"), 1)

        def peer(L):
            pe.wait_ge(sem("x_ready"), 2 * L + 2)
            project_x(2 * PH)
            pe.wait_ge(sem("skeys_in"), 16 * (L + 1))
            pe.wait_ge(evacuated, group[0])
            for a, (t0, n) in enumerate(TILES):
                if a:
                    pe.wait_ge(sem("scores_copied"), 2 * L + a)
                for h in range(2 * PH):
                    last = mm(pb[0:n, h // 4, (h % 4) * NK:(h % 4 + 1) * NK], pq[:, h, t0:t0 + n], skeys[:, h, :])
                last.then_inc(sem("scores_done"), 1)
            base, g0 = unit[0], group[0]
            low0 = 2 * _before(base, "pool")
            assert base % RING == 0 and base == U_U[L]
            with pe.Fori(0, NK // RING) as it:
                for k in range(RING):
                    pe.wait_ge(evacuated, it * RING + (g0 + k - 3))
                    x_tile(pa[:, (g0 + k) % 4, 0:T], "pool", it * (2 * RING) + (low0 + 2 * k + 2), n_split(base) + k)
            unit[0] += NK
            group[0] += NK
            pe.wait_ge(sem("gates_done"), L + 1)
            for a, (t0, n) in enumerate(TILES):
                for b, src in enumerate((sel_i, sel_j)):
                    pe.transpose(pb[:, b, t0:t0 + n], src[0:n, a, :], ident[0:n, 0:n])
                last = pe.transpose(pb[:, 2, t0:t0 + n], best_s[0:n, a, :, :].rearrange("p h k -> p (h k)"),
                                    ident[0:n, 0:n])
            last.then_inc(sem("choice_turned"), 1)

            def gate_set(n, s):
                pe.wait_ge(sem("hot_i"), n + 1)
                pe.wait_ge(sem("hot_j"), n + 1)
                for t in range(8):
                    out = gate_bank(s)[:, t // 4, (t % 4) * NK:(t % 4 + 1) * NK]
                    last = mm(out, hot[:, s, 1, t, :], hot[:, s, 0, t, :])
                last.then_inc(sem("gates_spread"), 1)

            n0 = SETS * L
            gate_set(n0, 0)
            gate_set(n0 + 1, 1)
            with pe.Fori(1, SETS // 2) as it:
                for s in range(2):
                    pe.wait_ge(sem("gates_applied"), it * 2 + (n0 + s - 1))
                    gate_set(it * 2 + (n0 + s), s)
            pe.wait_ge(sem("gates_applied"), n0 + SETS - 2)
            gate_set(n0 + SETS - 1, 0)
            pe.wait_ge(sem("gates_applied"), n0 + SETS)
            pe.wait_ge(evacuated, group[0])
            base = unit[0]
            low0 = 2 * _before(base, "dve")

            def y_unit(low_count, w_count, k, first=False, last=False):
                pe.wait_ge(sem("w_low"), w_count)
                for half in range(2):
                    pe.wait_ge(low_done["dve"], low_count - 1 + half)
                    for c in range(4):
                        out = (pa, pb)[half][:, c, 0:T]
                        ins = three(out, 2 * (k % 2) + half, c * P, wsplit[:, k, 0, :], wsplit[:, k, 1, :], first, last)
                    ins.then_inc(halves_used, 1)

            for k in range(RING):
                y_unit(low0 + 2 * k + 2, NK * L + k + 1, k, first=(k == 0))
            with pe.Fori(1, NK // RING - 1) as it:
                for k in range(RING):
                    y_unit(it * (2 * RING) + (low0 + 2 * k + 2), it * RING + (NK * L + k + 1), k)
            for k in range(RING):
                n = NK - RING + k
                y_unit(low0 + 2 * n + 2, NK * L + n + 1, k, last=(k == RING - 1))
            unit[0] += NK

        pe.wait_ge(sem("const_in"), 16)
        pe.wait_ge(sem("x_in"), 16)
        pe.wait_ge(sem("gate_in"), 80)
        for g in range(2):
            for k in range(DC):
                last = mm(pb[0:HA, g, 0:T], w_gate[:, k, g * HA:(g + 1) * HA], x[:, k, :], k == 0, k == DC - 1)
        last.then_inc(sem("gate_pre"), 1)
        pe.wait_ge(sem("bias_in"), 32)
        mm(pb[0:HB, 2, 0:WINDOW], relb[0:NB, :], onehot[0:NB, :]).then_inc(sem("bias_rows"), 1)
        pe.wait_ge(sem("x_ready"), 1)
        project_x(2 * IC)

        pe.wait_ge(sem("gate_exps"), 1)
        for s in range(2):
            pe.transpose(pb[:, 2, s * HA:(s + 1) * HA], rows[0:HA, 4, s * P:(s + 1) * P], ident[0:HA, 0:HA])
            pe.transpose(pb[:, 2, 8 + s * HA:8 + (s + 1) * HA], rows[0:HA, 7, s * P:(s + 1) * P], ident[0:HA, 0:HA])
        pe.transpose(pb[:, 2, 16:20], em_row[0:HA].rearrange("p a b -> p (a b)"), ident[0:HA, 0:HA])
        for h in range(HA):
            last = mm(pb[:, 3, h * 16:(h + 1) * 16], sel4[0:HA, h, :], rows[0:HA, 7, TP:TP + 16])
        last.then_inc(sem("gate_cols"), 1)

        def head_project(h):
            if h >= 2:
                pe.wait_ge(sem("head_done"), h - 1)
            if h == 0:
                pe.wait_ge(sem("conv_done"), IC)
            for part in range(2):
                for _ in range(2):
                    w = next_unit()
                    for m in range(2):
                        out = next_bank()
                        for k in range(HC):
                            last = mm(out[:, 0:T], w[:, k * 256 + m * P:k * 256 + (m + 1) * P], xc[:, h * HC + k, :],
                                      k == 0, k == HC - 1)
                    last.then_inc(units_used, 1)
            if h == 0:
                pe.wait_ge(sem("gate_cols_kept"), 1)
            for u in range(2):
                w = next_unit()
                for k in range(2):
                    kk = 2 * u + k
                    src = xp[:, h * HC + kk, :]
                    rhs = w[:, k * DH:(k + 1) * DH]
                    mm(pb[:, 0, :], src[:, 3:3 + P], rhs, kk == 0, kk == HC - 1)
                    mm(pb[:, 1, :], src[:, 3 + P:3 + TP], rhs, kk == 0, kk == HC - 1)
                    last = mm(pb[0:NSM, 2, :], src[:, TP + 6:XPW:4], rhs, kk == 0, kk == HC - 1)
                last.then_inc(units_used, 1)

        def head_prompt(h):
            q, k = qt[:, h % 2], kt[:, h % 2]
            pe.wait_ge(sem("v_kept"), min(h + 2, HA))
            mm(pb[:, 3, 0:TP], sel4[0:HA, h, :], rows[0:HA, 5, 0:TP])
            mm(pb[:, 3, TP:2 * TP], sel4[0:HA, h, :], rows[0:HA, 6, 0:TP]).then_inc(sem("rows_spread"), 1)
            for c in range(HC):
                mm(pb[:, 2, 0:TP], k[:, c, 0:P], q[:, c, 0:TP], c == 0, c == HC - 1)
            for c in range(HC):
                last = mm(pb[:, 2, TP:TP + P], k[:, c, P:TP], q[:, c, P:TP], c == 0, c == HC - 1)
            last.then_inc(sem("scores_t"), 1)
            for s in range(2):
                for c in range(HC):
                    last = pe.transpose(pb[:, s, c * P:(c + 1) * P], k[:, c, s * P:(s + 1) * P], ident)
            last.then_inc(sem("k_turned"), 1)
            pe.wait_ge(sem("weights_t"), h + 1)
            mm(pb[:, 3, 0:P], ones[:, 0:P], p0[:, 0:P])
            mm(pb[:, 3, P:TP], ones[:, 0:P], p0[:, P:TP], True, False)
            mm(pb[:, 3, P:TP], ones[:, 0:P], p1, False, True).then_inc(sem("den_done"), 1)
            for c in range(HC):
                o = pb[:, c // 2, (c % 2) * TP:(c % 2 + 1) * TP]
                v0, v1 = vn[:, h % 2, 0, c * P:(c + 1) * P], vn[:, h % 2, 1, c * P:(c + 1) * P]
                mm(o[:, 0:P], v0, p0[:, 0:P])
                mm(o[:, P:TP], v0, p0[:, P:TP], True, False)
                last = mm(o[:, P:TP], v1, p1, False, True)
            last.then_inc(sem("num_done"), 1)
            pe.wait_ge(sem("den_kept"), h + 1)
            for c in range(HC):
                b = 2 + c % 2
                if c >= 2:
                    pe.wait_ge(sem("c_kept"), HC * h + c - 1)
                mm(pb[:, b, :], wk[:, 0, c * P:(c + 1) * P], vn[:, h % 2, 0, :], True, False)
                mm(pb[:, b, :], wk[:, 1, c * P:(c + 1) * P], vn[:, h % 2, 1, :], False, True).then_inc(sem("c_done"), 1)
            pe.wait_ge(sem("num_used"), h + 1)
            for c in range(HC):
                mm(pb[:, 0, c:c + 1], wk[:, 0, c * P:(c + 1) * P], ones_col, True, False)
                last = mm(pb[:, 0, c:c + 1], wk[:, 1, c * P:(c + 1) * P], ones_col, False, True)
            last.then_inc(sem("n_done"), 1)

        def head_sample(h):
            pe.wait_ge(sem("sample_ready"), h + 1)
            pe.wait_ge(sem("n_kept"), h + 1)
            for c in range(HC):
                last = mm(pb[:, 0, 4:5], qn[:, c].rearrange("p a b -> p (a b)"), ones_col, c == 0, c == HC - 1)
            last.then_inc(sem("den_s_done"), 1)

            def spread_v(b):
                if b == 0:
                    pe.wait_ge(sem("c_kept"), HC * (h + 1))
                if b >= 2:
                    pe.wait_ge(sem("state_new"), NSM * h + b - 1)
                mm(pb[:, 2 + b % 2, :], sel8[0:NSM, b, :], vs[0:NSM, h % 2, :]).then_inc(sem("v_spread"), 1)

            spread_v(0)
            for b in range(NSM):
                if b + 1 < NSM:
                    spread_v(b + 1)
                n = NSM * h + b
                pe.wait_ge(sem("state_new"), n + 1)
                for c in range(HC):
                    last = mm(pb[32 * c:32 * c + 32, 1, :], qm[:, c, b, :], cs[:, n % 3, c, :], b == 0,
                              b == NSM - 1)
                last.then_inc(sem("state_read"), 1)
            pe.wait_ge(sem("h_sample"), h + 1)
            for c in range(HC):
                last = mm(pb[:, 0, 8 + c * NSM:8 + (c + 1) * NSM], hs[:, c * P:(c + 1) * P], fold)
            last.then_inc(sem("head_done"), 1)

        head_project(0)
        for h in range(HA):
            if h:
                pe.wait_ge(sem("head_gated"), h)
            if h + 1 < HA:
                head_project(h + 1)
            head_prompt(h)
            head_sample(h)
        pe.wait_ge(sem("head_gated"), HA)
        for m in range(DC):
            out = next_bank()
            for half in range(2):
                w = next_unit()
                for k in range(DC):
                    last = mm(out[:, 0:T], w[:, k * P:(k + 1) * P], so[:, half * DC + k, :],
                              half == 0 and k == 0, half == 1 and k == DC - 1)
                last.then_inc(units_used, 1)
        norm(0)
        peer(0)
        norm(1)
        pe.wait_ge(sem("x_ready"), 3)
        project(x, 2)
        for u in range(2):
            w = next_unit()
            for k in range(4):
                kk = 4 * u + k
                rhs = w[:, k * 256:(k + 1) * 256]
                mm(pb[:, 0, 0:256], x[:, kk, 0:P], rhs, kk == 0, kk == DC - 1)
                mm(pb[:, 1, 0:256], x[:, kk, P:TP], rhs, kk == 0, kk == DC - 1)
                last = mm(pb[0:NSM, 2, 0:256], x[:, kk, TP:T], rhs, kk == 0, kk == DC - 1)
            last.then_inc(units_used, 1)
        project_x(DC)
        pe.wait_ge(evacuated, group[0])
        pe.wait_ge(sem("vb_kept"), 1)

        groups = [(blk, g4) for blk in range(2) for g4 in range(4)]

        def att_scores(i):
            blk, g4 = groups[i]
            if i >= 2:
                pe.wait_ge(sem("att_scored"), i - 1)
            for e in range(4):
                half, c = e // 2, 2 * g4 + e % 2
                r = slice(half * HD, (half + 1) * HD)
                nk = P * (blk + 1)
                last = mm(pa[:, 2 * (i % 2) + e // 2, (e % 2) * 256:(e % 2) * 256 + nk],
                          qb[r, c, blk * P:(blk + 1) * P], ktb[r, c // 4, 0:nk])
            last.then_inc(sem("att_scores"), 1)

        def att_values(i):
            blk, g4 = groups[i]
            pe.wait_ge(sem("att_probs"), i + 1)
            if i >= 1:
                pe.wait_ge(sem("att_turned_kept"), i)
            for e in range(4):
                for s in range(blk + 1):
                    last = pe.transpose(pb[:, e // 2, (e % 2) * 256 + s * P:(e % 2) * 256 + (s + 1) * P],
                                        ss[:, i % 2, e, s * P:(s + 1) * P], ident)
            last.then_inc(sem("att_turned"), 1)
            pe.wait_ge(sem("att_turned_kept"), i + 1)
            if i >= 1:
                pe.wait_ge(sem("att_out_kept"), i)
            for e in range(4):
                half, c = e // 2, 2 * g4 + e % 2
                g = 2 * (c // 4) + half
                for s in range(blk + 1):
                    last = mm(pb[half * HD:(half + 1) * HD, 2, (e % 2) * P:(e % 2 + 1) * P],
                              vnb[:, s, g * HD:(g + 1) * HD], pt[:, i % 2, e, s, :], s == 0, s == blk)
            last.then_inc(sem("att_out"), 1)

        att_scores(0)
        for i in range(8):
            if i + 1 < 8:
                att_scores(i + 1)
            att_values(i)
        pe.wait_ge(sem("q_spread"), 1)
        pe.wait_ge(sem("window_ready"), 1)
        for b in range(NSM):
            for G in range(2):
                last = mm(pb[:, 3, 0:WINDOW], qbd[:, b, G, :], kw[:, G, b, :], b == 0 and G == 0,
                          b == NSM - 1 and G == 1)
        last.then_inc(sem("att_s_scores"), 1)
        pe.wait_ge(sem("att_s_probs"), 1)
        pe.transpose(pb[:, 3, 128:256], ss_s, ident).then_inc(sem("att_s_turned"), 1)
        pe.wait_ge(sem("att_s_kept"), 1)
        pe.wait_ge(sem("vw_in"), 32)
        for b in range(NSM):
            for G in range(2):
                o = 256 + (b * 2 + G) * 8
                last = mm(pb[:, 3, o:o + 8], vw[:, b, G * P:(G + 1) * P], pt_s[:, b * 16 + G * 8:b * 16 + G * 8 + 8])
        last.then_inc(sem("att_s_out"), 1)
        pe.wait_ge(sem("ot_ready"), 1)
        project(ot, DC)
        norm(2)
        peer(1)
        norm(3)

    @block.scalar
    def _(act):
        group = [0]
        chain = [0]

        def link(ins):
            chain[0] += 1
            ins.then_inc(sem("act_chain"), 1)
            act.wait_ge(sem("act_chain"), chain[0])

        def bank(units):
            kind = [k for k, a, b in PHASES if a < units <= b][0]
            if kind == "pe":
                act.wait_ge(units_used, _before(units, "pe"))
            else:
                act.wait_ge(halves_used, 2 * n_split(units))
            group[0] += 1
            return pa[:, (group[0] - 1) % 4, 0:T]

        def high(slot, n, count, landed_count, used_count=None):
            act.wait_ge(landed[slot], landed_count)
            for half in range(2):
                if used_count is not None:
                    act.wait_ge(halves_used, used_count + half)
                nc.scalar.copy(split[:, 2 * (n % 2) + half, 0, :], ring[:, slot, half * 512:(half + 1) * 512]).then_inc(
                    high_done, 1)

        def high_at(u):
            n = n_split(u)
            high(u % RING, n, 0, 16 * (u // RING + 1), 2 * n - 3 if n >= 2 else None)

        def high_loop(it, u):
            n = n_split(u)
            high(u % RING, n, 0, it * 16 + 16 * (u // RING + 1), it * (2 * RING) + (2 * n - 3))

        def norm(li):
            act.wait_ge(sem("ln_centred"), li + 1)
            nc.scalar.activation(sq, x, ACT.Square).then_inc(sem("ln_square"), 1)
            act.wait_ge(sem("ln_var"), li + 1)
            nc.scalar.activation(rstd, pb[:, 1, 0:T], ACT.Sqrt, bias=col("eps", 0), scale=1.0 / D).then_inc(
                sem("ln_std"), 1)

        def x_high(n):
            act.wait_ge(sem("x_full"), n)
            nc.scalar.copy(xh[:, :, :], x).then_inc(sem("x_high"), 1)

        def peer(L):
            act.wait_ge(sem("skeys_in"), 16 * (L + 1))
            for h in range(2 * PH):
                src = bank(U_PQ[L] + h + 1)
                high_at(U_PQ[L] + h + 2)
                nc.scalar.copy(pq[:, h, :], src).then_inc(evacuated, 1)
            for a, (t0, n) in enumerate(TILES[0:2]):
                act.wait_ge(sem("scores_done"), 3 * L + a + 1)
                nc.scalar.copy(score_of[a].rearrange("p h n -> p (h n)"),
                               pb[:, :, :].rearrange("p b n -> p (b n)")).then_inc(sem("scores_copied"), 1)
            g0 = group[0]
            with act.Fori(0, NK // RING) as it:
                for k in range(RING):
                    high_loop(it, U_U[L] + k + 2)
                    act.wait_ge(halves_used, it * (2 * RING) + 2 * n_split(U_U[L] + k + 1))
                    nc.scalar.activation(big[:, bass.ds(it * (4 * T) + k * T, T)], pa[:, (g0 + k) % 4, 0:T],
                                         ACT.Gelu).then_inc(evacuated, 1)
            group[0] += NK
            act.wait_ge(sem("best_shifted"), L + 1)
            for a, (t0, n) in enumerate(TILES):
                v = best_s[0:n, a].rearrange("p h k -> p (h k)")
                last = nc.scalar.activation(v, v, ACT.Exp)
            last.then_inc(sem("best_exp"), 1)

            def one_hot(n, s):
                v = hot[:, s, 1, :, :]
                act.wait_ge(sem("lane_minus_j"), n)
                nc.scalar.activation(v, v, ACT.Abs).then_inc(sem("lane_abs"), 1)
                act.wait_ge(sem("lane_abs"), n)
                nc.scalar.activation(v, v, ACT.Relu, bias=1.0, scale=-1.0).then_inc(sem("hot_j"), 1)

            with act.Fori(0, SETS // 2) as it:
                for s in range(2):
                    one_hot(it * 2 + (SETS * L + s + 1), s)
            one_hot(SETS * (L + 1), 0)
            act.wait_ge(sem("gates_applied"), SETS * (L + 1))
            n0 = n_split(U_V[L])

            def w_high(it, i):
                if it is not None:
                    act.wait_ge(halves_used, it * (2 * RING) + 2 * (n0 + i - 3))
                nc.scalar.copy(wsplit[:, i % 4, 0, :], big[:, bass.ds(it * (4 * T) + i * T, T)] if it is not None
                               else w3[:, i, :]).then_inc(sem("w_high"), 1)

            w_high(None, 0)
            w_high(None, 1)
            for k in range(RING):
                high_at(U_V[L] + k + 2)
                w_high(None if k < 2 else 0, k + 2)
            with act.Fori(1, NK // RING - 1) as it:
                for k in range(RING):
                    high_loop(it, U_V[L] + k + 2)
                    w_high(it, k + 2)
            for k in range(2):
                high_at(U_V[L] + NK - RING + k + 2)
                w_high(NK // RING - 1, k + 2)

        act.wait_ge(sem("x_in"), 16)
        nc.scalar.copy(xh[:, :, :], x).then_inc(sem("x_high"), 1)
        high_at(U_IN)
        high_at(U_IN + 1)
        act.wait_ge(sem("gate_in"), 80)
        act.wait_ge(sem("gate_pre"), 1)
        nc.scalar.activation(rows[0:HA, 0, 0:T], pb[0:HA, 0, 0:T], ACT.Identity, bias=b_rows[0:HA, 0:1]).then_inc(
            sem("gate_i"), 1)
        link(nc.scalar.activation(rows[0:HA, 1, 0:T], pb[0:HA, 1, 0:T], ACT.Identity, bias=b_rows[0:HA, 1:2]))
        link(nc.scalar.activation(rows[0:HA, 2, 0:T], rows[0:HA, 1, 0:T], ACT.Abs))
        link(nc.scalar.activation(rows[0:HA, 2, 0:T], rows[0:HA, 2, 0:T], ACT.Exp, scale=-1.0))
        nc.scalar.activation(rows[0:HA, 2, 0:T], rows[0:HA, 2, 0:T], ACT.Ln, bias=1.0).then_inc(sem("gate_soft"), 1)
        act.wait_ge(sem("gate_scanned"), 1)
        nc.scalar.activation(rows[0:HA, 6, 0:T], rows[0:HA, 6, 0:T], ACT.Exp, scale=-1.0)
        nc.scalar.activation(em_row[0:HA], em_row[0:HA], ACT.Exp, scale=-1.0)
        nc.scalar.activation(rows[0:HA, 7, :], rows[0:HA, 7, :], ACT.Exp).then_inc(sem("gate_exps"), 1)
        act.wait_ge(sem("cols_in"), 32)
        for c in range(IC):
            src = bank(U_IN + c + 1)
            high_at(U_IN + c + 2)
            b = col_a("b_in", c)
            nc.scalar.activation(xp[:, c, 3:3 + TP], src[:, 0:TP], ACT.Identity, bias=b)
            nc.scalar.activation(xp[:, c, TP + 6:XPW:4], src[:, TP:T], ACT.Identity, bias=b).then_inc(evacuated, 1)
        for c in range(IC):
            src = bank(U_IN + IC + c + 1)
            if c < IC - 2:
                high_at(U_IN + IC + c + 2)
            nc.scalar.activation(so[:, c, :], src, ACT.Sigmoid, bias=col_a("b_in", IC + c)).then_inc(evacuated, 1)
        for c in range(IC):
            act.wait_ge(sem("conv_summed"), c + 1)
            acc = conv_acc[:, c % 2, :]
            nc.scalar.activation(xc[:, c, 0:TP], acc[:, 0:TP], ACT.Silu, bias=col_a("conv_b", c))
            nc.scalar.activation(xc[:, c, TP:T], acc[:, TP + 3:XPW - 3:4], ACT.Silu,
                                 bias=col_a("conv_b", c)).then_inc(sem("conv_done"), 1)

        def head_keep(h):
            n = U_QKV + 6 * h
            if h >= 2:
                act.wait_ge(sem("head_done"), h - 1)
                act.wait_ge(sem("head_gated"), h - 1)
            for i, (dst, scale) in enumerate(((qt, 1.0), (kt, DH ** -0.5))):
                for m in range(HC):
                    src = bank(n + 2 * i + m // 2 + 1)
                    nc.scalar.mul(dst[:, h % 2, m, :], src, scale).then_inc(evacuated, 1)
            act.wait_ge(units_used, _before(n + 6, "pe"))
            for s in range(2):
                nc.scalar.copy(vn[:, h % 2, s, :], pb[:, s, :])
            nc.scalar.copy(vs[0:NSM, h % 2, :], pb[0:NSM, 2, :]).then_inc(sem("v_kept"), 1)

        head_keep(0)
        for h in range(HA):
            if h + 1 < HA:
                head_keep(h + 1)
            act.wait_ge(sem("decay_arg"), h + 1)
            nc.scalar.activation(p0, p0, ACT.Exp)
            nc.scalar.activation(p1, p1, ACT.Exp).then_inc(sem("decay_exp"), 1)
            act.wait_ge(sem("den_done"), h + 1)
            if h:
                act.wait_ge(sem("num_used"), h)
            nc.scalar.activation(den, pb[:, 3, 0:TP], ACT.Abs).then_inc(sem("den_kept"), 1)
            if h:
                act.wait_ge(sem("c_stored"), 16 * h)
            for c in range(HC):
                act.wait_ge(sem("c_done"), HC * h + c + 1)
                nc.scalar.copy(c_out[:, c, :], pb[:, 2 + c % 2, :]).then_inc(sem("c_kept"), 1)
            act.wait_ge(sem("n_done"), h + 1)
            nc.scalar.copy(n_prompt[:, h, :], pb[:, 0, 0:HC]).then_inc(sem("n_kept"), 1)
            for b in range(NSM):
                n = NSM * h + b
                act.wait_ge(sem(f"state_in_{n % 3}"), 16 * (n // 3 + 1))
                v = cs[:, n % 3].rearrange("p c e -> p (c e)")
                nc.scalar.mul(v, v, sg[:, h, NSM + b:NSM + b + 1]).then_inc(sem("state_decayed"), 1)
            act.wait_ge(sem("den_s_done"), h + 1)
            nc.scalar.activation(den_s[:, 0:1], pb[:, 0, 4:5], ACT.Abs).then_inc(sem("den_s_kept"), 1)
        for m in range(DC):
            src = bank(U_OUT + 2 * (m + 1))
            nc.scalar.copy(sub[:, m, :], src).then_inc(evacuated, 1)
        norm(0)
        high_at(U_PQ[0])
        high_at(U_PQ[0] + 1)
        x_high(1)
        peer(0)
        norm(1)
        x_high(2)
        for c in range(2):
            src = bank(U_KV + c + 1)
            nc.scalar.copy(ktb[:, c, :], src).then_inc(evacuated, 1)
        act.wait_ge(units_used, _before(U_KV + 4, "pe"))
        for s in range(2):
            nc.scalar.copy(vnb[:, s, :], pb[:, s, 0:256])
        nc.scalar.copy(vsb[0:NSM, :], pb[0:NSM, 2, 0:256]).then_inc(sem("vb_kept"), 1)
        high_at(U_BQ)
        high_at(U_BQ + 1)
        for c in range(DC):
            src = bank(U_BQ + c + 1)
            if c < DC - 2:
                high_at(U_BQ + c + 2)
            nc.scalar.copy(qb[:, c, :], src).then_inc(evacuated, 1)
        for i in range(8):
            nk = P * (1 + i // 4)
            act.wait_ge(sem("att_shifted"), i + 1)
            nc.scalar.activation(ss[:, i % 2, :, 0:nk], ss[:, i % 2, :, 0:nk], ACT.Exp)
            nc.scalar.activation(dx[:, i % 2, :], dx[:, i % 2, :], ACT.Exp).then_inc(sem("att_exp"), 1)
            act.wait_ge(sem("att_turned"), i + 1)
            nb = i // 4 + 1
            src = pb[:, 0:2, :].rearrange("p b (e s q) -> p (b e) s q", e=2, s=2)
            nc.scalar.copy(pt[:, i % 2, :, 0:nb, :], src[:, :, 0:nb, :]).then_inc(sem("att_turned_kept"), 1)
        act.wait_ge(sem("att_s_shifted"), 1)
        nc.scalar.activation(ss_s, ss_s, ACT.Exp)
        nc.scalar.activation(small_s[:, 1:2], small_s[:, 1:2], ACT.Exp).then_inc(sem("att_s_exp"), 1)
        for m in range(DC):
            src = bank(U_BO + m + 1)
            nc.scalar.copy(sub[:, m, :], src).then_inc(evacuated, 1)
        norm(2)
        high_at(U_PQ[1])
        high_at(U_PQ[1] + 1)
        x_high(3)
        peer(1)
        norm(3)
        act.wait_ge(sem("x_full"), 4)
        act.dma_start(io["y"], x).then_inc(sem("y_out"), 16)
        act.wait_ge(sem("y_out"), 16)

    @block.vector
    def _(dve):
        V = nc.vector
        chain = [0]

        def link(ins):
            chain[0] += 1
            ins.then_inc(sem("dve_chain"), 1)
            dve.wait_ge(sem("dve_chain"), chain[0])

        def norm(li, gn, bn, L):
            if li % 2 == 0:
                link(V.scalar_tensor_tensor(x, xh_f, ALPHA, sub, ALU.mult, ALU.add))
            else:
                for b, bank in enumerate((pa, pb)):
                    last = V.scalar_tensor_tensor(x[:, 4 * b:4 * b + 4, :], xh_f[:, 4 * b:4 * b + 4, :], ALPHA,
                                                  bank[:, :, 0:T], ALU.mult, ALU.add)
                link(last)
            V.scalar_tensor_tensor(x, xl_f, ALPHA, x, ALU.mult, ALU.add).then_inc(sem("ln_sum"), 1)
            dve.wait_ge(sem("ln_sum"), li + 1)
            dve.wait_ge(sem("ln_mean"), li + 1)
            V.scalar_tensor_tensor(x, pb[:, 0:1, 0:T].to_broadcast([P, DC, T]), -1.0 / D, x, ALU.mult,
                                   ALU.add).then_inc(sem("ln_centred"), 1)
            dve.wait_ge(sem("ln_centred"), li + 1)
            dve.wait_ge(sem("ln_std"), li + 1)
            link(V.reciprocal(rstd, rstd))
            link(V.tensor_tensor(x, x, rstd.rearrange("p (o t) -> p o t", o=1).to_broadcast([P, DC, T]), ALU.mult))
            for c in range(DC):
                last = V.tensor_scalar(x[:, c, :], x[:, c, :], col(gn, L * DC + c), col(bn, L * DC + c),
                                       ALU.mult, ALU.add)
            last.then_inc(sem("x_full"), 1)
            dve.wait_ge(sem("x_full"), li + 1)
            if li < 3:
                x_low(li + 2)

        def x_low(n):
            dve.wait_ge(sem("x_high"), n)
            V.tensor_tensor(xl[:, :, :], x, xh_f, ALU.subtract).then_inc(sem("x_ready"), 1)
            dve.wait_ge(sem("x_ready"), n)

        def low(slot, n, count):
            for half in range(2):
                o = slice(half * 512, (half + 1) * 512)
                dve.wait_ge(high_done, count + half)
                V.tensor_tensor(split[:, 2 * (n % 2) + half, 1, :], ring[:, slot, o],
                                split_f[:, 2 * (n % 2) + half, 0, :], ALU.subtract).then_inc(low_done["dve"], 1)

        def top16(vals, outs, idx, n):
            for step in range(2):
                o = slice(8 * step, 8 * step + 8)
                for v, s in zip(vals, outs):
                    last = V.max(s[:, o], v)
                link(last)
                for v, s, i in zip(vals, outs, idx):
                    last = V.max_index(i[:, o], s[:, o], v)
                if step == 0:
                    for v, s in zip(vals, outs):
                        last = V.match_replace(v, s[:, o], v, LOWEST)
                link(last)

        def choose(L, a, n):
            if a < 2:
                dve.wait_ge(sem("scores_copied"), 2 * L + a + 1)
            else:
                dve.wait_ge(sem("scores_done"), 3 * L + 3)
            sc = score_of[a][0:n]
            top16([sc[:, h] for h in range(2 * PH)], [top_s[0:n, h] for h in range(2 * PH)],
                  [top_iu[0:n, h] for h in range(2 * PH)], n)
            ts = top_s[0:n].rearrange("p (h two) k -> p h two k", two=2)
            cand = sc.rearrange("p (h two) (b c) -> p h (two b) c", two=2, c=TOPK)
            for h in range(PH):
                last = V.tensor_tensor(cand[:, h], ts[:, h, 0, :].rearrange("p (k o) -> p k o", o=1).to_broadcast(
                    [n, TOPK, TOPK]), ts[:, h, 1:2, :].to_broadcast([n, TOPK, TOPK]), ALU.add)
            link(last)
            link(V.tensor_copy(top_if[0:n], top_iu[0:n]))
            flat = sc.rearrange("p (h two) c -> p h (two c)", two=2)
            bs = best_s[0:n, a]
            top16([flat[:, h] for h in range(PH)], [bs[:, h] for h in range(PH)],
                  [best_u[0:n, h] for h in range(PH)], n)
            i16 = iota[0:n, 0:TOPK].rearrange("p (o k) -> p o k", o=1).to_broadcast([n, TOPK, TOPK])
            tf = top_if[0:n].rearrange("p (h two) k -> p h two k", two=2)
            eq = tmp[0:n, 0:512].rearrange("p (h k r) -> p h k r", h=2, r=TOPK)
            for half, (dst, op, arg) in enumerate(((sel_i, ALU.logical_shift_right, 4), (sel_j, ALU.bitwise_and, 15))):
                link(V.tensor_scalar(rank_u[0:n], best_u[0:n], arg, None, op))
                link(V.tensor_copy(rank_f[0:n], rank_u[0:n]))
                for hq in range(PH // 2):
                    for e in range(2):
                        last = V.tensor_tensor(eq[:, e], rank_f[0:n, 2 * hq + e, :].rearrange(
                            "p (k o) -> p k o", o=1).to_broadcast([n, TOPK, TOPK]), i16, ALU.is_equal)
                    link(last)
                    for e in range(2):
                        last = V.tensor_tensor(eq[:, e], eq[:, e], tf[:, 2 * hq + e, half:half + 1, :].to_broadcast(
                            [n, TOPK, TOPK]), ALU.mult)
                    link(last)
                    link(V.tensor_reduce(dst[0:n, a, 32 * hq:32 * (hq + 1)],
                                         tmp[0:n, 0:512].rearrange("p (k r) -> p k r", r=TOPK), AX.X, ALU.add))
            V.tensor_copy(gsum[0:n, a, :], bs[:, :, 0])
            link(V.engine_nop())
            link(V.tensor_tensor(bs, bs, gsum[0:n, a, :].rearrange("p (h o) -> p h o", o=1).to_broadcast(
                [n, PH, TOPK]), ALU.subtract))

        def peer(L):
            for a in (2, 0, 1):
                choose(L, a, TILES[a][1])
            V.engine_nop().then_inc(sem("best_shifted"), 1)
            nv = n_split(U_V[L])
            for k in range(2):
                low((U_V[L] + k) % RING, nv + k, 2 * (nv + k) + 1)
            dve.wait_ge(sem("best_exp"), L + 1)
            for a, (t0, n) in enumerate(TILES):
                last = V.tensor_reduce(gsum[0:n, a, :], best_s[0:n, a], AX.X, ALU.add)
            link(last)
            for a, (t0, n) in enumerate(TILES):
                last = V.reciprocal(gsum[0:n, a, :], gsum[0:n, a, :])
            link(last)
            for a, (t0, n) in enumerate(TILES):
                last = V.tensor_tensor(best_s[0:n, a], best_s[0:n, a], gsum[0:n, a, :].rearrange(
                    "p (h o) -> p h o", o=1).to_broadcast([n, PH, TOPK]), ALU.mult)
            last.then_inc(sem("gates_done"), 1)
            dve.wait_ge(sem("choice_turned"), L + 1)
            V.tensor_copy(turned[:, :, :], pb[:, 0:3, 0:T]).then_inc(sem("choice_kept"), 1)
            dve.wait_ge(sem("choice_kept"), L + 1)

            def hot_i(it, s):
                for t in range(8):
                    c = it * 16 + (8 * s + t) if it is not None else 8 * s + t
                    i_col, g_col = ((turned[:, r, bass.ds(c, 1)] if it is not None else turned[:, r, c:c + 1])
                                    for r in (0, 2))
                    last = V.tensor_scalar(hot[:, s % 2, 0, t, :], iota, i_col, g_col, ALU.is_equal, ALU.mult)
                last.then_inc(sem("hot_i"), 1)

            def apply(it, s, n):
                dve.wait_ge(sem("gates_spread"), n + 1)
                w = w3[:, :, bass.ds(it * 16 + 8 * s, 8)]
                g = gate_bank(s % 2).rearrange("p b (t i) -> p i (b t)", t=4)
                V.tensor_tensor(w, w, g, ALU.mult).then_inc(sem("gates_applied"), 1)

            n0 = SETS * L
            hot_i(None, 0)
            hot_i(None, 1)
            apply(0, 0, n0)
            hot_i(None, 2)
            apply(0, 1, n0 + 1)
            with dve.Fori(1, SETS // 2) as it:
                for s in range(2):
                    n = it * 2 + (n0 + s)
                    dve.wait_ge(sem("gates_spread"), n)
                    hot_i(it, s + 1)
                    apply(it, s, n)
            apply(SETS // 2, 0, n0 + SETS - 1)
            n_w = NK * L

            def w_low(it, i):
                dve.wait_ge(sem("w_high"), it * RING + (n_w + i + 1))
                V.tensor_tensor(wsplit[:, i % 4, 1, :], big[:, bass.ds(it * (4 * T) + i * T, T)],
                                wsplit_f[:, i % 4, 0, :], ALU.subtract).then_inc(sem("w_low"), 1)

            w_low(0, 0)
            w_low(0, 1)
            with dve.Fori(0, NK // RING - 1) as it:
                for k in range(RING):
                    u = nv + k + 2
                    low((U_V[L] + k + 2) % RING, u, it * (2 * RING) + (2 * u + 1))
                    w_low(it, k + 2)
            for k in range(2):
                u = nv + NK - RING + k + 2
                low((U_V[L] + k + 2) % RING, u, 2 * u + 1)
                w_low(NK // RING - 1, k + 2)
            dve.wait_ge(halves_used, 2 * (nv + NK))

        dve.wait_ge(sem("x_in"), 16)
        x_low(1)
        V.memset(em_row[0:HA], 0.0)
        link(V.memset(rt[0:HB, :], NEG))
        dve.wait_ge(sem("bias_rows"), 1)
        V.tensor_copy(rt[0:HB, WINDOW:2 * WINDOW], pb[0:HB, 2, 0:WINDOW]).then_inc(sem("bias_rows_kept"), 1)
        V.memset(qm, 0.0)
        V.memset(qn, 0.0)
        V.memset(xp[:, :, 0:3], 0.0)
        dve.wait_ge(sem("conv_in"), 16)
        link(V.tensor_copy(xp[:, :, 3 + TP:XPW].rearrange("p c (b w) -> p c b w", w=4)[:, :, :, 0:3], conv_in))
        dve.wait_ge(sem("gate_soft"), 1)
        R = rows[0:HA]
        r = lambda i, a=0, b=T: R[:, i, a:b]
        link(V.scalar_tensor_tensor(r(1), r(1), 0.0, r(2), ALU.min, ALU.subtract))
        link(V.memset(r(5), 1.0))
        link(V.tensor_tensor_scan(r(3, 0, TP), r(5, 0, TP), r(1, 0, TP), 0.0, ALU.mult, ALU.add))
        link(V.tensor_tensor(r(4, 0, TP), r(0, 0, TP), r(3, 0, TP), ALU.subtract))
        link(V.tensor_tensor_scan(r(2, 0, TP), r(5, 0, TP), r(4, 0, TP), 0.0, ALU.mult, ALU.max))
        V.tensor_scalar(r(5, 0, TP), r(2, 0, TP), -1.0, None, ALU.mult)
        V.tensor_tensor(r(6, 0, TP), r(3, 0, TP), r(2, 0, TP), ALU.add)
        V.tensor_scalar(r(7, 0, TP), r(4, 0, TP), r(2, TP - 1, TP), None, ALU.subtract)
        link(V.tensor_tensor(r(3, TP, T), r(1, TP, T), m_in[0:HA, :], ALU.add))
        link(V.tensor_tensor(r(6, TP, T), r(3, TP, T), r(0, TP, T), ALU.max))
        V.tensor_tensor(r(7, TP, T), r(0, TP, T), r(6, TP, T), ALU.subtract)
        V.tensor_copy(em_row[0:HA, :, 0:NSM], R[:, 6:7, TP:T].to_broadcast([HA, 4, NSM]))
        V.tensor_copy(m_out[0:HA, 0:1], r(6, TP - 1, TP))
        V.tensor_copy(m_out[0:HA, 1:1 + NSM], r(6, TP, T)).then_inc(sem("m_kept"), 1)
        V.tensor_tensor(r(7, T, T + NSM), r(3, TP, T), r(6, TP, T), ALU.subtract).then_inc(sem("gate_scanned"), 1)
        dve.wait_ge(sem("gate_cols"), 1)
        V.tensor_copy(gcol, pb[:, 2, 0:16])
        V.tensor_copy(em_s, pb[:, 2, 16:20])
        link(V.tensor_copy(sg.rearrange("p h n -> p (h n)"), pb[:, 3, 0:64]))
        V.engine_nop().then_inc(sem("gate_cols_kept"), 1)
        dve.wait_ge(evacuated, 2 * IC)
        dve.wait_ge(sem("cols_in"), 32)
        N = XPW - 3
        for c in range(IC):
            acc = conv_acc[:, c % 2, :]
            if c >= 2:
                dve.wait_ge(sem("conv_done"), c - 1)
            link(V.tensor_scalar(acc, xp[:, c, 3:3 + N], col_a("conv_w", 3 * IC + c), None, ALU.mult))
            for w in (2, 1, 0):
                ins = V.scalar_tensor_tensor(acc, xp[:, c, w:w + N], col_a("conv_w", w * IC + c), acc,
                                             ALU.mult, ALU.add)
                if w:
                    link(ins)
            ins.then_inc(sem("conv_summed"), 1)
        V.tensor_copy(conv_out[:, :, 0:3], xp[:, :, TP:TP + 3])
        V.tensor_copy(conv_out[:, :, 3:].rearrange("p c (b w) -> p c b w", w=3),
                      xp[:, :, 3 + TP:XPW].rearrange("p c (b w) -> p c b w", w=4)[:, :, :, 1:4]).then_inc(
            sem("conv_kept"), 1)

        for h in range(HA):
            q, k = qt[:, h % 2], kt[:, h % 2]
            dve.wait_ge(sem("rows_spread"), h + 1)
            V.tensor_copy(em, pb[:, 3, TP:2 * TP])
            V.tensor_scalar(p0, pb[:, 3, 0:TP], gcol[:, h:h + 1], 0.0, ALU.add, ALU.min)
            V.tensor_scalar(p1, pb[:, 3, P:TP], gcol[:, HA + h:HA + h + 1], 0.0, ALU.add, ALU.min).then_inc(
                sem("decay_arg"), 1)
            dve.wait_ge(sem("k_turned"), h + 1)
            for s in range(2):
                V.tensor_scalar(wk[:, s, :], pb[:, s, :], gcol[:, 8 + HA * s + h:9 + HA * s + h], None, ALU.mult)
            dve.wait_ge(sem("decay_exp"), h + 1)
            V.tensor_tensor(p0[:, 0:P], p0[:, 0:P], causal, ALU.mult)
            link(V.tensor_tensor(p1, p1, causal, ALU.mult))
            V.tensor_tensor(p0, p0, pb[:, 2, 0:TP], ALU.mult)
            V.tensor_tensor(p1, p1, pb[:, 2, TP:TP + P], ALU.mult).then_inc(sem("weights_t"), 1)
            dve.wait_ge(sem("den_kept"), h + 1)
            link(V.tensor_tensor(den, den, em, ALU.max))
            link(V.reciprocal(den, den))
            dve.wait_ge(sem("num_done"), h + 1)
            link(V.tensor_tensor(hn, pb[:, 0:2, :].rearrange("p b (c t) -> p (b c) t", t=TP),
                                 den.rearrange("p (o t) -> p o t", o=1).to_broadcast([P, HC, TP]), ALU.mult))
            sov = so[:, h * HC:(h + 1) * HC, 0:TP]
            V.tensor_tensor(sov, sov, hn, ALU.mult).then_inc(sem("num_used"), 1)
            if h == 0:
                dve.wait_ge(sem("state_n_in"), 16)
            if h:
                dve.wait_ge(sem("state_read"), NSM * h)
            ws = sg[:, h, 0:NSM].rearrange("p (o b) -> p o b", o=1).to_broadcast([P, HC, NSM])
            wd = sg[:, h, NSM:2 * NSM].rearrange("p (o b) -> p o b", o=1).to_broadcast([P, HC, NSM])
            V.tensor_tensor(kws, k[:, :, TP:T], ws, ALU.mult)
            for c in range(HC):
                V.tensor_copy(qm[:, c].rearrange("p a b -> p (a b)")[:, 0:NSM * 33 - 32:33], q[:, c, TP:T])
            link(V.tensor_tensor(n_new[:, h], n_in[:, h], wd, ALU.mult))
            link(V.tensor_tensor(n_new[:, h], n_new[:, h], kws, ALU.add))
            for a in range(4):
                last = V.tensor_tensor(qn[:, :, a, 0:NSM], q[:, :, TP:T], n_new[:, h], ALU.mult)
            last.then_inc(sem("sample_ready"), 1)
            for b in range(NSM):
                n = NSM * h + b
                dve.wait_ge(sem("v_spread"), n + 1)
                dve.wait_ge(sem("state_decayed"), n + 1)
                for c in range(HC):
                    st = cs[:, n % 3, c, :]
                    last = V.scalar_tensor_tensor(st, pb[:, 2 + b % 2, :], kws[:, c, b:b + 1], st,
                                                  ALU.mult, ALU.add)
                last.then_inc(sem("state_new"), 1)
            dve.wait_ge(sem("den_s_kept"), h + 1)
            link(V.tensor_tensor(den_s[:, 0:1], den_s[:, 0:1], em_s[:, h:h + 1], ALU.max))
            link(V.reciprocal(den_s[:, 1:2], den_s[:, 0:1]))
            dve.wait_ge(sem("state_read"), NSM * (h + 1))
            V.tensor_scalar(hs, pb[:, 1, :], den_s[:, 1:2], None, ALU.mult).then_inc(
                sem("h_sample"), 1)
            dve.wait_ge(sem("head_done"), h + 1)
            sov = so[:, h * HC:(h + 1) * HC, TP:T]
            V.tensor_tensor(sov, sov, pb[:, 0, 8:8 + HC * NSM].rearrange("p (c b) -> p c b", b=NSM),
                            ALU.mult).then_inc(sem("head_gated"), 1)
        dve.wait_ge(evacuated, out_groups)
        norm(0, "mix_g", "mix_b", 0)
        peer(0)
        norm(1, "ffn_g", "ffn_b", 0)
        V.memset(qbd, 0.0)
        dve.wait_ge(evacuated, kv_groups)
        dve.wait_ge(sem("kw_in"), 16)
        V.tensor_copy(kw[:, :, :, WINDOW - 1], ktb[:, :, TP:T]).then_inc(sem("window_ready"), 1)
        dve.wait_ge(evacuated, bq_groups)
        link(V.engine_nop())
        pitch = big.ap[0][0]
        for half in range(2):
            rr = slice(half * HD, (half + 1) * HD)
            base = qbd[rr, 0, 0, 2 * half:2 * half + 1]
            for G in range(2):
                dst = bass.AP(base.tensor, base.offset + G * (P + 8),
                              [[pitch, HD], [4, 2], [1, 2], [2 * P + 16, NSM]])
                last = V.tensor_copy(dst, qb[rr, 4 * G:4 * G + 4, TP:T].rearrange("p (a c) b -> p a c b", c=2))
        last.then_inc(sem("q_spread"), 1)
        dve.wait_ge(sem("bias_b_in"), 64)
        for i in range(8):
            blk, g4 = i // 4, i % 4
            nk = P * (blk + 1)
            s4 = ss[:, i % 2, :, 0:nk]
            dve.wait_ge(sem("att_scores"), i + 1)
            if i >= 2:
                dve.wait_ge(sem("att_turned"), i - 1)
            src = pa[:, 2 * (i % 2):2 * (i % 2) + 2, :].rearrange("p b (e k) -> p (b e) k", e=2)[:, :, 0:nk]
            link(V.scalar_tensor_tensor(s4, src, HD ** -0.5, bias[:, 4 * g4:4 * g4 + 4, 2 * P - nk:2 * P],
                                        ALU.mult, ALU.add))
            V.engine_nop().then_inc(sem("att_scored"), 1)
            m, sk, dn = mx[:, i % 2, :], sink[:, 4 * g4:4 * g4 + 4], dx[:, i % 2, :]
            link(V.tensor_reduce(m, s4, AX.X, ALU.max))
            link(V.tensor_tensor(m, m, sk, ALU.max))
            V.tensor_tensor(dn, sk, m, ALU.subtract)
            V.tensor_tensor(s4, s4, m.rearrange("p (e o) -> p e o", o=1).to_broadcast([P, 4, nk]),
                            ALU.subtract).then_inc(sem("att_shifted"), 1)
            dve.wait_ge(sem("att_exp"), i + 1)
            link(V.tensor_reduce(sx[:, i % 2, :], s4, AX.X, ALU.add))
            link(V.tensor_tensor(dn, dn, sx[:, i % 2, :], ALU.add))
            link(V.reciprocal(dn, dn))
            V.tensor_tensor(s4, s4, dn.rearrange("p (e o) -> p e o", o=1).to_broadcast([P, 4, nk]),
                            ALU.mult).then_inc(sem("att_probs"), 1)
            dve.wait_ge(sem("att_out"), i + 1)
            V.tensor_copy(ot[:, 2 * g4:2 * g4 + 2, blk * P:(blk + 1) * P],
                          pb[:, 2, 0:2 * P].rearrange("p (c q) -> p c q", c=2)).then_inc(sem("att_out_kept"), 1)
        dve.wait_ge(sem("att_s_scores"), 1)
        link(V.scalar_tensor_tensor(ss_s, pb[:, 3, 0:WINDOW], HD ** -0.5, bias_s, ALU.mult, ALU.add))
        link(V.tensor_reduce(small_s[:, 0:1], ss_s, AX.X, ALU.max))
        link(V.tensor_tensor(small_s[:, 0:1], small_s[:, 0:1], sink_s, ALU.max))
        V.tensor_tensor(small_s[:, 1:2], sink_s, small_s[:, 0:1], ALU.subtract)
        V.tensor_scalar(ss_s, ss_s, small_s[:, 0:1], None, ALU.subtract).then_inc(sem("att_s_shifted"), 1)
        dve.wait_ge(sem("att_s_exp"), 1)
        link(V.tensor_reduce(small_s[:, 2:3], ss_s, AX.X, ALU.add))
        link(V.tensor_tensor(small_s[:, 2:3], small_s[:, 2:3], small_s[:, 1:2], ALU.add))
        link(V.reciprocal(small_s[:, 3:4], small_s[:, 2:3]))
        V.tensor_scalar(ss_s, ss_s, small_s[:, 3:4], None, ALU.mult).then_inc(sem("att_s_probs"), 1)
        dve.wait_ge(sem("att_s_turned"), 1)
        V.tensor_copy(pt_s, pb[:, 3, 128:256]).then_inc(sem("att_s_kept"), 1)
        dve.wait_ge(sem("att_s_out"), 1)
        for half in range(2):
            rr = slice(half * HD, (half + 1) * HD)
            src = pb[rr, 3, 256:256 + NSM * 16].rearrange("p (b a h c) -> p a c b h", b=NSM, h=2, c=2)
            last = V.tensor_copy(ot[rr, :, TP:T].rearrange("p (a c) b -> p a c b", c=2), src[:, :, :, :, half])
        last.then_inc(sem("ot_ready"), 1)
        dve.wait_ge(evacuated, bo_groups)
        norm(2, "mix_g", "mix_b", 1)
        peer(1)
        norm(3, "ffn_g", "ffn_b", 1)

    @block.gpsimd
    def _(pool):
        def lows(a, b):
            n0 = n_split(a)
            with pool.Fori(0, (b - a) // RING) as it:
                for k in range(RING):
                    for half in range(2):
                        v, o = 2 * ((n0 + k) % 2) + half, slice(half * 512, (half + 1) * 512)
                        pool.wait_ge(high_done, it * (2 * RING) + (2 * (n0 + k) + half + 1))
                        nc.gpsimd.tensor_tensor(split[:, v, 1, :], ring[:, (a + k) % RING, o], split_f[:, v, 0, :],
                                                ALU.subtract).then_inc(low_done["pool"], 1)

        pool.dma_start(relb[0:NB, :], io["rel_bias"]).then_inc(sem("bias_in"), 16)
        pool.dma_start(onehot[0:NB, :], io["onehot"]).then_inc(sem("bias_in"), 16)
        pool.wait_ge(sem("bias_rows_kept"), 1)
        pool.dma_start(io["bias_rows"], rt[0:HB, :].rearrange("p (o w) -> p o w", o=1).to_broadcast(
            [HB, P, BIASW])).then_inc(sem("bias_stored"), 16)
        for n in range(3):
            pool.dma_start(cs[:, n], io["state_in"][n]).then_inc(sem(f"state_in_{n}"), 16)
        lows(U_IN, U_QKV)
        pool.wait_ge(sem("m_kept"), 1)
        pool.dma_start(io["m_out"], m_out[0:HA, :]).then_inc(sem("small_out"), 16)
        pool.wait_ge(sem("conv_kept"), 1)
        pool.dma_start(io["conv_out"], conv_out).then_inc(sem("small_out"), 16)
        for h in range(HA):
            pool.wait_ge(sem("c_kept"), HC * (h + 1))
            pool.dma_start(io["c_prompt"][h], c_out).then_inc(sem("c_stored"), 16)
            for b in range(NSM):
                n = NSM * h + b
                pool.wait_ge(sem("state_new"), n + 1)
                pool.dma_start(io["state_out"][n], cs[:, n % 3]).then_inc(sem(f"state_out_{n % 3}"), 16)
                if n >= 1 and n + 2 < NSM * HA:
                    o = n - 1
                    pool.wait_ge(sem("state_read"), o + 1)
                    pool.wait_ge(sem(f"state_out_{o % 3}"), 16 * (o // 3 + 1))
                    pool.dma_start(cs[:, o % 3], io["state_in"][n + 2]).then_inc(sem(f"state_in_{o % 3}"), 16)
        pool.wait_ge(sem("head_gated"), HA)
        pool.wait_ge(sem("n_kept"), HA)
        pool.dma_start(io["n_prompt"], n_prompt).then_inc(sem("small_out"), 16)
        pool.dma_start(io["n_sample"], n_new).then_inc(sem("small_out"), 16)
        pool.wait_ge(sem("small_out"), 64)
        pool.wait_ge(sem("c_stored"), 16 * HA)
        for s in range(3):
            pool.wait_ge(sem(f"state_out_{s}"), 16 * ((NSM * HA - s + 2) // 3))

        def load_skeys(L):
            pool.dma_start(skeys, io["skeys"][L]).then_inc(sem("skeys_in"), 16)

        def hot_j(L):
            pool.wait_ge(sem("choice_kept"), L + 1)
            io_b = iota.rearrange("p (o n) -> p o n", o=1).to_broadcast([P, 8, NK])

            def one(it, s):
                v = turned[:, 1, bass.ds(it * 16 + 8 * s, 8)].rearrange("p (t o) -> p t o", o=1)
                nc.gpsimd.tensor_tensor(hot[:, s, 1, :, :], io_b, v.to_broadcast([P, 8, NK]),
                                        ALU.subtract).then_inc(sem("lane_minus_j"), 1)

            one(0, 0)
            one(0, 1)
            with pool.Fori(1, SETS // 2) as it:
                for s in range(2):
                    pool.wait_ge(sem("gates_spread"), it * 2 + (SETS * L + s - 1))
                    one(it, s)
            pool.wait_ge(sem("gates_spread"), SETS * (L + 1) - 2)
            one(SETS // 2, 0)

        pool.wait_ge(sem("ln_sum"), 1)
        load_skeys(0)
        lows(U_PQ[0], U_V[0])
        hot_j(0)
        pool.wait_ge(sem("ln_sum"), 2)
        pool.dma_start(kw[:, :, :, 0:WINDOW - 1], io["kw_in"]).then_inc(sem("kw_in"), 16)
        pool.dma_start(vw[0:WINDOW - 1], io["vw_in"]).then_inc(sem("vw_in"), 16)
        pool.wait_ge(sem("bias_stored"), 16)
        br = io["bias_rows"]
        pool.dma_start(bias, bass.AP(br.tensor, br.offset + WINDOW - 1,
                                     [[BIASW - 1, P], [P * BIASW, HB], [1, 2 * WINDOW]])).then_inc(sem("bias_b_in"), 16)
        pool.dma_start(bias_s, bass.AP(br.tensor, br.offset + WINDOW,
                                       [[0, NSM], [P * BIASW, HB], [1, WINDOW]])).then_inc(sem("bias_b_in"), 16)
        sk = io["sinks"]
        pool.dma_start(sink, bass.AP(sk.tensor, sk.offset, [[0, P], [1, HB]])).then_inc(sem("bias_b_in"), 16)
        pool.dma_start(sink_s, bass.AP(sk.tensor, sk.offset, [[0, NSM], [1, HB], [1, 1]])).then_inc(
            sem("bias_b_in"), 16)
        pool.wait_ge(sem("vb_kept"), 1)
        pool.dma_start(vw[WINDOW - 1:WINDOW, :, :], vsb[0:NSM, :]).then_inc(sem("vw_in"), 16)
        pool.dma_start(io["k_prompt"], ktb[:, :, P:TP]).then_inc(sem("win_out"), 16)
        pool.dma_start(io["v_prompt"], vnb[:, 1, :]).then_inc(sem("win_out"), 16)
        lows(U_BQ, U_BO)
        pool.wait_ge(sem("window_ready"), 1)
        pool.dma_start(io["k_sample"], kw).then_inc(sem("win_out"), 16)
        pool.wait_ge(sem("vw_in"), 32)
        pool.dma_start(io["v_sample"], vw).then_inc(sem("win_out"), 16)
        pool.wait_ge(sem("win_out"), 64)
        pool.wait_ge(sem("ln_sum"), 3)
        load_skeys(1)
        lows(U_PQ[1], U_V[1])
        hot_j(1)


def _head_order():
    return [4 * (2 * (c // 4) + half) + c % 4 for c in range(DC) for half in range(2)]


def _row_order():
    return [_head_order()[2 * (2 * a + c) + half] for a in range(DC // 2) for half in range(2) for c in range(2)]


def _constants():
    f = np.float32
    c = np.zeros((P, NCONST), f)
    lane = np.arange(P)

    def put(name, v):
        a, n = CONSTS[name]
        c[:, a:a + n] = v
    put("ident", np.eye(P, dtype=f))
    put("iota", np.broadcast_to(lane.astype(f), (P, P)))
    put("ones", np.ones((P, P), f))
    sel4 = np.zeros((HA, HA, P), f)
    sel8 = np.zeros((NSM, NSM, P), f)
    for i in range(HA):
        sel4[i, i] = 1
    for i in range(NSM):
        sel8[i, i] = 1
    onehot = np.zeros((NB, WINDOW), f)
    exact = NB // 2
    for y in range(WINDOW):
        d = WINDOW - 1 - y
        b = d if d < exact else min(NB - 1, exact + int(np.log(d / exact) / np.log(128 / exact) * (NB - exact)))
        onehot[b, y] = 1
    causal = (lane[:, None] <= lane[None, :]).astype(f)
    fold = (lane[:, None] % 32 == lane[None, 0:NSM]).astype(f)
    return c, sel4, sel8, onehot, causal, fold


def kernel(x_prompt, x_sample, state_mlstm_C, state_mlstm_n, state_mlstm_m, state_mlstm_conv,
           cache_k_win, cache_v_win, a_w_in, a_b_in, a_conv_w, a_conv_b, a_w_q, a_w_k, a_w_v,
           a_w_out, kv_w, b_w_q, b_w_o, b_sinks, rel_bias, ln_mix_g, ln_mix_b, ln_ffn_g,
           ln_ffn_b, peer_w_q, peer_subkeys, peer_u, peer_v):
    import concourse.bacc as bacc
    from concourse.bass_utils import run_bass_kernel_spmd

    f = np.float32
    A = lambda a: np.asarray(a)
    order = _head_order()
    rows = _row_order()
    qcols = np.concatenate([np.arange(h * HD, (h + 1) * HD) for h in order])

    units = np.empty((N_UNITS, P, 1024), f)

    def kxm(w):
        m = w.shape[1] // P
        return w.reshape(DC, P, m, P).transpose(2, 1, 0, 3).reshape(m, P, 1024)

    w_in = A(a_w_in)[0]
    units[U_IN:U_QKV] = kxm(w_in[:, 0:2 * INNER])
    for h in range(HA):
        n = U_QKV + 6 * h
        for i, w in enumerate((A(a_w_q)[0, h], A(a_w_k)[0, h])):
            units[n + 2 * i:n + 2 * i + 2] = w.reshape(HC, P, 2, 256).transpose(2, 1, 0, 3).reshape(2, P, 1024)
        units[n + 4:n + 6] = A(a_w_v)[0, h].reshape(2, 2, P, DH).transpose(0, 2, 1, 3).reshape(2, P, 1024)
    units[U_OUT:U_PQ[0]] = A(a_w_out)[0].reshape(2, DC, P, DC, P).transpose(3, 0, 2, 1, 4).reshape(2 * DC, P, 1024)
    kv = A(kv_w)
    units[U_KV:U_KV + 2] = kxm(kv[:, 0:256])
    units[U_KV + 2:U_KV + 4] = kv[:, 256:512].reshape(2, 4, P, 256).transpose(0, 2, 1, 3).reshape(2, P, 1024)
    units[U_BQ:U_BO] = kxm(A(b_w_q)[0][:, qcols])
    units[U_BO:U_PQ[1]] = kxm(A(b_w_o)[0][qcols, :])
    for L in range(2):
        units[U_PQ[L]:U_U[L]] = kxm(A(peer_w_q)[L])
        units[U_U[L]:U_V[L]] = A(peer_u)[L].reshape(NK, NK, DC, P).transpose(0, 3, 2, 1).reshape(NK, P, 1024)
        units[U_V[L]:U_V[L] + NK] = A(peer_v)[L].reshape(NK, P, 1024)

    def fm(a):
        c = a.shape[-1] // P
        a = np.moveaxis(a, -1, 0)
        return np.moveaxis(a.reshape((c, P) + a.shape[1:]), 0, 1)

    const, sel4, sel8, onehot, causal, fold = _constants()
    xs = np.concatenate([A(x_prompt)[0], A(x_sample)[:, 0]], axis=0)
    b_in = A(a_b_in)[0]
    cols_a = np.concatenate([
        fm(b_in[0:2 * INNER]).reshape(P, -1),
        np.moveaxis(fm(A(a_conv_w)[0]), 2, 1).reshape(P, -1),
        fm(A(a_conv_b)[0]).reshape(P, -1), causal, fold], axis=1)
    cols = np.concatenate([np.moveaxis(fm(A(w)), 2, 1).reshape(P, -1)
                           for w in (ln_mix_g, ln_mix_b, ln_ffn_g, ln_ffn_b)] + [np.full((P, 1), LN_EPS, f)], axis=1)
    C = A(state_mlstm_C)[0]
    arrays = {
        "units": units,
        "x": fm(xs),
        "const": const, "cols": cols, "cols_a": cols_a, "sel4": sel4, "sel8": sel8, "onehot": onehot,
        "w_gate": w_in[:, 2 * INNER:].reshape(DC, P, 8).transpose(1, 0, 2),
        "b_gate": b_in[2 * INNER:].reshape(2, HA).T,
        "m_in": A(state_mlstm_m)[0].T,
        "conv_in": fm(A(state_mlstm_conv)[0]),
        "n_in": A(state_mlstm_n)[0].reshape(NSM, HA, HC, P).transpose(3, 1, 2, 0),
        "state_in": C.transpose(1, 0, 2, 3).reshape(HA * NSM, HC, P, DH).transpose(0, 2, 1, 3),
        "kw_in": A(cache_k_win)[:, 1:].reshape(NSM, WINDOW - 1, 2, P).transpose(3, 2, 0, 1),
        "vw_in": A(cache_v_win)[:, 1:].reshape(NSM, WINDOW - 1, KVH * HD).transpose(1, 0, 2),
        "rel_bias": A(rel_bias)[:, rows],
        "sinks": A(b_sinks)[0][rows],
        "skeys": A(peer_subkeys).transpose(0, 4, 1, 2, 3).reshape(2, P, 2 * PH, NK),
    }
    outs = {
        "y": (P, DC, T), "c_prompt": (HA, P, HC, DH), "n_prompt": (P, HA, HC), "m_out": (HA, 1 + NSM),
        "conv_out": (P, IC, 3 + 3 * NSM), "k_prompt": (P, 2, WINDOW), "v_prompt": (WINDOW, KVH * HD),
        "state_out": (HA * NSM, P, HC, DH), "n_sample": (P, HA, HC, NSM),
        "k_sample": (P, 2, NSM, WINDOW), "v_sample": (WINDOW, NSM, KVH * HD),
    }
    nc = bacc.Bacc("TRN2", target_bir_lowering=False, num_devices=1)
    io, feed = {}, {}
    for name, a in arrays.items():
        a = np.ascontiguousarray(a)
        feed["in_" + name] = a
        io[name] = nc.dram_tensor("in_" + name, a.shape, F32, kind="ExternalInput").ap()
    for name, shape in outs.items():
        io[name] = nc.dram_tensor("out_" + name, shape, F32, kind="ExternalOutput").ap()
    io["bias_rows"] = nc.dram_tensor("bias_rows", (HB, P, BIASW), F32, kind="Internal").ap()
    build(nc, io)
    r = run_bass_kernel_spmd(nc, [feed], core_ids=[0]).results[0]
    o = {name: r["out_" + name] for name in outs}

    y = o["y"].transpose(2, 1, 0).reshape(T, D)
    conv = o["conv_out"].transpose(2, 1, 0).reshape(3 + 3 * NSM, INNER)
    so_ = o["state_out"].reshape(HA, NSM, P, HC, DH).transpose(1, 0, 3, 2, 4).reshape(1, NSM, HA, DH, DH)
    return tuple(np.ascontiguousarray(a) for a in (
        y[:TP].reshape(1, TP, D),
        y[TP:].reshape(NSM, 1, D),
        o["c_prompt"].transpose(0, 2, 1, 3).reshape(1, 1, HA, DH, DH),
        o["n_prompt"].transpose(1, 2, 0).reshape(1, 1, HA, DH),
        o["m_out"][:, 0].reshape(1, 1, HA),
        conv[0:3].reshape(1, 1, 3, INNER),
        o["k_prompt"].transpose(2, 1, 0).reshape(1, WINDOW, KVH, HD),
        o["v_prompt"].reshape(1, WINDOW, KVH, HD),
        so_,
        o["n_sample"].transpose(3, 1, 2, 0).reshape(1, NSM, HA, DH),
        o["m_out"][:, 1:].T.reshape(1, NSM, HA),
        conv[3:].reshape(1, NSM, 3, INNER),
        o["k_sample"].transpose(2, 3, 1, 0).reshape(NSM, WINDOW, KVH, HD),
        o["v_sample"].transpose(1, 0, 2).reshape(NSM, WINDOW, KVH, HD),
    ))
```

```python
from contextlib import ExitStack

import numpy as np

import concourse.bass as bass
from concourse import mybir

F32 = mybir.dt.float32
U32 = mybir.dt.uint32
ALU = mybir.AluOpType
ACT = mybir.ActivationFunctionType
AX = mybir.AxisListType

P = 128
D = 1024
TP = 256
NSM = 8
T = TP + NSM
DC = D // P
INNER = 2048
IC = INNER // P
HA = 4
DH = INNER // HA
HC = DH // P
CONV_W = 4
KVH = 4
GROUP = 4
HB = 16
HD = 64
WINDOW = 128
NB = 32
PH = 8
NK = 128
TOPK = 16
DEPTH = 2
ALPHA = (2 * DEPTH) ** 0.25
LN_EPS = 1e-5
NEG = -1e30
LOWEST = -3.0e38
RING = 4
XPW = 3 + TP + 4 * NSM
BIASW = 3 * WINDOW

U_IN = 0
U_QKV = U_IN + 2 * IC
U_OUT = U_QKV + 6 * HA
U_PQ = [U_OUT + 2 * DC, 0]
U_U = [U_PQ[0] + 2 * PH, 0]
U_V = [U_U[0] + NK, 0]
U_KV = U_V[0] + NK
U_BQ = U_KV + 4
U_BO = U_BQ + DC
U_PQ[1] = U_BO + DC
U_U[1] = U_PQ[1] + 2 * PH
U_V[1] = U_U[1] + NK
N_UNITS = U_V[1] + NK

PHASES = [("pool", U_IN, U_QKV), ("pe", U_QKV, U_PQ[0]), ("pool", U_PQ[0], U_V[0]), ("dve", U_V[0], U_KV),
          ("pool", U_KV, U_BO), ("pe", U_BO, U_PQ[1]), ("pool", U_PQ[1], U_V[1]),
          ("dve", U_V[1], N_UNITS)]


def _before(n, *kinds):
    return sum(max(0, min(n, b) - a) for kind, a, b in PHASES if kind in kinds)


def n_split(n):
    return _before(n, "pool", "dve")

COLS = {}
_at = 0
for _n, _c in (("mix_g", 2 * DC), ("mix_b", 2 * DC), ("ffn_g", 2 * DC), ("ffn_b", 2 * DC), ("eps", 1)):
    COLS[_n] = (_at, _c)
    _at += _c
NCOLS = _at
COLS_A = {}
_at = 0
for _n, _c in (("b_in", 2 * IC), ("conv_w", CONV_W * IC), ("conv_b", IC), ("causal", P), ("fold", NSM)):
    COLS_A[_n] = (_at, _c)
    _at += _c
NCOLS_A = _at

CONSTS = {}
_at = 0
for _n, _c in (("ident", P), ("iota", P), ("ones", P)):
    CONSTS[_n] = (_at, _c)
    _at += _c
NCONST = _at
SETS = T // 8
EXP_AT = 56
TURN_AT = 60
SPREAD_AT = 64
SPREAD_TO = SPREAD_AT + 4 * (SETS // 2)
assert SETS % 2 == 1 and SPREAD_TO <= NK and all(n % RING == 0 for n in (EXP_AT, TURN_AT, SPREAD_AT, NK))
SLOTS = 5
NORMS = [("mix_g", "mix_b"), ("ffn_g", "ffn_b")] * DEPTH
TILES = [(0, P), (P, P), (TP, NSM)]


def build(nc, io):
    with ExitStack() as ctx:
        _build(nc, io, ctx)


def _build(nc, io, ctx):
    def sb(name, shape, dt=F32):
        return ctx.enter_context(nc.sbuf_tensor(name, shape, dt))

    sems = {}

    def sem(name):
        if name not in sems:
            sems[name] = ctx.enter_context(nc.semaphore(name))
        return sems[name]

    f32r = mybir.dt.float32r
    n_big, n_x = NK * T, DC * T
    sizes = [("big", n_big), ("raw", RING * 1024), ("halves", 4096), ("xh", n_x), ("xl", n_x), ("scb", 4096),
             ("top", 528 + 2 * 256 + 2 * 128 + 384 + 768), ("const", NCONST), ("cols", NCOLS)]
    total = sum(n for _, n in sizes)
    sb("arena", [P, total])
    base = nc.sbuf_base - 4 * total
    start = {}
    where = 0
    for name, n in sizes:
        start[name] = where
        where += n

    def area(name):
        return nc.alloc_sbuf_tensor_at(name, [P, dict(sizes)[name]], F32, offset=base + 4 * start[name])[:, :]

    def rounded(name, over, shape, skip=0):
        return nc.alloc_sbuf_tensor_at(name, shape, f32r, offset=base + 4 * (start[over] + skip))

    big = area("big")
    ring = area("raw").rearrange("p (k n) -> p k n", k=RING)
    scb = area("scb")
    const, cols = area("const"), area("cols")
    halves = area("halves")
    split = rounded("split", "halves", [P, 4, 2, 512])
    xh = rounded("xh", "xh", [P, DC, T])
    xl = rounded("xl", "xl", [P, DC, T])
    wsplit = rounded("wsplit", "scb", [P, 4, 2, T])
    xh_f, xl_f, split_f, wsplit_f = (v[:].bitcast(F32) for v in (xh, xl, split, wsplit))

    def cst(name, rows=P):
        a, n = CONSTS[name]
        return const[0:rows, a:a + n]

    def col(name, i):
        return cols[:, COLS[name][0] + i:COLS[name][0] + i + 1]

    ident, iota, ones = cst("ident"), cst("iota"), cst("ones")
    ones_col = ones[:, 0:1]

    def carver(of):
        at = [0]

        def carve(*dims, dt=F32):
            n = 1
            for d in dims:
                n *= d
            v = of[:, at[0]:at[0] + n]
            at[0] += n
            if dt is not F32:
                v = v.bitcast(dt)
            if len(dims) == 1:
                return v
            names = "abcd"[:len(dims)]
            return v.rearrange("p (%s) -> p %s" % (" ".join(names), " ".join(names)), **dict(zip(names, dims)))
        return carve

    top = area("top")
    carve = carver(top)
    tmp = carve(528)
    top_s = carve(2 * PH, TOPK)
    top_iu = carve(2 * PH, TOPK, dt=U32)
    best_u = carve(PH, TOPK, dt=U32)
    rank_f = carve(PH, TOPK)
    best_s = carve(3, PH, TOPK)
    sel_i = carve(3, PH * TOPK)
    sel_j = carve(3, PH * TOPK)
    top_if = top_iu.bitcast(F32)
    rank_u = rank_f.bitcast(U32)
    gsum = rank_f.rearrange("p h k -> p (h k)")[:, 0:3 * PH].rearrange("p (a h) -> p a h", a=3)
    turned = top[:, 0:3 * T].rearrange("p (k t) -> p k t", k=3)
    gelu = top[:, 3 * T:(3 + RING) * T].rearrange("p (k t) -> p k t", k=RING)

    pa = ctx.enter_context(nc.psum_tensor("pa", [P, 4, 512], F32))
    pb = ctx.enter_context(nc.psum_tensor("pb", [P, 4, 512], F32))

    carve = carver(big)
    so = carve(IC, T)
    xp = carve(IC, XPW)
    cs = carve(3, HC, DH)
    c_out = carve(HC, DH)
    conv_out = carve(IC, 3 + 3 * NSM)
    n_in = carve(HA, HC, NSM)
    n_new = carve(HA, HC, NSM)
    n_prompt = carve(HA, HC)
    m_in = carve(NSM)
    m_out = carve(1 + NSM)
    conv_in = carve(IC, NSM, 3)
    w_gate = carve(DC, 8)
    relb = carve(HB)
    onehot = carve(WINDOW)
    cols_a = carve(NCOLS_A)
    b_rows = carve(2)
    gcol = carve(16)
    sg = carve(HA, 2 * NSM)
    em_s = carve(HA)
    den_s = carve(2)
    kws = carve(HC, NSM)
    qm = carve(HC, NSM, 32)
    qn = carve(HC, 4, 32)
    conv_acc = carve(2, XPW - 3)
    vn = carve(2, 2, DH)
    vs = carve(2, DH)
    wk = carve(2, DH)
    den = carve(TP)
    qt = carve(2, HC, T)
    kt = carve(2, HC, T)
    xc = big[:, n_big - IC * T:].rearrange("p (c t) -> p c t", t=T)
    carve = carver(scb)
    rows = carve(8, 272)
    sel4 = carve(HA, P)
    sel8 = carve(NSM, P)
    rt = carve(BIASW)
    carve = carver(top)
    hn = carve(HC, TP)
    hs = carve(DH)
    em = carve(TP)
    p0 = carve(TP)
    p1 = carve(P)
    em_row = carve(4, 32)

    def state(n):
        k = n % SLOTS
        return cs[:, k] if k < 3 else halves[:, (k - 3) * HC * DH:(k - 2) * HC * DH].rearrange(
            "p (c e) -> p c e", e=DH)

    def col_a(name, i=0, n=1):
        return cols_a[:, COLS_A[name][0] + i:COLS_A[name][0] + i + n]

    causal, fold = col_a("causal", 0, P), col_a("fold", 0, NSM)

    carve = carver(big)
    qb = carve(DC, T)
    ktb = carve(2, T)
    vnb = carve(2, KVH * HD)
    vsb = carve(KVH * HD)
    kw = carve(2, NSM, WINDOW)
    vw = carve(NSM, KVH * HD)
    bias = carve(HB, 2 * WINDOW)
    bias_s = carve(WINDOW)
    ss = carve(3, 4, 2 * WINDOW)
    pt = carve(2, 4, 2, WINDOW)
    ot = carve(DC, T)
    qbd = carve(NSM, 2, P)
    sink = carve(HB)
    sink_s = carve(1)
    mx = carve(2, 4)
    neg_mx = carve(2, 4)
    sx = carve(2, 4)
    dx = carve(2, 4)
    ss_s = carve(WINDOW)
    pt_s = carve(P)
    small_s = carve(4)

    sq, x = (big[:, n_big - k * n_x:n_big - (k - 1) * n_x].rearrange("p (c t) -> p c t", t=T) for k in (2, 1))
    res = top[:, 0:n_x].rearrange("p (c t) -> p c t", t=T)
    rstd = top[:, n_x:n_x + T]

    w3 = big.rearrange("p (i t) -> p i t", t=T)
    skeys = big[:, (NK - 5 * PH) * T:(NK - 5 * PH) * T + 2 * PH * NK].rearrange("p (h n) -> p h n", n=NK)
    pq = w3[:, NK - 4 * PH:NK - 2 * PH, :]
    scores = scb.rearrange("p (a h n) -> p a h n", a=2, n=NK)
    score_of = [scores[:, 0], scores[:, 1], pb[:, :, :].rearrange("p b (h n) -> p (b h) n", n=NK)]
    hot = scb.rearrange("p (s k t n) -> p s k t n", s=2, k=2, t=8)

    landed = [sem(f"unit_landed_{k}") for k in range(RING)]
    units_used = sem("units_used")
    halves_used = sem("halves_used")
    high_done = sem("high_done")
    low_done = {k: sem(f"low_done_{k}") for k in ("pool", "dve")}
    evacuated = sem("bank_evacuated")

    def gate_bank(s):
        return pb[:, 2 * s:2 * s + 2, :]

    def turned_at(i):
        if i < 4:
            return pb[:, 0, :].rearrange("p (e s q) -> p e s q", e=4, s=1)
        return pb[:, 0:2, :].rearrange("p b (e s q) -> p (b e) s q", e=2, s=2)

    def sum_bank(li, k):
        return (pa if li % 2 else pb)[:, k, 0:T]

    out_groups = 2 * IC + HA * 2 * HC + DC
    peer_total = 2 * PH + NK
    peer_groups = [out_groups + peer_total, 0]
    kv_groups = peer_groups[0] + 2
    bq_groups = kv_groups + DC
    peer_groups[1] = bq_groups + peer_total

    block = ctx.enter_context(nc.Block())

    @block.sync
    def _(sp):
        sp.dma_start(ring[:, 0, :], io["units"][0]).then_inc(landed[0], 16)
        sp.dma_start(x, io["x"]).then_inc(sem("x_in"), 16)
        for k in range(1, RING):
            sp.dma_start(ring[:, k, :], io["units"][k]).then_inc(landed[k], 16)
        for dst, name in ((w_gate, "w_gate"), (b_rows[0:HA, :], "b_gate"), (m_in[0:HA, :], "m_in"),
                          (sel4[0:HA, :, :], "sel4"), (sel8[0:NSM, :, :], "sel8")):
            sp.dma_start(dst, io[name]).then_inc(sem("gate_in"), 16)
        sp.dma_start(const, io["const"]).then_inc(sem("const_in"), 16)
        sp.dma_start(cols, io["cols"]).then_inc(sem("cols_in"), 16)
        sp.dma_start(cols_a, io["cols_a"]).then_inc(sem("cols_in"), 16)
        sp.dma_start(conv_in, io["conv_in"]).then_inc(sem("conv_in"), 16)
        sp.dma_start(n_in, io["n_in"]).then_inc(sem("state_n_in"), 16)
        sp.dma_start(relb[0:NB, :], io["rel_bias"]).then_inc(sem("bias_in"), 16)
        sp.dma_start(onehot[0:NB, :], io["onehot"]).then_inc(sem("bias_in"), 16)
        for kind, a, b in PHASES:
            done = _before(a, kind)
            b = min(b, N_UNITS - RING)
            with sp.Fori(0, (b - a) // RING) as it:
                for k in range(RING):
                    if kind == "pe":
                        sp.wait_ge(units_used, it * RING + (done + k + 1))
                    else:
                        sp.wait_ge(low_done[kind], it * (2 * RING) + 2 * (done + k + 1))
                    sp.dma_start(ring[:, k, :], io["units"][it * RING + (a + RING + k)]).then_inc(landed[k], 16)

    @block.tensor
    def _(pe):
        unit = [0]
        group = [0]
        banks = [4]

        def mm(out, lhs, rhs, start=True, stop=True):
            return pe.matmul(out, lhs, rhs, start=start, stop=stop)

        def next_unit():
            n = unit[0]
            pe.wait_ge(landed[n % RING], 16 * (n // RING + 1))
            unit[0] += 1
            return ring[:, n % RING, :]

        def next_bank():
            g = group[0]
            if g >= 4:
                pe.wait_ge(evacuated, g - banks[0] + 1)
            group[0] += 1
            return pa[:, g % banks[0], :]

        def three(out, w_set, w_at, high, low, first, last):
            w = slice(w_at, w_at + P)
            mm(out, split[:, w_set, 0, w], high, first, False)
            mm(out, split[:, w_set, 0, w], low, False, False)
            return mm(out, split[:, w_set, 1, w], high, False, last)

        def x_tile(out, kind, low_count, k, x_count=None):
            for half in range(2):
                pe.wait_ge(low_done[kind], low_count - 1 + half)
                for c in range(4):
                    kk = 4 * half + c
                    if x_count is not None:
                        pe.wait_ge(sem("x_ready"), x_count + kk + 1)
                    last = three(out, 2 * (k % 2) + half, c * P, xh[:, kk, :], xl[:, kk, :], kk == 0, kk == DC - 1)
                last.then_inc(halves_used, 1)

        def project_x(n_tiles, norms):
            for k in range(n_tiles):
                out = next_bank()
                x_tile(out[:, 0:T], "pool", 2 * _before(unit[0] + 1, "pool"), n_split(unit[0]),
                       None if k or norms is None else DC * norms)
                unit[0] += 1

        def add_up(li, k):
            pe.wait_ge(sem("ln_sum"), DC * li + k + 1)
            return mm(sum_bank(li, 0), ones, x[:, k, :], k == 0, k == DC - 1)

        def project_back(li, src):
            pe.wait_ge(evacuated, group[0])
            for m in range(DC):
                if m >= 4:
                    pe.wait_ge(sem("ln_sum"), DC * li + m - 3)
                w = next_unit()
                for k in range(DC):
                    last = mm(pa[:, m % 4, 0:T], w[:, k * P:(k + 1) * P], src[:, k, :], k == 0, k == DC - 1)
                last.then_inc(units_used, 1)
                if m >= 2:
                    add_up(li, m - 2)

        def norm(li):
            for k in range(0 if li % 2 else DC - 2, DC):
                last = add_up(li, k)
            last.then_inc(sem("ln_mean"), 1)
            for k in range(DC):
                pe.wait_ge(sem("ln_square"), DC * li + k + 1)
                last = mm(sum_bank(li, 1), ones, sq[:, k, :], k == 0, k == DC - 1)
            last.then_inc(sem("ln_var"), 1)

        def peer(L):
            project_x(2 * PH, 2 * L + 1)
            pe.wait_ge(sem("skeys_in"), 16 * (L + 1))
            pe.wait_ge(evacuated, group[0])
            base, g0 = unit[0], group[0]
            low0 = 2 * _before(base, "pool")
            assert base % RING == 0 and base == U_U[L]

            def u_unit(it, i):
                pe.wait_ge(evacuated, it * RING + (g0 + i - 3))
                x_tile(pa[:, (g0 + i) % 4, 0:T], "pool", it * (2 * RING) + (low0 + 2 * i + 2), n_split(base) + i)

            for a, (t0, n) in enumerate(TILES):
                if a:
                    pe.wait_ge(sem("scores_copied"), 2 * L + a)
                for h in range(2 * PH):
                    last = mm(pb[0:n, h // 4, (h % 4) * NK:(h % 4 + 1) * NK], pq[:, h, t0:t0 + n], skeys[:, h, :])
                last.then_inc(sem("scores_done"), 1)
                u_unit(0, a)
            u_unit(0, 3)
            with pe.Fori(1, TURN_AT // RING) as it:
                for k in range(RING):
                    u_unit(it, k)
            pe.wait_ge(sem("gates_done"), L + 1)
            for a, (t0, n) in enumerate(TILES):
                for b, src in enumerate((sel_i, sel_j)):
                    pe.transpose(pb[:, b, t0:t0 + n], src[0:n, a, :], ident[0:n, 0:n])
                last = pe.transpose(pb[:, 2, t0:t0 + n], best_s[0:n, a, :, :].rearrange("p h k -> p (h k)"),
                                    ident[0:n, 0:n])
            last.then_inc(sem("choice_turned"), 1)
            for i in range(TURN_AT, SPREAD_AT):
                u_unit(0, i)

            def gate_set(n, s):
                pe.wait_ge(sem("hot"), n + 1)
                for t in range(8):
                    out = gate_bank(s)[:, t // 4, (t % 4) * NK:(t % 4 + 1) * NK]
                    last = mm(out, hot[:, s, 1, t, :], hot[:, s, 0, t, :])
                last.then_inc(sem("gates_spread"), 1)

            n0 = SETS * L
            for s in range(2):
                gate_set(n0 + s, s)
                for k in range(2):
                    u_unit(0, SPREAD_AT + 2 * s + k)
            with pe.Fori(1, SETS // 2) as it:
                for s in range(2):
                    pe.wait_ge(sem("gates_applied"), it * 2 + (n0 + s - 1))
                    gate_set(it * 2 + (n0 + s), s)
                    for k in range(2):
                        u_unit(it, SPREAD_AT + 2 * s + k)
            pe.wait_ge(sem("gates_applied"), n0 + SETS - 2)
            gate_set(n0 + SETS - 1, 0)
            for i in range(SPREAD_TO, NK):
                u_unit(0, i)
            unit[0] += NK
            group[0] += NK
            pe.wait_ge(sem("gates_applied"), n0 + SETS)
            pe.wait_ge(evacuated, group[0])
            base = unit[0]
            low0 = 2 * _before(base, "dve")

            def y_unit(low_count, w_count, k, first=False, last=False):
                pe.wait_ge(sem("w_low"), w_count)
                for half in range(2):
                    pe.wait_ge(low_done["dve"], low_count - 1 + half)
                    for c in range(4):
                        out = (pa, pb)[half][:, c, 0:T]
                        ins = three(out, 2 * (k % 2) + half, c * P, wsplit[:, k, 0, :], wsplit[:, k, 1, :], first, last)
                    ins.then_inc(halves_used, 1)

            for k in range(RING):
                y_unit(low0 + 2 * k + 2, NK * L + k + 1, k, first=(k == 0))
            with pe.Fori(1, NK // RING - 1) as it:
                for k in range(RING):
                    y_unit(it * (2 * RING) + (low0 + 2 * k + 2), it * RING + (NK * L + k + 1), k)
            for k in range(RING):
                n = NK - RING + k
                y_unit(low0 + 2 * n + 2, NK * L + n + 1, k, last=(k == RING - 1))
            unit[0] += NK

        project_x(2, 0)
        pe.wait_ge(sem("x_in"), 16)
        pe.wait_ge(sem("gate_in"), 80)
        for g in range(2):
            for k in range(DC):
                last = mm(pb[0:HA, g, 0:T], w_gate[:, k, g * HA:(g + 1) * HA], x[:, k, :], k == 0, k == DC - 1)
        last.then_inc(sem("gate_pre"), 1)
        project_x(2 * IC - 2, None)
        pe.wait_ge(sem("bias_in"), 32)
        pe.wait_ge(sem("const_in"), 16)
        mm(pb[0:HB, 0, 0:WINDOW], relb[0:NB, :], onehot[0:NB, :]).then_inc(sem("bias_rows"), 1)

        pe.wait_ge(sem("gate_exps"), 1)
        for s in range(2):
            pe.transpose(pb[:, 2, s * HA:(s + 1) * HA], rows[0:HA, 4, s * P:(s + 1) * P], ident[0:HA, 0:HA])
            pe.transpose(pb[:, 2, 8 + s * HA:8 + (s + 1) * HA], rows[0:HA, 7, s * P:(s + 1) * P], ident[0:HA, 0:HA])
        pe.transpose(pb[:, 2, 16:20], em_row[0:HA].rearrange("p a b -> p (a b)"), ident[0:HA, 0:HA])
        for h in range(HA):
            last = mm(pb[:, 3, h * 16:(h + 1) * 16], sel4[0:HA, h, :], rows[0:HA, 7, TP:TP + 16])
        last.then_inc(sem("gate_cols"), 1)

        banks[0] = 2

        def project_qk(h, u):
            w = next_unit()
            for m in range(2):
                out = next_bank()
                for k in range(HC):
                    last = mm(out[:, 0:T], w[:, k * 256 + m * P:k * 256 + (m + 1) * P], xc[:, h * HC + k, :],
                              k == 0, k == HC - 1)
            last.then_inc(units_used, 1)

        def project_v(h, u):
            w = next_unit()
            for k in range(2):
                kk = 2 * u + k
                src = xp[:, h * HC + kk, :]
                rhs = w[:, k * DH:(k + 1) * DH]
                mm(pb[:, 0, :], src[:, 3:3 + P], rhs, kk == 0, kk == HC - 1)
                mm(pb[:, 1, :], src[:, 3 + P:3 + TP], rhs, kk == 0, kk == HC - 1)
                last = mm(pb[0:NSM, 2, :], src[:, TP + 6:XPW:4], rhs, kk == 0, kk == HC - 1)
            last.then_inc(units_used, 1)

        def prompt_rows(h):
            if h:
                pe.wait_ge(sem("c_kept"), HC * h)
            mm(pb[:, 3, 0:TP], sel4[0:HA, h, :], rows[0:HA, 5, 0:TP])
            mm(pb[:, 3, TP:2 * TP], sel4[0:HA, h, :], rows[0:HA, 6, 0:TP]).then_inc(sem("rows_spread"), 1)

        def prompt_scores(h):
            q, k = qt[:, h % 2], kt[:, h % 2]
            pe.wait_ge(sem("v_kept"), h + 1)
            for c in range(HC):
                mm(pb[:, 2, 0:TP], k[:, c, 0:P], q[:, c, 0:TP], c == 0, c == HC - 1)
            for c in range(HC):
                last = mm(pb[:, 2, TP:TP + P], k[:, c, P:TP], q[:, c, P:TP], c == 0, c == HC - 1)
            last.then_inc(sem("scores_t"), 1)

        def prompt_turn(h):
            k = kt[:, h % 2]
            for s in range(2):
                for c in range(HC):
                    last = pe.transpose(pb[:, s, c * P:(c + 1) * P], k[:, c, s * P:(s + 1) * P], ident)
            last.then_inc(sem("k_turned"), 1)

        def prompt_values(h):
            pe.wait_ge(sem("weights_t"), h + 1)
            mm(pb[:, 3, 0:P], ones[:, 0:P], p0[:, 0:P])
            mm(pb[:, 3, P:TP], ones[:, 0:P], p0[:, P:TP], True, False)
            mm(pb[:, 3, P:TP], ones[:, 0:P], p1, False, True).then_inc(sem("den_done"), 1)
            pe.wait_ge(sem("k_weighted"), h + 1)
            for c in range(HC):
                o = pb[:, c // 2, (c % 2) * TP:(c % 2 + 1) * TP]
                v0, v1 = vn[:, h % 2, 0, c * P:(c + 1) * P], vn[:, h % 2, 1, c * P:(c + 1) * P]
                mm(o[:, 0:P], v0, p0[:, 0:P])
                mm(o[:, P:TP], v0, p0[:, P:TP], True, False)
                last = mm(o[:, P:TP], v1, p1, False, True)
            last.then_inc(sem("num_done"), 1)

        def prompt_close(h):
            pe.wait_ge(sem("den_kept"), h + 1)
            for c in range(HC):
                b = 2 + c % 2
                if c >= 2:
                    pe.wait_ge(sem("c_kept"), HC * h + c - 1)
                mm(pb[:, b, :], wk[:, 0, c * P:(c + 1) * P], vn[:, h % 2, 0, :], True, False)
                mm(pb[:, b, :], wk[:, 1, c * P:(c + 1) * P], vn[:, h % 2, 1, :], False, True).then_inc(sem("c_done"), 1)
            pe.wait_ge(sem("num_used"), h + 1)
            for c in range(HC):
                mm(pb[:, 0, c:c + 1], wk[:, 0, c * P:(c + 1) * P], ones_col, True, False)
                last = mm(pb[:, 0, c:c + 1], wk[:, 1, c * P:(c + 1) * P], ones_col, False, True)
            last.then_inc(sem("n_done"), 1)

        def sample_spread(h, b):
            mm(pa[:, 2, :], sel8[0:NSM, b, :], vs[0:NSM, h % 2, :]).then_inc(sem("v_spread"), 1)

        def sample_open(h):
            pe.wait_ge(sem("sample_ready"), h + 1)
            if h:
                pe.wait_ge(sem("head_gated"), h)
            for c in range(HC):
                last = mm(pa[:, 2, 4:5], qn[:, c].rearrange("p a b -> p (a b)"), ones_col, c == 0, c == HC - 1)
            last.then_inc(sem("den_s_done"), 1)

        def sample_step(h, b):
            n = NSM * h + b
            pe.wait_ge(sem("state_new"), n + 1)
            for c in range(HC):
                last = mm(pa[32 * c:32 * c + 32, 3, :], qm[:, c, b, :], state(n)[:, c, :], b == 0, b == NSM - 1)
            last.then_inc(sem("state_read"), 1)
            if b + 1 < NSM:
                sample_spread(h, b + 1)

        def sample_turn(h):
            pe.wait_ge(sem("h_sample"), h + 1)
            for c in range(HC):
                last = mm(pa[:, 2, 8 + c * NSM:8 + (c + 1) * NSM], hs[:, c * P:(c + 1) * P], fold)
            last.then_inc(sem("head_done"), 1)

        def out_tile():
            w = next_unit()
            out = next_bank()
            for k in range(DC):
                last = mm(out[:, 0:T], w[:, k * P:(k + 1) * P], so[:, k, :], k == 0, k == DC - 1)
            last.then_inc(units_used, 1)

        pe.wait_ge(sem("conv_done"), IC)
        for u in range(4):
            project_qk(0, u)
        pe.wait_ge(sem("gate_cols_kept"), 1)
        for u in range(2):
            project_v(0, u)
        for h in range(HA):
            if h:
                sample_turn(h - 1)
            prompt_rows(h)
            prompt_scores(h)
            sample_open(h)
            prompt_turn(h)
            pe.wait_ge(sem("den_s_kept"), h + 1)
            sample_spread(h, 0)
            prompt_values(h)
            sample_step(h, 0)
            sample_step(h, 1)
            prompt_close(h)
            for b in range(2, NSM):
                sample_step(h, b)
                if h == HA - 1:
                    for _ in range(2 if b < 4 else 1):
                        out_tile()
                elif b < 6:
                    project_qk(h + 1, b - 2)
                else:
                    if b == 6:
                        pe.wait_ge(sem("n_kept"), h + 1)
                        pe.wait_ge(sem("c_kept"), HC * (h + 1))
                    project_v(h + 1, b - 6)
        sample_turn(HA - 1)
        pe.wait_ge(sem("head_gated"), HA)
        banks[0] = 4
        project_back(0, so[:, DC:, :])
        norm(0)
        peer(0)
        norm(1)
        project_x(2, 2)
        for u in range(2):
            w_set = 2 * (n_split(unit[0]) % 2)
            for half in range(2):
                pe.wait_ge(low_done["pool"], 2 * _before(unit[0], "pool") + half + 1)
                for k in range(2):
                    kk = 4 * u + 2 * half + k
                    w = slice(k * 256, (k + 1) * 256)
                    for out, tokens in ((pb[:, 0, 0:256], slice(0, P)), (pb[:, 1, 0:256], slice(P, TP)),
                                        (pb[0:NSM, 2, 0:256], slice(TP, T))):
                        mm(out, xh[:, kk, tokens], split[:, w_set + half, 0, w], kk == 0, False)
                        mm(out, xl[:, kk, tokens], split[:, w_set + half, 0, w], False, False)
                        last = mm(out, xh[:, kk, tokens], split[:, w_set + half, 1, w], False, kk == DC - 1)
                last.then_inc(halves_used, 1)
            unit[0] += 1
        project_x(DC, None)
        pe.wait_ge(evacuated, group[0])
        pe.wait_ge(sem("vb_kept"), 1)

        groups = [(blk, g4) for blk in range(2) for g4 in range(4)]

        def att_scores(i):
            blk, g4 = groups[i]
            if i >= 2:
                pe.wait_ge(sem("att_scored"), i - 1)
            for e in range(4):
                half, c = e // 2, 2 * g4 + e % 2
                r = slice(half * HD, (half + 1) * HD)
                nk = P * (blk + 1)
                last = mm(pa[:, 2 * (i % 2) + e // 2, (e % 2) * 256:(e % 2) * 256 + nk],
                          qb[r, c, blk * P:(blk + 1) * P], ktb[r, c // 4, 0:nk])
            last.then_inc(sem("att_scores"), 1)

        def att_turn(i):
            nb = groups[i][0] + 1
            pe.wait_ge(sem("att_probs"), i + 1)
            if i >= 1:
                pe.wait_ge(sem("att_turned_kept"), i)
            for e in range(4):
                for s in range(nb):
                    last = pe.transpose(turned_at(i)[:, e, s, :], ss[:, i % 3, e, s * P:(s + 1) * P], ident)
            last.then_inc(sem("att_turned"), 1)

        def att_values(i):
            blk, g4 = groups[i]
            pe.wait_ge(sem("att_turned_kept"), i + 1)
            if i >= 2:
                pe.wait_ge(sem("att_out_kept"), i - 1)
            for e in range(4):
                half, c = e // 2, 2 * g4 + e % 2
                g = 2 * (c // 4) + half
                for s in range(blk + 1):
                    last = mm(pb[half * HD:(half + 1) * HD, 2 + i % 2, (e % 2) * P:(e % 2 + 1) * P],
                              vnb[:, s, g * HD:(g + 1) * HD], pt[:, i % 2, e, s, :], s == 0, s == blk)
            last.then_inc(sem("att_out"), 1)

        def sample_scores():
            pe.wait_ge(sem("q_spread"), 1)
            pe.wait_ge(sem("window_ready"), 1)
            for b in range(NSM):
                for G in range(2):
                    last = mm(pb[:, 1, 0:WINDOW], qbd[:, b, G, :], kw[:, G, b, :], b == 0 and G == 0,
                              b == NSM - 1 and G == 1)
            last.then_inc(sem("att_s_scores"), 1)

        def sample_values():
            pe.wait_ge(sem("att_s_kept"), 1)
            pe.wait_ge(sem("vw_in"), 32)
            for b in range(NSM):
                for G in range(2):
                    o = 256 + (b * 2 + G) * 8
                    last = mm(pb[:, 1, o:o + 8], vw[:, b, G * P:(G + 1) * P],
                              pt_s[:, b * 16 + G * 8:b * 16 + G * 8 + 8])
            last.then_inc(sem("att_s_out"), 1)

        att_scores(0)
        att_scores(1)
        sample_scores()
        for i in range(8):
            if i + 2 < 8:
                att_scores(i + 2)
            if i == 4:
                pe.wait_ge(sem("att_s_done"), 1)
            att_turn(i)
            if i:
                att_values(i - 1)
            if i == 1:
                pe.wait_ge(sem("att_s_probs"), 1)
                pe.transpose(pb[:, 1, 128:256], ss_s, ident).then_inc(sem("att_s_turned"), 1)
            if i == 2:
                sample_values()
        att_values(7)
        pe.wait_ge(sem("att_out_kept"), 8)
        project_back(2, ot)
        norm(2)
        peer(1)
        norm(3)

    @block.scalar
    def _(act):
        group = [0]
        chain = [0]
        banks = [4]

        def link(ins):
            chain[0] += 1
            ins.then_inc(sem("act_chain"), 1)
            act.wait_ge(sem("act_chain"), chain[0])

        def bank(units):
            kind = [k for k, a, b in PHASES if a < units <= b][0]
            if kind == "pe":
                act.wait_ge(units_used, _before(units, "pe"))
            else:
                act.wait_ge(halves_used, 2 * n_split(units))
            group[0] += 1
            return pa[:, (group[0] - 1) % banks[0], 0:T]

        def high(slot, n, count, landed_count, used_count=None):
            act.wait_ge(landed[slot], landed_count)
            for half in range(2):
                if used_count is not None:
                    act.wait_ge(halves_used, used_count + half)
                nc.scalar.copy(split[:, 2 * (n % 2) + half, 0, :], ring[:, slot, half * 512:(half + 1) * 512]).then_inc(
                    high_done, 1)

        def high_at(u):
            n = n_split(u)
            high(u % RING, n, 0, 16 * (u // RING + 1), 2 * n - 3 if n >= 2 else None)

        def high_loop(it, u):
            n = n_split(u)
            high(u % RING, n, 0, it * 16 + 16 * (u // RING + 1), it * (2 * RING) + (2 * n - 3))

        def store_y(half):
            cc = slice(half * DC // 2, (half + 1) * DC // 2)
            act.wait_ge(sem("x_full"), 3 * DC + cc.stop)
            act.dma_start(io["y"][:, cc, :], x[:, cc, :]).then_inc(sem("y_out"), 16)

        def norm(li):
            for c in range(DC):
                act.wait_ge(sem("ln_centred"), DC * li + c + 1)
                nc.scalar.activation(sq[:, c, :], x[:, c, :], ACT.Square).then_inc(sem("ln_square"), 1)
            act.wait_ge(sem("ln_var"), li + 1)
            nc.scalar.activation(rstd, sum_bank(li, 1), ACT.Sqrt, bias=col("eps", 0), scale=1.0 / D).then_inc(
                sem("ln_std"), 1)
            for c in range(DC):
                act.wait_ge(sem("ln_scaled"), DC * li + c + 1)
                nc.scalar.activation(x[:, c, :], x[:, c, :], ACT.Identity, bias=col(NORMS[li][1], li // 2 * DC + c),
                                     scale=col(NORMS[li][0], li // 2 * DC + c)).then_inc(sem("x_full"), 1)
                if c and li < 3:
                    x_high(li + 1, c - 1)
                if c == DC // 2 - 1 and li == 3:
                    store_y(0)
            if li < 3:
                x_high(li + 1, DC - 1)

        def x_high(n, c):
            if n:
                act.wait_ge(sem("x_full"), DC * (n - 1) + c + 1)
            nc.scalar.copy(xh[:, c, :], x[:, c, :]).then_inc(sem("x_high"), 1)

        def peer(L):
            act.wait_ge(sem("skeys_in"), 16 * (L + 1))
            for h in range(2 * PH):
                src = bank(U_PQ[L] + h + 1)
                high_at(U_PQ[L] + h + 2)
                nc.scalar.copy(pq[:, h, :], src).then_inc(evacuated, 1)
            g0 = group[0]

            def u_row(it, i, first=False):
                high_loop(it, U_U[L] + i + 2)
                if i >= SPREAD_AT and not first:
                    act.wait_ge(sem("row_gated"), it * RING + (n_r + i - SPREAD_AT - 3))
                act.wait_ge(halves_used, it * (2 * RING) + 2 * n_split(U_U[L] + i + 1))
                out = gelu[:, i % RING, :] if i >= SPREAD_AT else big[:, bass.ds(it * (4 * T) + i * T, T)]
                nc.scalar.activation(out, pa[:, (g0 + i) % 4, 0:T], ACT.Gelu).then_inc(evacuated, 1)

            n_r = (NK - SPREAD_AT) * L
            for a in range(2):
                act.wait_ge(sem("scores_done"), 3 * L + a + 1)
                nc.scalar.copy(score_of[a].rearrange("p h n -> p (h n)"),
                               pb[:, :, :].rearrange("p b n -> p (b n)")).then_inc(sem("scores_copied"), 1)
                u_row(0, a)
            act.wait_ge(sem("scores_done"), 3 * L + 3)
            ones_t = ones[:, 0:T // 3].rearrange("p (o n) -> p o n", o=1).to_broadcast([P, 3, T // 3])

            def ones_row(it, k):
                row = big[:, bass.ds(it * (4 * T) + (SPREAD_AT + k) * T, T)]
                nc.scalar.copy(row.rearrange("p (o n) -> p o n", o=3), ones_t).then_inc(sem("ones_written"), 1)

            for k in range(RING):
                if k >= 2:
                    u_row(0, k)
                ones_row(0, k)
            with act.Fori(1, EXP_AT // RING) as it:
                for k in range(RING):
                    u_row(it, k)
                    ones_row(it, k)
            act.wait_ge(sem("best_shifted"), L + 1)
            for a, (t0, n) in enumerate(TILES):
                v = best_s[0:n, a].rearrange("p h k -> p (h k)")
                last = nc.scalar.activation(v, v, ACT.Exp)
            last.then_inc(sem("best_exp"), 1)
            for i in range(EXP_AT, SPREAD_AT):
                u_row(0, i)
            act.wait_ge(sem("choice_kept"), L + 1)
            for k in range(RING):
                u_row(0, SPREAD_AT + k, first=(L == 0))
            with act.Fori(1, (NK - SPREAD_AT) // RING) as it:
                for k in range(RING):
                    u_row(it, SPREAD_AT + k)
            group[0] += NK
            act.wait_ge(sem("row_gated"), n_r + NK - SPREAD_AT)
            act.wait_ge(sem("gates_applied"), SETS * (L + 1))
            n0 = n_split(U_V[L])

            def w_high(it, i):
                if it is not None:
                    act.wait_ge(halves_used, it * (2 * RING) + 2 * (n0 + i - 3))
                nc.scalar.copy(wsplit[:, i % 4, 0, :], big[:, bass.ds(it * (4 * T) + i * T, T)] if it is not None
                               else w3[:, i, :]).then_inc(sem("w_high"), 1)

            w_high(None, 0)
            w_high(None, 1)
            for k in range(RING):
                high_at(U_V[L] + k + 2)
                w_high(None if k < 2 else 0, k + 2)
            with act.Fori(1, NK // RING - 1) as it:
                for k in range(RING):
                    high_loop(it, U_V[L] + k + 2)
                    w_high(it, k + 2)
            for k in range(2):
                high_at(U_V[L] + NK - RING + k + 2)
                w_high(NK // RING - 1, k + 2)

        high_at(U_IN)
        act.wait_ge(sem("x_in"), 16)
        for c in range(DC):
            x_high(0, c)
        high_at(U_IN + 1)
        def gates():
            act.wait_ge(sem("gate_in"), 80)
            act.wait_ge(sem("gate_pre"), 1)
            nc.scalar.activation(rows[0:HA, 0, 0:T], pb[0:HA, 0, 0:T], ACT.Identity, bias=b_rows[0:HA, 0:1]).then_inc(
                sem("gate_i"), 1)
            link(nc.scalar.activation(rows[0:HA, 1, 0:T], pb[0:HA, 1, 0:T], ACT.Identity, bias=b_rows[0:HA, 1:2]))
            link(nc.scalar.activation(rows[0:HA, 2, 0:T], rows[0:HA, 1, 0:T], ACT.Abs))
            link(nc.scalar.activation(rows[0:HA, 2, 0:T], rows[0:HA, 2, 0:T], ACT.Exp, scale=-1.0))
            nc.scalar.activation(rows[0:HA, 2, 0:T], rows[0:HA, 2, 0:T], ACT.Ln, bias=1.0).then_inc(sem("gate_soft"), 1)

        def gate_exps():
            act.wait_ge(sem("gate_scanned"), 1)
            nc.scalar.activation(rows[0:HA, 6, 0:T], rows[0:HA, 6, 0:T], ACT.Exp, scale=-1.0)
            nc.scalar.activation(em_row[0:HA], em_row[0:HA], ACT.Exp, scale=-1.0)
            nc.scalar.activation(rows[0:HA, 7, :], rows[0:HA, 7, :], ACT.Exp).then_inc(sem("gate_exps"), 1)

        act.wait_ge(sem("cols_in"), 32)

        def silu(c):
            act.wait_ge(sem("conv_summed"), c + 1)
            acc = conv_acc[:, c % 2, :]
            nc.scalar.activation(xc[:, c, 0:TP], acc[:, 0:TP], ACT.Silu, bias=col_a("conv_b", c))
            nc.scalar.activation(xc[:, c, TP:T], acc[:, TP + 3:XPW - 3:4], ACT.Silu,
                                 bias=col_a("conv_b", c)).then_inc(sem("conv_done"), 1)

        for c in range(IC):
            src = bank(U_IN + c + 1)
            high_at(U_IN + c + 2)
            b = col_a("b_in", c)
            nc.scalar.activation(xp[:, c, 3:3 + TP], src[:, 0:TP], ACT.Identity, bias=b)
            nc.scalar.activation(xp[:, c, TP + 6:XPW:4], src[:, TP:T], ACT.Identity, bias=b).then_inc(evacuated, 1)
            if c == 1:
                gates()
            elif c == 4:
                gate_exps()
            if c >= 3:
                silu(c - 3)
        for c in range(IC - 3, IC):
            silu(c)
        for c in range(IC):
            src = bank(U_IN + IC + c + 1)
            if c < IC - 2:
                high_at(U_IN + IC + c + 2)
            nc.scalar.activation(so[:, c, :], src, ACT.Sigmoid, bias=col_a("b_in", IC + c)).then_inc(evacuated, 1)

        banks[0] = 2

        def keep_qk(h, u):
            if h >= 2 and u == 0:
                act.wait_ge(sem("k_turned"), h - 1)
                act.wait_ge(sem("sample_ready"), h - 1)
            dst, scale = ((qt, 1.0), (kt, DH ** -0.5))[u // 2]
            for m in range(2):
                src = bank(U_QKV + 6 * h + u + 1)
                nc.scalar.mul(dst[:, h % 2, 2 * (u % 2) + m, :], src, scale).then_inc(evacuated, 1)

        def keep_v(h):
            if h >= 2:
                act.wait_ge(sem("v_spread"), NSM * (h - 1))
            act.wait_ge(units_used, _before(U_QKV + 6 * (h + 1), "pe"))
            for s in range(2):
                nc.scalar.copy(vn[:, h % 2, s, :], pb[:, s, :])
            nc.scalar.copy(vs[0:NSM, h % 2, :], pb[0:NSM, 2, :]).then_inc(sem("v_kept"), 1)

        def decay(h, b):
            n = NSM * h + b
            h, b = n // NSM, n % NSM
            if h < HA:
                act.wait_ge(sem(f"state_in_{n % SLOTS}"), 16 * (n // SLOTS + 1))
                v = state(n)
                nc.scalar.mul(v, v, sg[:, h, NSM + b:NSM + b + 1]).then_inc(sem("state_decayed"), 1)

        for u in range(4):
            keep_qk(0, u)
        act.wait_ge(sem("gate_cols_kept"), 1)
        decay(0, 0)
        keep_v(0)
        for h in range(HA):
            act.wait_ge(sem("decay_arg"), h + 1)
            nc.scalar.activation(p0, p0, ACT.Exp)
            nc.scalar.activation(p1, p1, ACT.Exp).then_inc(sem("decay_exp"), 1)
            act.wait_ge(sem("den_s_done"), h + 1)
            nc.scalar.activation(den_s[:, 0:1], pa[:, 2, 4:5], ACT.Abs).then_inc(sem("den_s_kept"), 1)
            decay(h, 1)
            act.wait_ge(sem("den_done"), h + 1)
            if h:
                act.wait_ge(sem("num_used"), h)
            nc.scalar.activation(den, pb[:, 3, 0:TP], ACT.Abs).then_inc(sem("den_kept"), 1)
            decay(h, 2)
            if h:
                act.wait_ge(sem("c_stored"), 16 * h)
            for c in range(HC):
                act.wait_ge(sem("c_done"), HC * h + c + 1)
                nc.scalar.copy(c_out[:, c, :], pb[:, 2 + c % 2, :]).then_inc(sem("c_kept"), 1)
            act.wait_ge(sem("n_done"), h + 1)
            nc.scalar.copy(n_prompt[:, h, :], pb[:, 0, 0:HC]).then_inc(sem("n_kept"), 1)
            out = 0
            for b in range(2, NSM):
                decay(h, b + 1)
                if h == HA - 1:
                    for _ in range(2 if b < 4 else 1):
                        src = bank(U_OUT + out + 1)
                        nc.scalar.copy(sq[:, out, :], src).then_inc(evacuated, 1)
                        out += 1
                elif b < 6:
                    keep_qk(h + 1, b - 2)
            if h < HA - 1:
                keep_v(h + 1)
        banks[0] = 4
        for k in range(3, SLOTS):
            act.wait_ge(sem(f"state_out_{k}"), 16 * ((NSM * HA - k + SLOTS - 1) // SLOTS))
        high_at(U_PQ[0])
        high_at(U_PQ[0] + 1)
        norm(0)
        peer(0)
        high_at(U_KV)
        high_at(U_KV + 1)
        norm(1)
        for c in range(2):
            src = bank(U_KV + c + 1)
            high_at(U_KV + c + 2)
            nc.scalar.copy(ktb[:, c, :], src).then_inc(evacuated, 1)
        high_at(U_BQ)
        high_at(U_BQ + 1)
        act.wait_ge(halves_used, 2 * n_split(U_BQ))
        for s in range(2):
            nc.scalar.copy(vnb[:, s, :], pb[:, s, 0:256])
        nc.scalar.copy(vsb[0:NSM, :], pb[0:NSM, 2, 0:256]).then_inc(sem("vb_kept"), 1)
        for c in range(DC):
            src = bank(U_BQ + c + 1)
            if c < DC - 2:
                high_at(U_BQ + c + 2)
            nc.scalar.copy(qb[:, c, :], src).then_inc(evacuated, 1)

        def att_exp(i):
            act.wait_ge(sem("att_shifted"), i + 1)
            for e in range(4):
                v = ss[:, i % 3, e, 0:P * (1 + i // 4)]
                nc.scalar.activation(v, v, ACT.Exp, bias=neg_mx[:, i % 2, e:e + 1])
            nc.scalar.activation(dx[:, i % 2, :], dx[:, i % 2, :], ACT.Exp).then_inc(sem("att_exp"), 1)

        att_exp(0)
        for i in range(8):
            if i + 1 < 8:
                att_exp(i + 1)
            if i == 0:
                act.wait_ge(sem("att_s_shifted"), 1)
                nc.scalar.activation(ss_s, ss_s, ACT.Exp)
                nc.scalar.activation(small_s[:, 1:2], small_s[:, 1:2], ACT.Exp).then_inc(sem("att_s_exp"), 1)
            act.wait_ge(sem("att_turned"), i + 1)
            if i >= 2:
                act.wait_ge(sem("att_out"), i - 1)
            nc.scalar.copy(pt[:, i % 2, :, 0:i // 4 + 1, :], turned_at(i)).then_inc(sem("att_turned_kept"), 1)
        high_at(U_PQ[1])
        high_at(U_PQ[1] + 1)
        norm(2)
        peer(1)
        norm(3)
        store_y(1)
        act.wait_ge(sem("y_out"), 32)

    @block.vector
    def _(dve):
        V = nc.vector
        chain = [0]

        def link(ins):
            chain[0] += 1
            ins.then_inc(sem("dve_chain"), 1)
            dve.wait_ge(sem("dve_chain"), chain[0])

        def residual(norms):
            dve.wait_ge(sem("x_ready"), DC * (norms + 1))
            link(V.tensor_scalar(res, xh_f, ALPHA, None, ALU.mult))
            link(V.scalar_tensor_tensor(res, xl_f, ALPHA, res, ALU.mult, ALU.add))

        def norm(li, units=None):
            for c in range(DC):
                if units is not None:
                    dve.wait_ge(units_used, _before(units + c + 1, "pe"))
                out = pa[:, c % 4, 0:T] if units is not None or c < 4 else pb[:, c % 4, 0:T]
                V.tensor_tensor(x[:, c, :], out, res[:, c, :], ALU.add).then_inc(sem("ln_sum"), 1)
            dve.wait_ge(sem("ln_sum"), DC * (li + 1))
            dve.wait_ge(sem("ln_mean"), li + 1)
            for c in range(DC):
                V.scalar_tensor_tensor(x[:, c, :], sum_bank(li, 0), -1.0 / D, x[:, c, :], ALU.mult,
                                       ALU.add).then_inc(sem("ln_centred"), 1)
            dve.wait_ge(sem("ln_centred"), DC * (li + 1))
            dve.wait_ge(sem("ln_std"), li + 1)
            link(V.reciprocal(rstd, rstd))
            for c in range(DC):
                V.tensor_tensor(x[:, c, :], x[:, c, :], rstd, ALU.mult).then_inc(sem("ln_scaled"), 1)
                if c >= 3 and li < 3:
                    x_low(li + 1, c - 3)
            for c in range(DC - 3, DC):
                if li < 3:
                    x_low(li + 1, c)

        def x_low(n, c):
            dve.wait_ge(sem("x_high"), DC * n + c + 1)
            V.tensor_tensor(xl[:, c, :], x[:, c, :], xh_f[:, c, :], ALU.subtract).then_inc(sem("x_ready"), 1)

        def low(slot, n, count):
            for half in range(2):
                o = slice(half * 512, (half + 1) * 512)
                dve.wait_ge(high_done, count + half)
                V.tensor_tensor(split[:, 2 * (n % 2) + half, 1, :], ring[:, slot, o],
                                split_f[:, 2 * (n % 2) + half, 0, :], ALU.subtract).then_inc(low_done["dve"], 1)

        def top16(vals, outs, idx, n):
            for step in range(2):
                o = slice(8 * step, 8 * step + 8)
                for v, s in zip(vals, outs):
                    last = V.max(s[:, o], v)
                link(last)
                for v, s, i in zip(vals, outs, idx):
                    last = V.max_index(i[:, o], s[:, o], v)
                if step == 0:
                    for v, s in zip(vals, outs):
                        last = V.match_replace(v, s[:, o], v, LOWEST)
                link(last)

        def choose(L, a, n):
            if a < 2:
                dve.wait_ge(sem("scores_copied"), 2 * L + a + 1)
            else:
                dve.wait_ge(sem("scores_done"), 3 * L + 3)
            sc = score_of[a][0:n]
            top16([sc[:, h] for h in range(2 * PH)], [top_s[0:n, h] for h in range(2 * PH)],
                  [top_iu[0:n, h] for h in range(2 * PH)], n)
            ts = top_s[0:n].rearrange("p (h two) k -> p h two k", two=2)
            cand = sc.rearrange("p (h two) (b c) -> p h (two b) c", two=2, c=TOPK)
            for h in range(PH):
                last = V.tensor_tensor(cand[:, h], ts[:, h, 0, :].rearrange("p (k o) -> p k o", o=1).to_broadcast(
                    [n, TOPK, TOPK]), ts[:, h, 1:2, :].to_broadcast([n, TOPK, TOPK]), ALU.add)
            link(last)
            link(V.tensor_copy(top_if[0:n], top_iu[0:n]))
            flat = sc.rearrange("p (h two) c -> p h (two c)", two=2)
            bs = best_s[0:n, a]
            top16([flat[:, h] for h in range(PH)], [bs[:, h] for h in range(PH)],
                  [best_u[0:n, h] for h in range(PH)], n)
            heads, room = (2, tmp) if a == 0 else (PH, scb)
            flat_eq = room[0:n, 0:heads * TOPK * TOPK]
            eq = flat_eq.rearrange("p (k r) -> p k r", r=TOPK)
            eq_h = flat_eq.rearrange("p (h k r) -> p h k r", h=heads, r=TOPK)
            nk = heads * TOPK
            i16 = iota[0:n, 0:TOPK].rearrange("p (o k) -> p o k", o=1).to_broadcast([n, nk, TOPK])
            tf = top_if[0:n].rearrange("p (h two) k -> p h two k", two=2)
            for half, (dst, op, arg) in enumerate(((sel_i, ALU.logical_shift_right, 4), (sel_j, ALU.bitwise_and, 15))):
                link(V.tensor_scalar(rank_u[0:n], best_u[0:n], arg, None, op))
                link(V.tensor_copy(rank_f[0:n], rank_u[0:n]))
                for hq in range(0, PH, heads):
                    rank = rank_f[0:n, hq:hq + heads, :].rearrange("p h (k o) -> p (h k) o", o=1)
                    link(V.tensor_tensor(eq, rank.to_broadcast([n, nk, TOPK]), i16, ALU.is_equal))
                    link(V.tensor_tensor(eq_h, eq_h, tf[:, hq:hq + heads, half:half + 1, :].to_broadcast(
                        [n, heads, TOPK, TOPK]), ALU.mult))
                    link(V.tensor_reduce(dst[0:n, a, TOPK * hq:TOPK * (hq + heads)], eq, AX.X, ALU.add))
            V.tensor_copy(gsum[0:n, a, :], bs[:, :, 0])
            link(V.engine_nop())
            link(V.tensor_tensor(bs, bs, gsum[0:n, a, :].rearrange("p (h o) -> p h o", o=1).to_broadcast(
                [n, PH, TOPK]), ALU.subtract))

        def peer(L):
            choose(L, 0, P)
            dve.wait_ge(sem("scores_done"), 3 * L + 3)
            V.memset(w3[:, SPREAD_AT + EXP_AT:, :], 1.0)
            choose(L, 1, P)
            choose(L, 2, NSM)
            V.engine_nop().then_inc(sem("best_shifted"), 1)
            dve.wait_ge(sem("best_exp"), L + 1)
            for a, (t0, n) in enumerate(TILES):
                last = V.tensor_reduce(gsum[0:n, a, :], best_s[0:n, a], AX.X, ALU.add)
            link(last)
            for a, (t0, n) in enumerate(TILES):
                last = V.reciprocal(gsum[0:n, a, :], gsum[0:n, a, :])
            link(last)
            for a, (t0, n) in enumerate(TILES):
                last = V.tensor_tensor(best_s[0:n, a], best_s[0:n, a], gsum[0:n, a, :].rearrange(
                    "p (h o) -> p h o", o=1).to_broadcast([n, PH, TOPK]), ALU.mult)
            last.then_inc(sem("gates_done"), 1)
            dve.wait_ge(sem("choice_turned"), L + 1)
            V.tensor_copy(turned[:, :, :], pb[:, 0:3, 0:T]).then_inc(sem("choice_kept"), 1)
            dve.wait_ge(sem("choice_kept"), L + 1)

            def one_hots(it, s):
                for t in range(8):
                    c = it * 16 + (8 * s + t)
                    i_col, j_col, g_col = (turned[:, r, bass.ds(c, 1)] for r in range(3))
                    V.tensor_scalar(hot[:, s % 2, 1, t, :], iota, j_col, None, ALU.is_equal)
                    last = V.tensor_scalar(hot[:, s % 2, 0, t, :], iota, i_col, g_col, ALU.is_equal, ALU.mult)
                last.then_inc(sem("hot"), 1)

            def apply(it, s):
                dve.wait_ge(sem("gates_spread"), it * 2 + (n0 + s + 1))
                w = w3[:, :, bass.ds(it * 16 + 8 * s, 8)]
                g = gate_bank(s % 2).rearrange("p b (t i) -> p i (b t)", t=4)
                V.tensor_tensor(w, w, g, ALU.mult).then_inc(sem("gates_applied"), 1)

            def take_row(it, i, sets):
                dve.wait_ge(evacuated, it * RING + (peer_groups[L] - NK + i + 1))
                dve.wait_ge(sem("gates_applied"), sets)
                w = big[:, bass.ds(it * (4 * T) + i * T, T)]
                V.tensor_tensor(w, w, gelu[:, i % RING, :], ALU.mult).then_inc(sem("row_gated"), 1)

            n0 = SETS * L
            n_r = (NK - SPREAD_AT) * L
            dve.wait_ge(sem("ones_written"), EXP_AT * (L + 1))
            one_hots(0, 0)
            one_hots(0, 1)
            for s in range(2):
                dve.wait_ge(evacuated, peer_groups[L] - NK + SPREAD_AT + 2 * s)
                if s:
                    dve.wait_ge(sem("row_gated"), n_r + 2)
                apply(0, s)
                if s == 0:
                    one_hots(0, 2)
                for k in range(2):
                    take_row(0, SPREAD_AT + 2 * s + k, n0 + s + 1)
            with dve.Fori(1, SETS // 2) as it:
                for s in range(2):
                    dve.wait_ge(sem("gates_spread"), it * 2 + (n0 + s))
                    one_hots(it, s + 1)
                    dve.wait_ge(sem("row_gated"), it * RING + (n_r + 2 * s))
                    apply(it, s)
                    for k in range(2):
                        take_row(it, SPREAD_AT + 2 * s + k, it * 2 + (n0 + s + 1))
            nv = n_split(U_V[L])
            low(U_V[L] % RING, nv, 2 * nv + 1)
            dve.wait_ge(sem("row_gated"), n_r + SPREAD_TO - SPREAD_AT)
            apply(0, SETS - 1)
            for i in range(SPREAD_TO, NK):
                take_row(0, i, n0 + SETS)
            n_w = NK * L

            def w_low(it, i):
                dve.wait_ge(sem("w_high"), it * RING + (n_w + i + 1))
                V.tensor_tensor(wsplit[:, i % 4, 1, :], big[:, bass.ds(it * (4 * T) + i * T, T)],
                                wsplit_f[:, i % 4, 0, :], ALU.subtract).then_inc(sem("w_low"), 1)

            w_low(0, 0)
            low((U_V[L] + 1) % RING, nv + 1, 2 * (nv + 1) + 1)
            w_low(0, 1)
            with dve.Fori(0, NK // RING - 1) as it:
                for k in range(RING):
                    u = nv + k + 2
                    low((U_V[L] + k + 2) % RING, u, it * (2 * RING) + (2 * u + 1))
                    w_low(it, k + 2)
            for k in range(2):
                u = nv + NK - RING + k + 2
                low((U_V[L] + k + 2) % RING, u, 2 * u + 1)
                w_low(NK // RING - 1, k + 2)
            residual(2 * L + 1)
            dve.wait_ge(halves_used, 2 * (nv + NK))

        dve.wait_ge(sem("x_in"), 16)
        for c in range(DC):
            x_low(0, c)
        V.memset(em_row[0:HA], 0.0)
        link(V.memset(rt[0:HB, :], NEG))
        V.memset(qm, 0.0)
        V.memset(qn, 0.0)
        V.memset(xp[:, :, 0:3], 0.0)
        dve.wait_ge(sem("conv_in"), 16)
        link(V.tensor_copy(xp[:, :, 3 + TP:XPW].rearrange("p c (b w) -> p c b w", w=4)[:, :, :, 0:3], conv_in))
        dve.wait_ge(sem("gate_soft"), 1)
        R = rows[0:HA]
        r = lambda i, a=0, b=T: R[:, i, a:b]
        link(V.scalar_tensor_tensor(r(1), r(1), 0.0, r(2), ALU.min, ALU.subtract))
        link(V.memset(r(5), 1.0))
        link(V.tensor_tensor_scan(r(3, 0, TP), r(5, 0, TP), r(1, 0, TP), 0.0, ALU.mult, ALU.add))
        link(V.tensor_tensor(r(4, 0, TP), r(0, 0, TP), r(3, 0, TP), ALU.subtract))
        link(V.tensor_tensor_scan(r(2, 0, TP), r(5, 0, TP), r(4, 0, TP), 0.0, ALU.mult, ALU.max))
        V.tensor_scalar(r(5, 0, TP), r(2, 0, TP), -1.0, None, ALU.mult)
        V.tensor_tensor(r(6, 0, TP), r(3, 0, TP), r(2, 0, TP), ALU.add)
        V.tensor_scalar(r(7, 0, TP), r(4, 0, TP), r(2, TP - 1, TP), None, ALU.subtract)
        link(V.tensor_tensor(r(3, TP, T), r(1, TP, T), m_in[0:HA, :], ALU.add))
        link(V.tensor_tensor(r(6, TP, T), r(3, TP, T), r(0, TP, T), ALU.max))
        V.tensor_tensor(r(7, TP, T), r(0, TP, T), r(6, TP, T), ALU.subtract)
        V.tensor_copy(em_row[0:HA, :, 0:NSM], R[:, 6:7, TP:T].to_broadcast([HA, 4, NSM]))
        V.tensor_copy(m_out[0:HA, 0:1], r(6, TP - 1, TP))
        V.tensor_copy(m_out[0:HA, 1:1 + NSM], r(6, TP, T)).then_inc(sem("m_kept"), 1)
        V.tensor_tensor(r(7, T, T + NSM), r(3, TP, T), r(6, TP, T), ALU.subtract).then_inc(sem("gate_scanned"), 1)
        dve.wait_ge(sem("cols_in"), 32)
        N = XPW - 3
        for c in range(IC):
            acc = conv_acc[:, c % 2, :]
            dve.wait_ge(evacuated, c + 1)
            if c >= 2:
                dve.wait_ge(sem("conv_done"), c - 1)
            link(V.tensor_scalar(acc, xp[:, c, 3:3 + N], col_a("conv_w", 3 * IC + c), None, ALU.mult))
            for w in (2, 1, 0):
                ins = V.scalar_tensor_tensor(acc, xp[:, c, w:w + N], col_a("conv_w", w * IC + c), acc,
                                             ALU.mult, ALU.add)
                if w:
                    link(ins)
            ins.then_inc(sem("conv_summed"), 1)
        V.tensor_copy(conv_out[:, :, 0:3], xp[:, :, TP:TP + 3])
        V.tensor_copy(conv_out[:, :, 3:].rearrange("p c (b w) -> p c b w", w=3),
                      xp[:, :, 3 + TP:XPW].rearrange("p c (b w) -> p c b w", w=4)[:, :, :, 1:4]).then_inc(
            sem("conv_kept"), 1)
        dve.wait_ge(sem("bias_rows"), 1)
        V.tensor_copy(rt[0:HB, WINDOW:2 * WINDOW], pb[0:HB, 0, 0:WINDOW]).then_inc(sem("bias_rows_kept"), 1)
        dve.wait_ge(sem("gate_cols"), 1)
        V.tensor_copy(gcol, pb[:, 2, 0:16])
        V.tensor_copy(em_s, pb[:, 2, 16:20])
        link(V.tensor_copy(sg.rearrange("p h n -> p (h n)"), pb[:, 3, 0:64]))
        V.engine_nop().then_inc(sem("gate_cols_kept"), 1)

        def update(h, b):
            n = NSM * h + b
            dve.wait_ge(sem("v_spread"), n + 1)
            dve.wait_ge(sem("state_decayed"), n + 1)
            for c in range(HC):
                st = state(n)[:, c, :]
                last = V.scalar_tensor_tensor(st, pa[:, 2, :], kws[:, c, b:b + 1], st, ALU.mult, ALU.add)
            last.then_inc(sem("state_new"), 1)

        def gate_sample(h):
            dve.wait_ge(sem("head_done"), h + 1)
            sov = so[:, h * HC:(h + 1) * HC, TP:T]
            V.tensor_tensor(sov, sov, pa[:, 2, 8:8 + HC * NSM].rearrange("p (c b) -> p c b", b=NSM),
                            ALU.mult).then_inc(sem("head_gated"), 1)

        for h in range(HA):
            q, k = qt[:, h % 2], kt[:, h % 2]
            if h:
                gate_sample(h - 1)
            dve.wait_ge(sem("rows_spread"), h + 1)
            V.tensor_copy(em, pb[:, 3, TP:2 * TP])
            V.tensor_scalar(p0, pb[:, 3, 0:TP], gcol[:, h:h + 1], 0.0, ALU.add, ALU.min)
            V.tensor_scalar(p1, pb[:, 3, P:TP], gcol[:, HA + h:HA + h + 1], 0.0, ALU.add, ALU.min).then_inc(
                sem("decay_arg"), 1)
            dve.wait_ge(evacuated, 2 * IC + 8 * (h + 1))
            if h == 0:
                dve.wait_ge(sem("state_n_in"), 16)
            ws = sg[:, h, 0:NSM].rearrange("p (o b) -> p o b", o=1).to_broadcast([P, HC, NSM])
            wd = sg[:, h, NSM:2 * NSM].rearrange("p (o b) -> p o b", o=1).to_broadcast([P, HC, NSM])
            V.tensor_tensor(kws, k[:, :, TP:T], ws, ALU.mult)
            for c in range(HC):
                V.tensor_copy(qm[:, c].rearrange("p a b -> p (a b)")[:, 0:NSM * 33 - 32:33], q[:, c, TP:T])
            link(V.tensor_tensor(n_new[:, h], n_in[:, h], wd, ALU.mult))
            link(V.tensor_tensor(n_new[:, h], n_new[:, h], kws, ALU.add))
            for a in range(4):
                last = V.tensor_tensor(qn[:, :, a, 0:NSM], q[:, :, TP:T], n_new[:, h], ALU.mult)
            last.then_inc(sem("sample_ready"), 1)
            dve.wait_ge(sem("decay_exp"), h + 1)
            dve.wait_ge(sem("scores_t"), h + 1)
            V.tensor_tensor(p0[:, 0:P], p0[:, 0:P], causal, ALU.mult)
            link(V.tensor_tensor(p1, p1, causal, ALU.mult))
            V.tensor_tensor(p0, p0, pb[:, 2, 0:TP], ALU.mult)
            V.tensor_tensor(p1, p1, pb[:, 2, TP:TP + P], ALU.mult).then_inc(sem("weights_t"), 1)
            dve.wait_ge(sem("k_turned"), h + 1)
            for s in range(2):
                last = V.tensor_scalar(wk[:, s, :], pb[:, s, :], gcol[:, 8 + HA * s + h:9 + HA * s + h], None, ALU.mult)
            last.then_inc(sem("k_weighted"), 1)
            update(h, 0)
            update(h, 1)
            dve.wait_ge(sem("den_kept"), h + 1)
            link(V.tensor_tensor(den, den, em, ALU.max))
            link(V.reciprocal(den, den))
            dve.wait_ge(sem("num_done"), h + 1)
            link(V.tensor_tensor(hn, pb[:, 0:2, :].rearrange("p b (c t) -> p (b c) t", t=TP),
                                 den.rearrange("p (o t) -> p o t", o=1).to_broadcast([P, HC, TP]), ALU.mult))
            sov = so[:, h * HC:(h + 1) * HC, 0:TP]
            V.tensor_tensor(sov, sov, hn, ALU.mult).then_inc(sem("num_used"), 1)
            for b in range(2, NSM):
                update(h, b)
            link(V.tensor_tensor(den_s[:, 0:1], den_s[:, 0:1], em_s[:, h:h + 1], ALU.max))
            link(V.reciprocal(den_s[:, 1:2], den_s[:, 0:1]))
            dve.wait_ge(sem("state_read"), NSM * (h + 1))
            V.tensor_scalar(hs, pa[:, 3, :], den_s[:, 1:2], None, ALU.mult).then_inc(
                sem("h_sample"), 1)
        gate_sample(HA - 1)
        residual(0)
        dve.wait_ge(evacuated, out_groups)
        link(V.tensor_tensor(res, res, sq, ALU.add))
        norm(0, U_OUT + DC)
        peer(0)
        norm(1)
        V.memset(qbd, 0.0)
        residual(2)
        dve.wait_ge(evacuated, kv_groups)
        dve.wait_ge(sem("kw_in"), 16)
        V.tensor_copy(kw[:, :, :, WINDOW - 1], ktb[:, :, TP:T]).then_inc(sem("window_ready"), 1)
        dve.wait_ge(evacuated, bq_groups)
        link(V.engine_nop())
        pitch = big.ap[0][0]
        for half in range(2):
            rr = slice(half * HD, (half + 1) * HD)
            base = qbd[rr, 0, 0, 2 * half:2 * half + 1]
            for G in range(2):
                dst = bass.AP(base.tensor, base.offset + G * (P + 8),
                              [[pitch, HD], [4, 2], [1, 2], [2 * P + 16, NSM]])
                last = V.tensor_copy(dst, qb[rr, 4 * G:4 * G + 4, TP:T].rearrange("p (a c) b -> p a c b", c=2))
        last.then_inc(sem("q_spread"), 1)
        dve.wait_ge(sem("bias_b_in"), 64)

        def att_front(i):
            g4 = i % 4
            nk = P * (i // 4 + 1)
            s4 = ss[:, i % 3, :, 0:nk]
            dve.wait_ge(sem("att_scores"), i + 1)
            if i >= 3:
                dve.wait_ge(sem("att_turned"), i - 2)
            src = pa[:, 2 * (i % 2):2 * (i % 2) + 2, :].rearrange("p b (e k) -> p (b e) k", e=2)[:, :, 0:nk]
            V.scalar_tensor_tensor(s4, src, HD ** -0.5, bias[:, 4 * g4:4 * g4 + 4, 2 * P - nk:2 * P],
                                   ALU.mult, ALU.add).then_inc(sem("att_scored"), 1)
            dve.wait_ge(sem("att_scored"), i + 1)
            m, sk = mx[:, i % 2, :], sink[:, 4 * g4:4 * g4 + 4]
            link(V.tensor_reduce(m, s4, AX.X, ALU.max))
            link(V.tensor_tensor(m, m, sk, ALU.max))
            V.tensor_scalar(neg_mx[:, i % 2, :], m, -1.0, None, ALU.mult)
            V.tensor_tensor(dx[:, i % 2, :], sk, m, ALU.subtract).then_inc(sem("att_shifted"), 1)

        def att_back(i):
            nk = P * (i // 4 + 1)
            s4, dn = ss[:, i % 3, :, 0:nk], dx[:, i % 2, :]
            dve.wait_ge(sem("att_exp"), i + 1)
            link(V.tensor_reduce(sx[:, i % 2, :], s4, AX.X, ALU.add))
            link(V.tensor_tensor(dn, dn, sx[:, i % 2, :], ALU.add))
            link(V.reciprocal(dn, dn))
            V.tensor_tensor(s4, s4, dn.rearrange("p (e o) -> p e o", o=1).to_broadcast([P, 4, nk]),
                            ALU.mult).then_inc(sem("att_probs"), 1)

        def att_keep(i):
            blk, g4 = i // 4, i % 4
            dve.wait_ge(sem("att_out"), i + 1)
            V.tensor_copy(ot[:, 2 * g4:2 * g4 + 2, blk * P:(blk + 1) * P],
                          pb[:, 2 + i % 2, 0:2 * P].rearrange("p (c q) -> p c q", c=2)).then_inc(sem("att_out_kept"), 1)

        att_front(0)
        dve.wait_ge(sem("att_s_scores"), 1)
        link(V.scalar_tensor_tensor(ss_s, pb[:, 1, 0:WINDOW], HD ** -0.5, bias_s, ALU.mult, ALU.add))
        link(V.tensor_reduce(small_s[:, 0:1], ss_s, AX.X, ALU.max))
        link(V.tensor_tensor(small_s[:, 0:1], small_s[:, 0:1], sink_s, ALU.max))
        V.tensor_tensor(small_s[:, 1:2], sink_s, small_s[:, 0:1], ALU.subtract)
        V.tensor_scalar(ss_s, ss_s, small_s[:, 0:1], None, ALU.subtract).then_inc(sem("att_s_shifted"), 1)
        for i in range(8):
            if i + 1 < 8:
                att_front(i + 1)
            att_back(i)
            if i >= 2:
                att_keep(i - 2)
            if i == 0:
                dve.wait_ge(sem("att_s_exp"), 1)
                link(V.tensor_reduce(small_s[:, 2:3], ss_s, AX.X, ALU.add))
                link(V.tensor_tensor(small_s[:, 2:3], small_s[:, 2:3], small_s[:, 1:2], ALU.add))
                link(V.reciprocal(small_s[:, 3:4], small_s[:, 2:3]))
                V.tensor_scalar(ss_s, ss_s, small_s[:, 3:4], None, ALU.mult).then_inc(sem("att_s_probs"), 1)
            if i == 2:
                dve.wait_ge(sem("att_s_turned"), 1)
                V.tensor_copy(pt_s, pb[:, 1, 128:256]).then_inc(sem("att_s_kept"), 1)
            if i == 3:
                dve.wait_ge(sem("att_s_out"), 1)
                for half in range(2):
                    rr = slice(half * HD, (half + 1) * HD)
                    src = pb[rr, 1, 256:256 + NSM * 16].rearrange("p (b a h c) -> p a c b h", b=NSM, h=2, c=2)
                    last = V.tensor_copy(ot[rr, :, TP:T].rearrange("p (a c) b -> p a c b", c=2),
                                         src[:, :, :, :, half])
                last.then_inc(sem("att_s_done"), 1)
        att_keep(6)
        att_keep(7)
        norm(2, U_BO)
        peer(1)
        norm(3)

    @block.gpsimd
    def _(pool):
        def lows(a, b):
            n0 = n_split(a)
            with pool.Fori(0, (b - a) // RING) as it:
                for k in range(RING):
                    for half in range(2):
                        v, o = 2 * ((n0 + k) % 2) + half, slice(half * 512, (half + 1) * 512)
                        pool.wait_ge(high_done, it * (2 * RING) + (2 * (n0 + k) + half + 1))
                        nc.gpsimd.tensor_tensor(split[:, v, 1, :], ring[:, (a + k) % RING, o], split_f[:, v, 0, :],
                                                ALU.subtract).then_inc(low_done["pool"], 1)

        lows(U_IN, U_QKV)
        for n in range(3):
            pool.dma_start(cs[:, n], io["state_in"][n]).then_inc(sem(f"state_in_{n}"), 16)
        pool.wait_ge(sem("m_kept"), 1)
        pool.dma_start(io["m_out"], m_out[0:HA, :]).then_inc(sem("small_out"), 16)
        pool.wait_ge(sem("conv_kept"), 1)
        pool.dma_start(io["conv_out"], conv_out).then_inc(sem("small_out"), 16)
        pool.wait_ge(sem("bias_rows_kept"), 1)
        pool.dma_start(io["bias_rows"], rt[0:HB, :].rearrange("p (o w) -> p o w", o=1).to_broadcast(
            [HB, P, BIASW])).then_inc(sem("bias_stored"), 16)
        pool.wait_ge(halves_used, 2 * (U_QKV - U_IN))
        for n in range(3, SLOTS):
            pool.dma_start(state(n), io["state_in"][n]).then_inc(sem(f"state_in_{n}"), 16)
        for h in range(HA):
            for b in range(NSM):
                n = NSM * h + b
                pool.wait_ge(sem("state_new"), n + 1)
                pool.dma_start(io["state_out"][n], state(n)).then_inc(sem(f"state_out_{n % SLOTS}"), 16)
                if b == 2:
                    pool.wait_ge(sem("c_kept"), HC * (h + 1))
                    pool.dma_start(io["c_prompt"][h], c_out).then_inc(sem("c_stored"), 16)
                if n >= 1 and n - 1 + SLOTS < NSM * HA:
                    o = n - 1
                    pool.wait_ge(sem("state_read"), o + 1)
                    pool.wait_ge(sem(f"state_out_{o % SLOTS}"), 16 * (o // SLOTS + 1))
                    pool.dma_start(state(o), io["state_in"][o + SLOTS]).then_inc(sem(f"state_in_{o % SLOTS}"), 16)
        pool.wait_ge(sem("head_gated"), HA)
        pool.wait_ge(sem("n_kept"), HA)
        pool.dma_start(io["n_prompt"], n_prompt).then_inc(sem("small_out"), 16)
        pool.dma_start(io["n_sample"], n_new).then_inc(sem("small_out"), 16)
        pool.wait_ge(sem("small_out"), 64)
        pool.wait_ge(sem("c_stored"), 16 * HA)
        for k in range(SLOTS):
            pool.wait_ge(sem(f"state_out_{k}"), 16 * ((NSM * HA - k + SLOTS - 1) // SLOTS))

        def load_skeys(L):
            pool.dma_start(skeys, io["skeys"][L]).then_inc(sem("skeys_in"), 16)

        pool.wait_ge(sem("ln_sum"), DC)
        load_skeys(0)
        lows(U_PQ[0], U_V[0])
        pool.wait_ge(sem("ln_sum"), 2 * DC)
        pool.dma_start(kw[:, :, :, 0:WINDOW - 1], io["kw_in"]).then_inc(sem("kw_in"), 16)
        pool.dma_start(vw[0:WINDOW - 1], io["vw_in"]).then_inc(sem("vw_in"), 16)
        pool.wait_ge(sem("bias_stored"), 16)
        br = io["bias_rows"]
        pool.dma_start(bias, bass.AP(br.tensor, br.offset + WINDOW - 1,
                                     [[BIASW - 1, P], [P * BIASW, HB], [1, 2 * WINDOW]])).then_inc(sem("bias_b_in"), 16)
        pool.dma_start(bias_s, bass.AP(br.tensor, br.offset + WINDOW,
                                       [[0, NSM], [P * BIASW, HB], [1, WINDOW]])).then_inc(sem("bias_b_in"), 16)
        sk = io["sinks"]
        pool.dma_start(sink, bass.AP(sk.tensor, sk.offset, [[0, P], [1, HB]])).then_inc(sem("bias_b_in"), 16)
        pool.dma_start(sink_s, bass.AP(sk.tensor, sk.offset, [[0, NSM], [1, HB], [1, 1]])).then_inc(
            sem("bias_b_in"), 16)
        lows(U_KV, U_BO)
        pool.wait_ge(sem("vb_kept"), 1)
        pool.dma_start(vw[WINDOW - 1:WINDOW, :, :], vsb[0:NSM, :]).then_inc(sem("vw_in"), 16)
        pool.dma_start(io["k_prompt"], ktb[:, :, P:TP]).then_inc(sem("win_out"), 16)
        pool.dma_start(io["v_prompt"], vnb[:, 1, :]).then_inc(sem("win_out"), 16)
        pool.wait_ge(sem("window_ready"), 1)
        pool.dma_start(io["k_sample"], kw).then_inc(sem("win_out"), 16)
        pool.wait_ge(sem("vw_in"), 32)
        pool.dma_start(io["v_sample"], vw).then_inc(sem("win_out"), 16)
        pool.wait_ge(sem("win_out"), 64)
        pool.wait_ge(sem("ln_sum"), 3 * DC)
        load_skeys(1)
        lows(U_PQ[1], U_V[1])


def _head_order():
    return [4 * (2 * (c // 4) + half) + c % 4 for c in range(DC) for half in range(2)]


def _row_order():
    return [_head_order()[2 * (2 * a + c) + half] for a in range(DC // 2) for half in range(2) for c in range(2)]


def _constants():
    f = np.float32
    c = np.zeros((P, NCONST), f)
    lane = np.arange(P)

    def put(name, v):
        a, n = CONSTS[name]
        c[:, a:a + n] = v
    put("ident", np.eye(P, dtype=f))
    put("iota", np.broadcast_to(lane.astype(f), (P, P)))
    put("ones", np.ones((P, P), f))
    sel4 = np.zeros((HA, HA, P), f)
    sel8 = np.zeros((NSM, NSM, P), f)
    for i in range(HA):
        sel4[i, i] = 1
    for i in range(NSM):
        sel8[i, i] = 1
    onehot = np.zeros((NB, WINDOW), f)
    exact = NB // 2
    for y in range(WINDOW):
        d = WINDOW - 1 - y
        b = d if d < exact else min(NB - 1, exact + int(np.log(d / exact) / np.log(128 / exact) * (NB - exact)))
        onehot[b, y] = 1
    causal = (lane[:, None] <= lane[None, :]).astype(f)
    fold = (lane[:, None] % 32 == lane[None, 0:NSM]).astype(f)
    return c, sel4, sel8, onehot, causal, fold


def kernel(x_prompt, x_sample, state_mlstm_C, state_mlstm_n, state_mlstm_m, state_mlstm_conv,
           cache_k_win, cache_v_win, a_w_in, a_b_in, a_conv_w, a_conv_b, a_w_q, a_w_k, a_w_v,
           a_w_out, kv_w, b_w_q, b_w_o, b_sinks, rel_bias, ln_mix_g, ln_mix_b, ln_ffn_g,
           ln_ffn_b, peer_w_q, peer_subkeys, peer_u, peer_v):
    import concourse.bacc as bacc
    from concourse.bass_utils import run_bass_kernel_spmd

    f = np.float32
    A = lambda a: np.asarray(a)
    order = _head_order()
    rows = _row_order()
    qcols = np.concatenate([np.arange(h * HD, (h + 1) * HD) for h in order])

    units = np.empty((N_UNITS, P, 1024), f)

    def kxm(w):
        m = w.shape[1] // P
        return w.reshape(DC, P, m, P).transpose(2, 1, 0, 3).reshape(m, P, 1024)

    w_in = A(a_w_in)[0]
    units[U_IN:U_QKV] = kxm(w_in[:, 0:2 * INNER])
    for h in range(HA):
        n = U_QKV + 6 * h
        for i, w in enumerate((A(a_w_q)[0, h], A(a_w_k)[0, h])):
            units[n + 2 * i:n + 2 * i + 2] = w.reshape(HC, P, 2, 256).transpose(2, 1, 0, 3).reshape(2, P, 1024)
        units[n + 4:n + 6] = A(a_w_v)[0, h].reshape(2, 2, P, DH).transpose(0, 2, 1, 3).reshape(2, P, 1024)
    units[U_OUT:U_OUT + DC] = kxm(A(a_w_out)[0][0:D])
    units[U_OUT + DC:U_PQ[0]] = kxm(A(a_w_out)[0][D:])
    kv = A(kv_w)
    units[U_KV:U_KV + 2] = kxm(kv[:, 0:256])
    units[U_KV + 2:U_KV + 4] = kv[:, 256:512].reshape(2, 4, P, 256).transpose(0, 2, 1, 3).reshape(2, P, 1024)
    units[U_BQ:U_BO] = kxm(A(b_w_q)[0][:, qcols])
    units[U_BO:U_PQ[1]] = kxm(A(b_w_o)[0][qcols, :])
    for L in range(2):
        units[U_PQ[L]:U_U[L]] = kxm(A(peer_w_q)[L])
        units[U_U[L]:U_V[L]] = A(peer_u)[L].reshape(NK, NK, DC, P).transpose(0, 3, 2, 1).reshape(NK, P, 1024)
        units[U_V[L]:U_V[L] + NK] = A(peer_v)[L].reshape(NK, P, 1024)

    def fm(a):
        c = a.shape[-1] // P
        a = np.moveaxis(a, -1, 0)
        return np.moveaxis(a.reshape((c, P) + a.shape[1:]), 0, 1)

    const, sel4, sel8, onehot, causal, fold = _constants()
    xs = np.concatenate([A(x_prompt)[0], A(x_sample)[:, 0]], axis=0)
    b_in = A(a_b_in)[0]
    cols_a = np.concatenate([
        fm(b_in[0:2 * INNER]).reshape(P, -1),
        np.moveaxis(fm(A(a_conv_w)[0]), 2, 1).reshape(P, -1),
        fm(A(a_conv_b)[0]).reshape(P, -1), causal, fold], axis=1)
    cols = np.concatenate([np.moveaxis(fm(A(w)), 2, 1).reshape(P, -1)
                           for w in (ln_mix_g, ln_mix_b, ln_ffn_g, ln_ffn_b)] + [np.full((P, 1), LN_EPS, f)], axis=1)
    C = A(state_mlstm_C)[0]
    arrays = {
        "units": units,
        "x": fm(xs),
        "const": const, "cols": cols, "cols_a": cols_a, "sel4": sel4, "sel8": sel8, "onehot": onehot,
        "w_gate": w_in[:, 2 * INNER:].reshape(DC, P, 8).transpose(1, 0, 2),
        "b_gate": b_in[2 * INNER:].reshape(2, HA).T,
        "m_in": A(state_mlstm_m)[0].T,
        "conv_in": fm(A(state_mlstm_conv)[0]),
        "n_in": A(state_mlstm_n)[0].reshape(NSM, HA, HC, P).transpose(3, 1, 2, 0),
        "state_in": C.transpose(1, 0, 2, 3).reshape(HA * NSM, HC, P, DH).transpose(0, 2, 1, 3),
        "kw_in": A(cache_k_win)[:, 1:].reshape(NSM, WINDOW - 1, 2, P).transpose(3, 2, 0, 1),
        "vw_in": A(cache_v_win)[:, 1:].reshape(NSM, WINDOW - 1, KVH * HD).transpose(1, 0, 2),
        "rel_bias": A(rel_bias)[:, rows],
        "sinks": A(b_sinks)[0][rows],
        "skeys": A(peer_subkeys).transpose(0, 4, 1, 2, 3).reshape(2, P, 2 * PH, NK),
    }
    outs = {
        "y": (P, DC, T), "c_prompt": (HA, P, HC, DH), "n_prompt": (P, HA, HC), "m_out": (HA, 1 + NSM),
        "conv_out": (P, IC, 3 + 3 * NSM), "k_prompt": (P, 2, WINDOW), "v_prompt": (WINDOW, KVH * HD),
        "state_out": (HA * NSM, P, HC, DH), "n_sample": (P, HA, HC, NSM),
        "k_sample": (P, 2, NSM, WINDOW), "v_sample": (WINDOW, NSM, KVH * HD),
    }
    nc = bacc.Bacc("TRN2", target_bir_lowering=False, num_devices=1)
    io, feed = {}, {}
    for name, a in arrays.items():
        a = np.ascontiguousarray(a)
        feed["in_" + name] = a
        io[name] = nc.dram_tensor("in_" + name, a.shape, F32, kind="ExternalInput").ap()
    for name, shape in outs.items():
        io[name] = nc.dram_tensor("out_" + name, shape, F32, kind="ExternalOutput").ap()
    io["bias_rows"] = nc.dram_tensor("bias_rows", (HB, P, BIASW), F32, kind="Internal").ap()
    build(nc, io)
    r = run_bass_kernel_spmd(nc, [feed], core_ids=[0]).results[0]
    o = {name: r["out_" + name] for name in outs}

    y = o["y"].transpose(2, 1, 0).reshape(T, D)
    conv = o["conv_out"].transpose(2, 1, 0).reshape(3 + 3 * NSM, INNER)
    so_ = o["state_out"].reshape(HA, NSM, P, HC, DH).transpose(1, 0, 3, 2, 4).reshape(1, NSM, HA, DH, DH)
    return tuple(np.ascontiguousarray(a) for a in (
        y[:TP].reshape(1, TP, D),
        y[TP:].reshape(NSM, 1, D),
        o["c_prompt"].transpose(0, 2, 1, 3).reshape(1, 1, HA, DH, DH),
        o["n_prompt"].transpose(1, 2, 0).reshape(1, 1, HA, DH),
        o["m_out"][:, 0].reshape(1, 1, HA),
        conv[0:3].reshape(1, 1, 3, INNER),
        o["k_prompt"].transpose(2, 1, 0).reshape(1, WINDOW, KVH, HD),
        o["v_prompt"].reshape(1, WINDOW, KVH, HD),
        so_,
        o["n_sample"].transpose(3, 1, 2, 0).reshape(1, NSM, HA, DH),
        o["m_out"][:, 1:].T.reshape(1, NSM, HA),
        conv[3:].reshape(1, NSM, 3, INNER),
        o["k_sample"].transpose(2, 3, 1, 0).reshape(NSM, WINDOW, KVH, HD),
        o["v_sample"].transpose(1, 0, 2).reshape(NSM, WINDOW, KVH, HD),
    ))
```
